# Optimizing a Trainium2 kernel written in Bass

```python
import math
import jax, jax.numpy as jnp
from jax import lax
import numpy as np

'''One inference step (DEPTH layers) of a hybrid decoder: parallel mLSTM + Mamba-2 (SSD) head groups
sharing one combined input projection and one output projection, followed by a hierarchical
(top-1 group, top-2 expert) MoE of SwiGLU experts; pre-RMSNorm, plain residuals, final RMSNorm;
16 learned meta tokens prepended to prompt sequences.

Inputs:
  x_prompt (BATCH, SEQ, D_MODEL), x_sample (DEC_BATCH, DEC_SEQ, D_MODEL)
  state_mlstm_C    (DEPTH, DEC_BATCH, H_A, DH_A, DH_A)  stabilised matrix memory C~ = C*exp(-m)
  state_mlstm_n    (DEPTH, DEC_BATCH, H_A, DH_A)        stabilised normaliser n~ = n*exp(-m)
  state_mlstm_m    (DEPTH, DEC_BATCH, H_A)              running-max stabiliser
  state_mlstm_conv (DEPTH, DEC_BATCH, CONV_W-1, D_A)    last 3 pre-conv mLSTM input rows
  state_ssm        (DEPTH, DEC_BATCH, H_B, HD_B, N_STATE) SSD state
  state_ssm_conv   (DEPTH, DEC_BATCH, CONV_W-1, CONV_B) last 3 pre-conv x/B/C rows
  followed by weights.
Output tuple:
  (y_prompt (BATCH, SEQ, D_MODEL), y_sample (DEC_BATCH, DEC_SEQ, D_MODEL),
   prompt states: C, n, m, mlstm_conv, ssm, ssm_conv  (same layouts, leading dims DEPTH, BATCH),
   sample states: C, n, m, mlstm_conv, ssm, ssm_conv  (leading dims DEPTH, DEC_BATCH))
'''

D_MODEL = 1024
BATCH = 1
SEQ = 256
DEPTH = 1
DEC_BATCH = 8
DEC_SEQ = 1
PAST_LEN = 2048
PAGE_SIZE = 128

N_META = 16
CHUNK = 128
CONV_W = 4
EPS = 1e-6
D_A = D_MODEL
H_A = 8
DH_A = D_A // H_A
D_B = D_MODEL
HD_B = 64
H_B = D_B // HD_B
N_STATE = 128
G_B = 2
CONV_B = D_B + 2 * G_B * N_STATE
D_MIX = D_A + D_B
D_IN = 2 * D_A + 2 * H_A + D_B + CONV_B + H_B
N_EGROUPS = 4
N_EPG = 4
N_EXPERTS = N_EGROUPS * N_EPG
TOP_K = 2
D_FF = 1024

kernel_name = 'hybrid_mlstm_ssd_hmoe_step'

def rmsnorm(x, g):
    xf = x.astype(jnp.float32)
    y = xf * lax.rsqrt(jnp.mean(xf * xf, -1, keepdims=True) + EPS)
    return (y * g.astype(jnp.float32)).astype(x.dtype)

def causal_conv(x, prev, w, b):
    xp = jnp.concatenate([prev.astype(x.dtype), x], axis=1)
    L = x.shape[1]
    y = sum(w[j] * xp[:, j:j + L] for j in range(CONV_W)) + b
    return y, xp[:, -(CONV_W - 1):]

def chunk_for(L):
    return CHUNK if L % CHUNK == 0 else L

def to_chunks(a, chunk):
    Bn, L = a.shape[0], a.shape[1]
    a = a.reshape((Bn, L // chunk, chunk) + a.shape[2:])
    return jnp.swapaxes(jnp.moveaxis(a, 1, 0), 2, 3)

def from_chunks(a):
    nc, Bn, H, c, D = a.shape
    return jnp.swapaxes(jnp.moveaxis(a, 0, 1), 2, 3).reshape(Bn, nc * c, H, D)

def mlstm_chunk_scan(q, k, v, ig, fg, state, chunk):
    xs = tuple(to_chunks(a, chunk) for a in (q, k, v, ig, fg))
    causal = jnp.tril(jnp.ones((chunk, chunk), bool))

    def step(carry, inp):
        C0, n0, m0 = carry
        qc, kc, vc, ic, fc = inp
        bcum = jnp.cumsum(jax.nn.log_sigmoid(fc), -1)
        dmat = jnp.where(causal, bcum[..., :, None] - bcum[..., None, :] + ic[..., None, :], -jnp.inf)
        m_inter = bcum + m0[..., None]
        m = jnp.maximum(m_inter, dmat.max(-1))
        w_inter = jnp.exp(m_inter - m)
        s = jnp.einsum('bhtd,bhsd->bhts', qc, kc) * jnp.exp(dmat - m[..., None])
        num = jnp.einsum('bhts,bhse->bhte', s, vc) + w_inter[..., None] * jnp.einsum('bhtd,bhde->bhte', qc, C0)
        den = s.sum(-1) + w_inter * jnp.einsum('bhtd,bhd->bht', qc, n0)
        h = num / jnp.maximum(jnp.abs(den), jnp.exp(-m))[..., None]
        mL = m[..., -1]
        dec = jnp.exp(bcum[..., -1] + m0 - mL)
        ws = jnp.exp(bcum[..., -1:] - bcum + ic - mL[..., None])
        kw = kc * ws[..., None]
        C1 = dec[..., None, None] * C0 + jnp.einsum('bhsd,bhse->bhde', kw, vc)
        n1 = dec[..., None] * n0 + kw.sum(2)
        return (C1, n1, mL), h

    state, hs = lax.scan(step, state, xs)
    return from_chunks(hs), state

def ssd_chunk_scan(x, dt, A, bm, cm, S, chunk):
    xs = tuple(to_chunks(a, chunk) for a in (x, dt, bm, cm))
    causal = jnp.tril(jnp.ones((chunk, chunk), bool))

    def step(S0, inp):
        xc, dtc, bc, cc = inp
        a = jnp.cumsum(dtc * A[:, None], -1)
        decay = jnp.exp(jnp.where(causal, a[..., :, None] - a[..., None, :], -jnp.inf))
        scores = jnp.einsum('bhtn,bhsn->bhts', cc, bc) * decay * dtc[..., None, :]
        y = jnp.einsum('bhts,bhsp->bhtp', scores, xc) + jnp.exp(a)[..., None] * jnp.einsum('bhtn,bhpn->bhtp', cc, S0)
        aL = a[..., -1]
        w = jnp.exp(aL[..., None] - a) * dtc
        S1 = jnp.exp(aL)[..., None, None] * S0 + jnp.einsum('bhsp,bhsn->bhpn', xc * w[..., None], bc)
        return S1, y

    S, ys = lax.scan(step, S, xs)
    return from_chunks(ys), S

def run_segments(scan_fn, arrays, state, segments):
    outs, start = [], 0
    for length, chunk in segments:
        y, state = scan_fn(*[a[:, start:start + length] for a in arrays], state, chunk)
        outs.append(y)
        start += length
    return jnp.concatenate(outs, axis=1), state

def mixer_block(hn, conv_a_prev, conv_b_prev, m_state, s_state, segments, p):
    f32 = jnp.float32
    Bn, L, _ = hn.shape
    u = hn @ p['w_in']
    offs = list(np.cumsum([D_A, D_A, H_A, H_A, D_B, CONV_B]))
    xa, za, ia, fa, zb, xbc, dtr = jnp.split(u, offs, axis=-1)
    xa_c, conv_a_new = causal_conv(xa, conv_a_prev, p['conv_a_w'], p['conv_a_b'])
    xc = jax.nn.silu(xa_c).reshape(Bn, L, H_A, DH_A)
    xa_h = xa.reshape(Bn, L, H_A, DH_A)
    q = jnp.einsum('blhd,hde->blhe', xc, p['w_q']).astype(f32)
    k = (jnp.einsum('blhd,hde->blhe', xc, p['w_k']) * DH_A ** -0.5).astype(f32)
    v = jnp.einsum('blhd,hde->blhe', xa_h, p['w_v']).astype(f32)
    ig = (ia + p['b_i']).astype(f32)
    fg = (fa + p['b_f']).astype(f32)
    h_a, m_state = run_segments(mlstm_chunk_scan, (q, k, v, ig, fg), m_state, segments)
    h_a = h_a * lax.rsqrt(jnp.mean(h_a * h_a, -1, keepdims=True) + EPS) * p['norm_a'].astype(f32)
    h_a = h_a.reshape(Bn, L, D_A) * jax.nn.sigmoid(za.astype(f32))
    xbc_c, conv_b_new = causal_conv(xbc, conv_b_prev, p['conv_b_w'], p['conv_b_b'])
    xbc_c = jax.nn.silu(xbc_c)
    xs, bm, cm = jnp.split(xbc_c, [D_B, D_B + G_B * N_STATE], axis=-1)
    xs = xs.reshape(Bn, L, H_B, HD_B).astype(f32)
    rep = H_B // G_B
    bm = jnp.repeat(bm.reshape(Bn, L, G_B, N_STATE), rep, axis=2).astype(f32)
    cm = jnp.repeat(cm.reshape(Bn, L, G_B, N_STATE), rep, axis=2).astype(f32)
    dt = jax.nn.softplus((dtr + p['dt_bias']).astype(f32))
    A = -jnp.exp(p['a_log'].astype(f32))
    y, s_state = run_segments(lambda x_, d_, b_, c_, s_, ch: ssd_chunk_scan(x_, d_, A, b_, c_, s_, ch),
                              (xs, dt, bm, cm), s_state, segments)
    y = y + p['d_skip'].astype(f32)[:, None] * xs
    y = y.reshape(Bn, L, D_B) * jax.nn.silu(zb.astype(f32))
    yg = y.reshape(Bn, L, G_B, D_B // G_B)
    yg = yg * lax.rsqrt(jnp.mean(yg * yg, -1, keepdims=True) + EPS)
    y = yg.reshape(Bn, L, D_B) * p['norm_b'].astype(f32)
    out = jnp.concatenate([h_a, y], axis=-1).astype(hn.dtype) @ p['w_out']
    C1, n1, m1 = m_state
    return out, (C1, n1, m1, conv_a_new, s_state, conv_b_new)

def hier_moe(x, p):
    xf = x.astype(jnp.float32)
    p1 = jax.nn.softmax(xf @ p['w_r1'].astype(jnp.float32) + p['b_r1'], axis=-1)
    gp, gidx = lax.top_k(p1, 1)
    l2 = jnp.einsum('bsd,dge->bsge', xf, p['w_r2'].astype(jnp.float32)) + p['b_r2']
    l2 = jnp.take_along_axis(l2, gidx[..., None], axis=2)[:, :, 0]
    v2, i2 = lax.top_k(l2, TOP_K)
    w2 = jax.nn.softmax(v2, axis=-1)
    eid = gidx * N_EPG + i2
    gate = gp * jnp.sum(w2[..., None] * jax.nn.one_hot(eid, N_EXPERTS, dtype=jnp.float32), axis=-2)
    gate = gate.astype(x.dtype)

    def per_row(args):
        xr, gr = args
        hg = jnp.einsum('sd,edf->sef', xr, p['w_gate'])
        hu = jnp.einsum('sd,edf->sef', xr, p['w_up'])
        return jnp.einsum('sef,efd->sd', jax.nn.silu(hg) * hu * gr[..., None], p['w_down'])

    return lax.map(per_row, (x, gate))

def trunk(h, init_states, segments, drop_meta, layers, norm_final):
    outs = []
    for l in range(DEPTH):
        p = layers[l]
        conv_a, conv_b, mst, sst = init_states[l]
        mix, new = mixer_block(rmsnorm(h, p['norm_mix']), conv_a, conv_b, mst, sst, segments, p)
        h = h + mix
        if drop_meta and l == DEPTH - 1:
            h = h[:, N_META:]
        h = h + hier_moe(rmsnorm(h, p['norm_ffn']), p)
        outs.append(new)
    y = rmsnorm(h, norm_final)
    return y, [jnp.stack(s) for s in zip(*outs)]

def setup_inputs(seed: int = 0) -> dict:
    key = jax.random.key(seed)
    ks = iter(jax.random.split(key, 48))
    f32 = jnp.float32

    def nrm(shape, scale):
        return jax.random.normal(next(ks), shape, f32) * scale

    x_prompt = nrm((BATCH, SEQ, D_MODEL), 1.0)
    x_sample = nrm((DEC_BATCH, DEC_SEQ, D_MODEL), 1.0)
    state_mlstm_C = nrm((DEPTH, DEC_BATCH, H_A, DH_A, DH_A), 0.1)
    state_mlstm_n = nrm((DEPTH, DEC_BATCH, H_A, DH_A), 0.5)
    state_mlstm_m = nrm((DEPTH, DEC_BATCH, H_A), 1.0)
    state_mlstm_conv = nrm((DEPTH, DEC_BATCH, CONV_W - 1, D_A), 1.0)
    state_ssm = nrm((DEPTH, DEC_BATCH, H_B, HD_B, N_STATE), 0.3)
    state_ssm_conv = nrm((DEPTH, DEC_BATCH, CONV_W - 1, CONV_B), 1.0)
    meta_tokens = nrm((N_META, D_MODEL), 1.0)
    norm_mix = 1.0 + nrm((DEPTH, D_MODEL), 0.02)
    w_in = nrm((DEPTH, D_MODEL, D_IN), D_MODEL ** -0.5)
    conv_a_w = nrm((DEPTH, CONV_W, D_A), 0.5)
    conv_a_b = nrm((DEPTH, D_A), 0.01)
    w_q = nrm((DEPTH, H_A, DH_A, DH_A), DH_A ** -0.5)
    w_k = nrm((DEPTH, H_A, DH_A, DH_A), DH_A ** -0.5)
    w_v = nrm((DEPTH, H_A, DH_A, DH_A), DH_A ** -0.5)
    b_i = nrm((DEPTH, H_A), 0.1)
    b_f = jnp.linspace(3.0, 6.0, H_A, dtype=f32)[None] + nrm((DEPTH, H_A), 0.1)
    norm_a = 1.0 + nrm((DEPTH, H_A, DH_A), 0.02)
    conv_b_w = nrm((DEPTH, CONV_W, CONV_B), 0.5)
    conv_b_b = nrm((DEPTH, CONV_B), 0.01)
    dt0 = jnp.exp(jax.random.uniform(next(ks), (DEPTH, H_B), f32, math.log(1e-3), math.log(1e-1)))
    dt_bias = dt0 + jnp.log(-jnp.expm1(-dt0))
    a_log = jnp.log(jax.random.uniform(next(ks), (DEPTH, H_B), f32, 1.0, 16.0))
    d_skip = 1.0 + nrm((DEPTH, H_B), 0.02)
    norm_b = 1.0 + nrm((DEPTH, D_B), 0.02)
    w_out = nrm((DEPTH, D_MIX, D_MODEL), D_MIX ** -0.5)
    norm_ffn = 1.0 + nrm((DEPTH, D_MODEL), 0.02)
    w_r1 = nrm((DEPTH, D_MODEL, N_EGROUPS), D_MODEL ** -0.5)
    b_r1 = nrm((DEPTH, N_EGROUPS), 0.01)
    w_r2 = nrm((DEPTH, D_MODEL, N_EGROUPS, N_EPG), D_MODEL ** -0.5)
    b_r2 = nrm((DEPTH, N_EGROUPS, N_EPG), 0.01)
    w_gate = nrm((DEPTH, N_EXPERTS, D_MODEL, D_FF), D_MODEL ** -0.5)
    w_up = nrm((DEPTH, N_EXPERTS, D_MODEL, D_FF), D_MODEL ** -0.5)
    w_down = nrm((DEPTH, N_EXPERTS, D_FF, D_MODEL), D_FF ** -0.5)
    norm_final = 1.0 + nrm((D_MODEL,), 0.02)
    return {'x_prompt': x_prompt, 'x_sample': x_sample,
            'state_mlstm_C': state_mlstm_C, 'state_mlstm_n': state_mlstm_n, 'state_mlstm_m': state_mlstm_m,
            'state_mlstm_conv': state_mlstm_conv, 'state_ssm': state_ssm, 'state_ssm_conv': state_ssm_conv,
            'meta_tokens': meta_tokens, 'norm_mix': norm_mix, 'w_in': w_in,
            'conv_a_w': conv_a_w, 'conv_a_b': conv_a_b, 'w_q': w_q, 'w_k': w_k, 'w_v': w_v,
            'b_i': b_i, 'b_f': b_f, 'norm_a': norm_a, 'conv_b_w': conv_b_w, 'conv_b_b': conv_b_b,
            'dt_bias': dt_bias, 'a_log': a_log, 'd_skip': d_skip, 'norm_b': norm_b, 'w_out': w_out,
            'norm_ffn': norm_ffn, 'w_r1': w_r1, 'b_r1': b_r1, 'w_r2': w_r2, 'b_r2': b_r2,
            'w_gate': w_gate, 'w_up': w_up, 'w_down': w_down, 'norm_final': norm_final}

def reference(x_prompt, x_sample, state_mlstm_C, state_mlstm_n, state_mlstm_m, state_mlstm_conv,
              state_ssm, state_ssm_conv, meta_tokens, norm_mix, w_in, conv_a_w, conv_a_b, w_q, w_k, w_v,
              b_i, b_f, norm_a, conv_b_w, conv_b_b, dt_bias, a_log, d_skip, norm_b, w_out, norm_ffn,
              w_r1, b_r1, w_r2, b_r2, w_gate, w_up, w_down, norm_final):
    f32 = jnp.float32
    layers = [dict(norm_mix=norm_mix[l], w_in=w_in[l], conv_a_w=conv_a_w[l], conv_a_b=conv_a_b[l],
                   w_q=w_q[l], w_k=w_k[l], w_v=w_v[l], b_i=b_i[l], b_f=b_f[l], norm_a=norm_a[l],
                   conv_b_w=conv_b_w[l], conv_b_b=conv_b_b[l], dt_bias=dt_bias[l], a_log=a_log[l],
                   d_skip=d_skip[l], norm_b=norm_b[l], w_out=w_out[l], norm_ffn=norm_ffn[l],
                   w_r1=w_r1[l], b_r1=b_r1[l], w_r2=w_r2[l], b_r2=b_r2[l],
                   w_gate=w_gate[l], w_up=w_up[l], w_down=w_down[l]) for l in range(DEPTH)]
    bp, sp = x_prompt.shape[0], x_prompt.shape[1]
    dt_x = x_prompt.dtype
    h_p = jnp.concatenate([jnp.broadcast_to(meta_tokens.astype(dt_x)[None], (bp, N_META, D_MODEL)), x_prompt], axis=1)
    init_p = [(jnp.zeros((bp, CONV_W - 1, D_A), dt_x), jnp.zeros((bp, CONV_W - 1, CONV_B), dt_x),
               (jnp.zeros((bp, H_A, DH_A, DH_A), f32), jnp.zeros((bp, H_A, DH_A), f32), jnp.zeros((bp, H_A), f32)),
               jnp.zeros((bp, H_B, HD_B, N_STATE), f32)) for _ in range(DEPTH)]
    seg_p = ((N_META, N_META), (sp, chunk_for(sp)))
    y_prompt, st_p = trunk(h_p, init_p, seg_p, True, layers, norm_final)
    ds = x_sample.shape[1]
    init_s = [(state_mlstm_conv[l], state_ssm_conv[l],
               (state_mlstm_C[l].astype(f32), state_mlstm_n[l].astype(f32), state_mlstm_m[l].astype(f32)),
               state_ssm[l].astype(f32)) for l in range(DEPTH)]
    seg_s = ((ds, chunk_for(ds)),)
    y_sample, st_s = trunk(x_sample, init_s, seg_s, False, layers, norm_final)
    p_C, p_n, p_m, p_conv_a, p_ssm, p_conv_b = st_p
    s_C, s_n, s_m, s_conv_a, s_ssm, s_conv_b = st_s
    return (y_prompt, y_sample, p_C, p_n, p_m, p_conv_a, p_ssm, p_conv_b,
            s_C, s_n, s_m, s_conv_a, s_ssm, s_conv_b)


_drawn_inputs = setup_inputs


def setup_inputs(seed=0):
    import zlib

    import numpy as np

    out = dict(_drawn_inputs(seed))
    spreads = {}
    factors = {'conv_a_b': 2.722,
     'norm_a': 18.847,
     'd_skip': 26.389,
     'norm_b': 11.29,
     'b_r1': 64.0,
     'b_r2': 35.558,
     'norm_final': 8.076,
     'conv_b_b': 3.781,
     'norm_ffn': 6.723}
    for name, (base, spread) in spreads.items():
        noise = np.random.default_rng([zlib.crc32(name.encode()), seed]).standard_normal(out[name].shape)
        drawn = base * np.exp(spread * noise) if base else spread * noise
        out[name] = __import__('jax').numpy.asarray(drawn.astype(out[name].dtype))
    for name, factor in factors.items():
        out[name] = (out[name] * factor).astype(out[name].dtype)
    return out
```

```python
from contextlib import ExitStack

import concourse.bass as bass
from concourse import mybir

F32 = mybir.dt.float32
I32 = mybir.dt.int32
ALU = mybir.AluOpType
ACT = mybir.ActivationFunctionType
AX = mybir.AxisListType.X

P = 128
D = 1024
KD = D // P
META, SEQ, NB = 16, 256, 8
NP = META + SEQ
T = NP + NB
TAPS = 4
PAD = TAPS - 1
SC0 = NP + PAD
CW = SC0 + NB * TAPS
W = CW - PAD
LAST = PAD + NB
HA, DH = 8, 128
HB, HD, NG, NST = 16, 64, 2, 128
CB_T = (D + 2 * NG * NST) // P
QT = W
S_TILES = [(0, 128), (128, 128), (256, 16)]
BLK = [0, NP, NP + NP - 128]
BLKW = BLK[2] + NP - 256
TOK = [(0, 128), (128, 128), (256, 8)]
NOUT = SEQ + NB
EG, EPG, FF = 4, 4, 1024
SLOT = 4 * 1024
BIG = 1e30
EPS = 1e-6
ATANH = [1.0 / (2 * i + 1) for i in range(1, 9)]

O_XA, O_ZA, O_I, O_F = 0, 1024, 2048, 2056
O_ZB, O_XBC, O_DT = 2064, 3088, 4624
WIN = [O_XA, O_XA + 512, O_XBC, O_XBC + 512, O_XBC + 1024, O_ZA, O_ZA + 512, O_ZB, O_ZB + 512]
U_QKV = len(WIN)
U_OUT = U_QKV + 1
N_MIX = U_OUT + 4
MR = 3
EXP_SLOT = [3, 4, 5, 2, 0, 1]
EXP_FREE = [1, 1, 1, 2, 3, 4]

V_NMIX, V_CAW, V_CAB, V_NA, V_NB, V_NFF, V_CBB, V_CBW = 0, 8, 40, 48, 56, 64, 72, 84


class Signals:

    def __init__(self, sem):
        self.params_in = sem("params_in")
        self.prev_in = sem("prev_in")
        self.gates_in = sem("gates_in")
        self.late_in = sem("late_in")
        self.x_again = sem("x_again")
        self.nf_in = sem("nf_in")
        self.pv_ps = sem("pv_ps")
        self.ht_ps = sem("ht_ps")
        self.prev_ps = sem("prev_ps")
        self.u_ps = sem("u_ps")
        self.tm_ps = sem("tm_ps")
        self.bcm_ps = sem("bcm_ps")
        self.lct_ps = sem("lct_ps")
        self.q_ps = sem("q_ps")
        self.k_ps = sem("k_ps")
        self.kt_ps = sem("kt_ps")
        self.vt_ps = sem("vt_ps")
        self.sc_ps = sem("sc_ps")
        self.nc_ps = sem("nc_ps")
        self.n0_ps = sem("n0_ps")
        self.vb_ps = sem("vb_ps")
        self.down_ps = sem("down_ps")
        self.cq_ps = sem("cq_ps")
        self.den_ps = sem("den_ps")
        self.n1_ps = sem("n1_ps")
        self.xs_ps = sem("xs_ps")
        self.bt_ps = sem("bt_ps")
        self.gt_ps = sem("gt_ps")
        self.bc_ps = sem("bc_ps")
        self.y_ps = sem("y_ps")
        self.sst_ps = sem("sst_ps")
        self.bb_ps = sem("bb_ps")
        self.sq_ps = sem("sq_ps")
        self.hbc_ps = sem("hbc_ps")
        self.gbc_ps = sem("gbc_ps")
        self.wo_unit = sem("wo_unit")
        self.xt_ps = sem("xt_ps")
        self.lg_ps = sem("lg_ps")
        self.rank_ps = sem("rank_ps")
        self.xg_ps = sem("xg_ps")
        self.pt_ps = sem("pt_ps")
        self.gate_ps = sem("gate_ps")
        self.gu_ps = sem("gu_ps")
        self.ft_ps = sem("ft_ps")
        self.d_ps = sem("d_ps")
        self.sc_out_ps = sem("sc_out_ps")
        self.consts = sem("consts")
        self.pv_ready = sem("pv_ready")
        self.rstd_ready = sem("rstd_ready")
        self.xn_ready = sem("xn_ready")
        self.ht_ready = sem("ht_ready")
        self.prev_ready = sem("prev_ready")
        self.x_abs = sem("x_abs")
        self.x_exp = sem("x_exp")
        self.alog_exp = sem("alog_exp")
        self.rows_pre = sem("rows_pre")
        self.rows_exp = sem("rows_exp")
        self.lc_ready = sem("lc_ready")
        self.conv_y = sem("conv_y")
        self.conv_sig = sem("conv_sig")
        self.conv_done = sem("conv_done")
        self.z_sig = sem("z_sig")
        self.tm_ready = sem("tm_ready")
        self.bcm_ready = sem("bcm_ready")
        self.lct_sb = sem("lct_sb")
        self.q_sb = sem("q_sb")
        self.k_sb = sem("k_sb")
        self.v_sb = sem("v_sb")
        self.kw_sb = sem("kw_sb")
        self.arg_done = sem("arg_done")
        self.exp_done = sem("exp_done")
        self.st_done = sem("st_done")
        self.num_sb = sem("num_sb")
        self.qs_done = sem("qs_done")
        self.nst_ready = sem("nst_ready")
        self.nst_sb = sem("nst_sb")
        self.n1_ready = sem("n1_ready")
        self.n1_sb = sem("n1_sb")
        self.st_dec = sem("st_dec")
        self.st_new = sem("st_new")
        self.cq_sb = sem("cq_sb")
        self.xdt_ready = sem("xdt_ready")
        self.xw_ready = sem("xw_ready")
        self.bt_ready = sem("bt_ready")
        self.gt_ready = sem("gt_ready")
        self.arg2_done = sem("arg2_done")
        self.exp2_done = sem("exp2_done")
        self.st2_done = sem("st2_done")
        self.sst_ready = sem("sst_ready")
        self.s_y = sem("s_y")
        self.sq_done = sem("sq_done")
        self.rden_ready = sem("rden_ready")
        self.sc_exp = sem("sc_exp")
        self.scale_ready = sem("scale_ready")
        self.num_ready = sem("num_ready")
        self.ynorm_in = sem("ynorm_in")
        self.ysc_exp = sem("ysc_exp")
        self.yb_norm = sem("yb_norm")
        self.h_ready = sem("h_ready")
        self.h_rstd = sem("h_rstd")
        self.xn2_ready = sem("xn2_ready")
        self.xt_ready = sem("xt_ready")
        self.lx_ready = sem("lx_ready")
        self.p1_exp = sem("p1_exp")
        self.l2_ready = sem("l2_ready")
        self.e2_exp = sem("e2_exp")
        self.router = sem("router")
        self.rank_ready = sem("rank_ready")
        self.rounds_ready = sem("rounds_ready")
        self.p_ready = sem("p_ready")
        self.xg_dve = sem("xg_dve")
        self.xg_act = sem("xg_act")
        self.pt_ready = sem("pt_ready")
        self.yg_zero = sem("yg_zero")
        self.xs_ready = sem("xs_ready")
        self.silu_done = sem("silu_done")
        self.a_ready = sem("a_ready")
        self.ht_sb = sem("ht_sb")
        self.yg_done = sem("yg_done")
        self.h_add = sem("h_add")
        self.f_rstd = sem("f_rstd")
        self.y_ready = sem("y_ready")
        self.out_conv = sem("out_conv")
        self.out_mn = sem("out_mn")
        self.out_S = sem("out_S")
        self.out_y = sem("out_y")


def program(nc, x_prompt, x_sample, C0, n0, m0, conv_a0, S0, conv_b0, meta, norm_mix, w_in,
            conv_a_w, conv_a_b, w_q, w_k, w_v, b_i, b_f, norm_a, conv_b_w, conv_b_b, dt_bias, a_log,
            d_skip, norm_b, w_out, norm_ffn, w_r1, b_r1, w_r2, b_r2, w_gate, w_up, w_down, norm_final,
            y_p, y_s, p_C, p_n, p_m, p_ca, p_S, p_cb, s_C, s_n, s_m, s_ca, s_S, s_cb):
    ctx = ExitStack()
    with ctx:
        def sb(name, shape, dt=F32):
            return ctx.enter_context(nc.sbuf_tensor(name, shape, dt))

        def sem(name):
            return ctx.enter_context(nc.semaphore(name))

        def carve(t, start, *dims):
            n = 1
            for d in dims:
                n *= d
            v = t[:, start:start + n]
            if len(dims) == 2:
                v = v.rearrange("p (a b) -> p a b", b=dims[1])
            if len(dims) == 3:
                v = v.rearrange("p (a b c) -> p a b c", b=dims[1], c=dims[2])
            return v

        ring = sb("ring", [P, 6 * SLOT])
        tmp0 = 3 * SLOT
        XDT = carve(ring, tmp0, 3, D)
        XWT = carve(ring, tmp0 + 3072, 3, D)
        CPREV = carve(ring, tmp0, (KD + CB_T) * P)
        LCT = carve(ring, tmp0 + 3072, (KD + CB_T) * P)
        kw = carve(ring, tmp0 + 6144, 2, 3, P)
        vv = carve(ring, tmp0 + 6912, 2, 3, P + 1)
        SST = carve(ring, tmp0 + 6144, 2, 512)
        BCS = ring[0:NB, tmp0 + 6144 + D:tmp0 + 6144 + D + 512]
        VS = ring[0:NB, tmp0:tmp0 + D]
        assert D + 512 <= 2 * 3 * (2 * P + 1)
        TMPS = carve(ring, tmp0 + 7686, D)
        rows0 = tmp0 + 8710

        def rowt(i, w=T):
            return ring[:, rows0 + i * T:rows0 + i * T + w]

        XR = ring[:, rows0:rows0 + 2 * T]
        EX = ring[:, rows0 + 2 * T:rows0 + 4 * T]
        SS = ring[:, rows0 + 4 * T:rows0 + 6 * T]
        HN = ring[:, rows0 + 6 * T:rows0 + 8 * T]
        RI, AC, AR = rowt(8), rowt(9), rowt(10)
        MX = rowt(11)
        WSR, EDR = rowt(2), rowt(3)
        BN, MROW = rowt(4), rowt(5)
        DEN, SCL, YSC = rowt(6), rowt(7), rowt(8)
        assert rows0 + 12 * T <= 6 * SLOT

        h_tok = sb("h_tok", [P, 3, D])
        stage = h_tok
        xn = sb("xn", [P, 3, D])
        xnf = xn[:, :, :].rearrange("p a b -> p (a b)")
        qT = carve(xnf, 0, 2, QT)
        kT = carve(xnf, 2 * QT, 2, QT)
        GT = carve(xnf, 4 * QT, 2, BLKW)
        BT = carve(xnf, 4 * QT + 2 * BLKW, 3, NG * NST)
        SDEN = 4 * QT + 2 * BLKW + 3 * NG * NST
        assert SDEN <= 3 * D

        arena = sb("arena", [P, 15304])
        CA = carve(arena, 0, KD, CW)
        CBX = carve(arena, 2456, CB_T, CW)
        ZA = carve(arena, 6140, KD, T)
        ZB = carve(arena, 8380, KD, T)
        hT = carve(arena, 10620, KD, T)
        NUM = hT
        XC = carve(arena, 12860, KD, W)
        YB = carve(arena, 12860, KD, T)
        XG = carve(arena, 0, KD, EG * P)
        YG = carve(arena, 4096, EG, D)
        XT = carve(arena, 4096, KD, NOUT)
        PT = carve(arena, 8192, EG, NOUT)
        PG = carve(arena, 9248, 3, EG * P)
        XS = carve(arena, 10784, KD, P)
        SG = carve(arena, 11808, D)
        AH = carve(arena, 12832, D)
        HT = carve(arena, 13856, KD, P)

        shared = sb("shared", [P, 1216])
        CY = carve(shared, 0, 2, W)
        CSG = carve(shared, 2 * W, 2, W)
        ARG = carve(shared, 0, 2, BLKW)
        SQ = carve(shared, 2 * BLKW, T)
        NF = carve(shared, 0, D)

        ident = sb("ident", [P, P])
        mask = sb("mask", [P, NP])
        before = sb("before", [P, P])
        ones = sb("ones", [P, P])
        iota_i = sb("iota_i", [P, P], I32)
        iota = sb("iota", [P, P])
        strip = sb("strip", [P, 15])
        PR = sb("PR", [84, 2, P])
        PV = sb("PV", [P, 132])
        c16 = sb("c16", [HB, 8])
        WG = sb("WG", [P, KD, 32])
        LC = sb("LC", [P, KD + CB_T, LAST])
        TM = sb("TM", [P, 3, 64])
        RS = sb("RS", [HA, 16])
        RX = sb("RX", [HB, 17])
        BCM = sb("BCM", [P, HA, 16])
        XE = sb("XE", [P, KD, 17])
        m0s = sb("m0s", [HA, NB])
        N0 = sb("N0", [64, P])
        N1 = sb("N1", [P, 64])
        NT = sb("NT", [P, 64])
        QN = sb("QN", [P, 64])
        N1T = sb("N1T", [64, P])
        QS = sb("QS", [P, HA, NB])
        KS = sb("KS", [P, HA, NB])
        XDS = sb("XDS", [P, KD, NB])
        YS = sb("YS", [P, KD, NB])
        CST = sb("CST", [P, 2, P + 1])
        NSTt = sb("NSTt", [P, HA])
        NSTo = sb("NSTo", [HA, P])
        ENM = sb("ENM", [HB, T])
        YS2 = sb("YS2", [P, KD, NB])
        st3 = sb("st3", [P, 8])
        wr = sb("wr", [P, KD, 20])
        br = sb("br", [1, 20])
        epst = sb("epst", [P, 2])

        bank = [ctx.enter_context(nc.psum_tensor(f"bank{i}", [P, 512], F32)) for i in range(8)]

        L = sb("L", [P, 3, 20])
        LX = sb("LX", [P, 3, 4])
        M1 = sb("M1", [P, 3, 4])
        K1 = sb("K1", [P, 3, 4])
        L2 = sb("L2", [P, 3, 4])
        O1 = sb("O1", [P, 3, 4])
        O2 = sb("O2", [P, 3, 4])
        LP = sb("LP", [P, 3, 4, 4])
        r1 = sb("r1", [P, 3, 8])
        GATE = sb("GATE", [P, 3, 4])
        rank = sb("rank", [P, 3, 4])
        order = sb("order", [P, 4])
        GS = sb("GS", [P, EG * EPG])
        cnt = sb("cnt", [P, 8])
        rounds = sb("rounds", [P, 1], I32)

        s = Signals(sem)
        x_in = [sem(f"x_in{i}") for i in range(3)]
        u_free = [sem(f"u_free{b}") for b in range(4)]
        y_free = [sem(f"y_free{b}") for b in range(2)]
        arrived = [sem(f"arrived{i}") for i in range(6)]
        st_in = [sem(f"st_in{i}") for i in range(3)]
        st_out = [sem(f"st_out{i}") for i in range(3)]
        cst_out = [sem(f"cst_out{i}") for i in range(2)]
        dch, ach, gch = sem("dve_chain"), sem("act_chain"), sem("pool_chain")

        slot = [ring[:, i * SLOT:(i + 1) * SLOT] for i in range(6)]

        def slot_k(i, n):
            return slot[i].rearrange("p (k n) -> p k n", n=n)

        def unit_at(u):
            return u % MR, 16 * (u // MR + 1) + (32 if u % MR == U_QKV % MR and u >= U_QKV else 0)

        mix_in = [0] * 6
        for u in range(N_MIX):
            mix_in[u % MR] += 48 if u == U_QKV else 16

        UT = [("xa", c, c // 4, (c % 4) * P) for c in range(KD)]
        UT += [("xbc", c, 2 + c // 4, (c % 4) * P) for c in range(CB_T)]
        UT += [("za", c, 5 + c // 4, (c % 4) * P) for c in range(KD)]
        UT += [("zb", c, 7 + c // 4, (c % 4) * P) for c in range(KD)]
        NCONV = KD + CB_T

        def col(t, n):
            return t[:, n:n + 1].to_broadcast([t.shape[0], P])

        def bc_last(v, n):
            return v.unsqueeze(len(v.shape)).to_broadcast(list(v.shape) + [n])

        def smp(v):
            return v[:, SC0:SC0 + TAPS * (NB - 1) + 1:TAPS]

        def rounds_of(eng):
            eng.wait_ge(s.rounds_ready, 1)
            return eng.value_load(rounds[0:1, 0:1], min_val=1, max_val=3)

        def head_state_out(pool, h):
            pool.wait_ge(s.num_sb, h + 1)
            pool.dma_start(p_C[0, 0, h], CST[:, h % 2, 0:P]).then_inc(cst_out[h % 2], 16)
            nc.gpsimd.tensor_copy(NSTt[:, h:h + 1], CST[:, h % 2, P:P + 1]).then_inc(s.nst_ready, 1)

        def state_store(pool, n, buf, dram):
            pool.wait_ge(s.st_new, n + 1)
            pool.dma_start(dram(n, False), buf(n)).then_inc(st_out[n % 3], 16)

        def state_free(pool, n):
            pool.wait_ge(st_out[n % 3], 16 * (n // 3 + 1))
            if n < NB:
                pool.wait_ge(s.cq_ps, n + 1)
            else:
                pool.wait_ge(s.s_y, n - NB + 1)

        def turn_hidden(act, x2, j):
            act.wait_ge(s.ft_ps, x2 + (j + 1))
            nc.scalar.activation(HT[:, 4 * j:4 * j + 4, :], bank[4 + j][:, :].rearrange("p (k n) -> p k n", n=P),
                                 ACT.Copy).then_inc(s.ht_sb, 1)

        def ssd_out(dve, c):
            dve.wait_ge(s.y_ps, 2 * c + 2)
            nc.vector.scalar_tensor_tensor(out=YB[:, c, 0:NP], in0=CBX[:, c, 0:NP], scalar=XE[:, c, 16:17],
                                           in1=bank[6 if c % 2 == 0 else 0][:, 0:NP], op0=ALU.mult, op1=ALU.add)\
                .then_inc(y_free[c % 2], 1)

        ctx.enter_context(nc.allow_non_contiguous_dma(reason="small [sample, head] tables, transposed"))
        block = ctx.enter_context(nc.Block())

        @block.sync
        def _(sp):
            for u in range(N_MIX):
                if u >= MR:
                    before_u = u - MR
                    if before_u < U_QKV:
                        sp.wait_ge(s.u_ps, 3 + 4 * (before_u + 1))
                    elif before_u == U_QKV:
                        sp.wait_ge(s.vt_ps, HA)
                    else:
                        sp.wait_ge(s.wo_unit, before_u - U_QKV)
                i = u % MR
                if u < U_QKV:
                    src = w_in[0, :, WIN[u]:WIN[u] + 512].rearrange("(k p) n -> p k n", p=P)
                    sp.dma_start(slot_k(i, 512), src).then_inc(arrived[i], 16)
                elif u == U_QKV:
                    for j, wt in enumerate((w_q, w_k, w_v)):
                        dst = slot[i][:, j * D:(j + 1) * D].rearrange("p (h e) -> p h e", e=DH)
                        sp.dma_start(dst, wt[0].rearrange("h d e -> d h e")).then_inc(arrived[i], 16)
                else:
                    r0 = 512 * (u - U_OUT)
                    src = w_out[0, r0:r0 + 512, :].rearrange("(k p) n -> p k n", p=P)
                    sp.dma_start(slot_k(i, D), src).then_inc(arrived[i], 16)

            gate_v = w_gate[0].rearrange("e (k p) n -> e p k n", p=P)
            up_v = w_up[0].rearrange("e (k p) n -> e p k n", p=P)
            down_v = w_down[0].rearrange("e (k p) n -> e p k n", p=P)

            def expert_units(e, free):
                for c in range(6):
                    sp.wait_ge(*free[c])
                    i = EXP_SLOT[c]
                    if c < 4:
                        v = gate_v if c % 2 == 0 else up_v
                        src = v[bass.ds(e, 1), :, :, (c // 2) * 512:(c // 2 + 1) * 512]
                        dst = slot_k(i, 512)
                    else:
                        src = down_v[bass.ds(e, 1), :, (c - 4) * 4:(c - 3) * 4, :]
                        dst = slot_k(i, D)
                    src = src.rearrange("o p k n -> (o p) k n")
                    sp.dma_start(dst, src).then_inc(arrived[i], 16)

            def read_by(x):
                return [(s.gate_ps, x * 2 - 1), (s.gu_ps, x * 2), (s.gate_ps, x * 2), (s.gu_ps, x * 2 + 1),
                        (s.down_ps, x), (s.d_ps, x)]

            sp.wait_ge(s.out_S, 16 * 2)
            expert_units(0, [(s.wo_unit, n) for n in EXP_FREE])
            with sp.Fori(1, EG * EPG) as e:
                expert_units(e, read_by(e))
            again = rounds_of(sp)
            with sp.If(again > 1):
                with sp.Fori(1, again) as r:
                    with sp.Fori(0, EG * EPG) as e:
                        expert_units(e, read_by(r * (EG * EPG) + e))
            sp.wait_ge(s.out_y, 16 * 3)
            sp.wait_ge(s.out_conv, 16 * 6)
            sp.wait_ge(s.out_mn, 16 * 4)
            sp.wait_ge(s.out_S, 16 * 2)
            for i in range(2):
                sp.wait_ge(cst_out[i], 16 * 4)
            for i in range(3):
                sp.wait_ge(st_out[i], 16 * len(range(i, 2 * NB, 3)))

        @block.gpsimd
        def _(pool):
            g = nc.gpsimd
            links = [0]

            def link(ins):
                links[0] += 1
                ins.then_inc(gch, 1)
                pool.wait_ge(gch, links[0])

            g.memset(ones[:], 1.0)
            g.memset(ident[:], 0.0)
            g.memset(mask[:], 0.0)
            g.memset(strip[:], 0.0)
            g.memset(epst[:, 0:1], EPS)
            g.iota(iota_i[:], pattern=[[1, P]], base=0, channel_multiplier=0)
            link(g.memset(epst[:, 1:2], 1.0))
            g.memset(strip[:, 7:8], 1.0)
            g.affine_select(out=ident[:], in_=ident[:], compare_op=ALU.not_equal, fill=1.0, base=0,
                            pattern=[[-1, P]], channel_multiplier=1)
            g.affine_select(out=mask[:], in_=mask[:], compare_op=ALU.is_ge, fill=BIG, base=0,
                            pattern=[[1, NP]], channel_multiplier=-1)
            g.affine_select(out=before[:], in_=ones[:], compare_op=ALU.is_gt, fill=0.0, base=0,
                            pattern=[[1, P]], channel_multiplier=-1)
            g.tensor_copy(iota[:], iota_i[:])
            for j in range(4):
                g.memset(order[:, j:j + 1], 4.0 - j)
            g.memset(CA[:, :, 0:PAD], 0.0)
            g.memset(CBX[:, :, 0:PAD], 0.0)
            g.memset(vv[:, :, :, P:P + 1].rearrange("p a b c -> p (a b) c"), 1.0)
            g.memset(XR[0:HB, T:2 * T], 0.0)
            g.memset(ENM[0:HB, :], 1.0)
            g.memset(L[:], 0.0).then_inc(s.consts, 1)

            def state_buf(n):
                return stage[:, n % 3, :].rearrange("p (a b) -> p a b", b=P)

            def state_dram(n, old):
                if n < NB:
                    t = C0 if old else s_C
                    return t[0, n].rearrange("h d e -> d h e")
                t = S0 if old else s_S
                return t[0, n - NB].rearrange("h q n -> (h q) n").rearrange("(c p) n -> p c n", p=P)

            def state_load(n):
                pool.dma_start(state_buf(n), state_dram(n, True)).then_inc(st_in[n % 3], 16)

            pool.wait_ge(s.xn_ready, 3)
            for n in range(3):
                state_load(n)
            pool.dma_start(s_ca[0, :, 0:2, :], conv_a0[0, :, 1:3, :]).then_inc(s.out_conv, 16)
            pool.dma_start(s_cb[0, :, 0:2, :], conv_b0[0, :, 1:3, :]).then_inc(s.out_conv, 16)
            pool.wait_ge(s.rows_pre, 1)
            pool.dma_start(p_m[0, 0, :].unsqueeze(1), MROW[0:HA, NP - 1:NP]).then_inc(s.out_mn, 16)
            pool.dma_start(s_m[0].rearrange("b h -> h b"), MROW[0:HA, NP:T]).then_inc(s.out_mn, 16)
            pool.wait_ge(s.lct_sb, 5)
            pool.dma_start(p_ca[0, 0], LCT[0:PAD, 0:D]).then_inc(s.out_conv, 16)
            pool.dma_start(p_cb[0, 0], LCT[0:PAD, D:]).then_inc(s.out_conv, 16)
            pool.dma_start(s_ca[0, :, 2, :], LCT[PAD:LAST, 0:D]).then_inc(s.out_conv, 16)
            pool.dma_start(s_cb[0, :, 2, :], LCT[PAD:LAST, D:]).then_inc(s.out_conv, 16)

            for h in range(HA):
                pool.wait_ge(s.q_sb, h + 1)
                pool.wait_ge(s.k_sb, h + 1)
                g.tensor_copy(QS[:, h, :], smp(qT[:, h % 2, :]))
                g.tensor_copy(KS[:, h, :], smp(kT[:, h % 2, :])).then_inc(s.qs_done, 1)
                if h > 0:
                    head_state_out(pool, h - 1)
            head_state_out(pool, HA - 1)

            for n in range(2 * NB):
                pool.wait_ge(st_in[n % 3], 16 * (n // 3 + 1))
                v = state_buf(n)
                if n < NB:
                    if n == 0:
                        pool.wait_ge(s.bcm_ready, 1)
                    g.tensor_tensor(v, v, bc_last(BCM[:, :, n], P), ALU.mult).then_inc(s.st_dec, 1)
                else:
                    g.tensor_tensor(v, v, bc_last(XE[:, :, n - NB], P), ALU.mult).then_inc(s.st_dec, 1)
                if n >= 1:
                    state_store(pool, n - 1, state_buf, state_dram)
                    if n + 2 < 2 * NB:
                        state_free(pool, n - 1)
                        state_load(n + 2)
                if n == NB:
                    pool.wait_ge(s.nst_sb, 1)
                    pool.dma_start(p_n[0, 0], NSTo[:, :]).then_inc(s.out_mn, 16)
                    pool.wait_ge(s.n1_sb, 1)
                    pool.dma_start(s_n[0].rearrange("b h d -> (b h) d"), N1T[:, :]).then_inc(s.out_mn, 16)
                    pool.wait_ge(s.out_conv, 16 * 6)
                    for i, (_t0, m) in enumerate(S_TILES):
                        pool.wait_ge(s.xdt_ready, 2 * (i + 1))
                        g.tensor_tensor(XWT[0:m, i, :].rearrange("p (h q) -> p h q", q=HD),
                                        XDT[0:m, i, :].rearrange("p (h q) -> p h q", q=HD),
                                        bc_last(TM[0:m, i, 48:64], HD), ALU.mult).then_inc(s.xw_ready, 1)
            state_store(pool, 2 * NB - 1, state_buf, state_dram)
            for half in range(2):
                pool.wait_ge(s.sst_ready, half + 1)
                dst = p_S[0, 0].rearrange("h q n -> (h q) n").rearrange("(c p) n -> p c n", p=P)
                pool.dma_start(dst[:, 4 * half:4 * half + 4, :],
                               SST[:, half, :].rearrange("p (c n) -> p c n", n=NST)).then_inc(s.out_S, 16)
            for n in range(2 * NB - 3, 2 * NB):
                state_free(pool, n)
            for i, (t0, m) in enumerate(TOK):
                src = x_prompt[0, t0:t0 + m, :] if i < 2 else x_sample[:, 0, :]
                pool.dma_start(h_tok[0:m, i, :], src).then_inc(s.x_again, 16)
            pool.wait_ge(s.h_ready, 1)
            pool.dma_start(NF, norm_final.rearrange("(o n) -> o n", o=1).to_broadcast([P, D]))\
                .then_inc(s.nf_in, 16)

        @block.scalar
        def _(act):
            a = nc.scalar
            links = [0]

            def link(ins):
                links[0] += 1
                ins.then_inc(ach, 1)
                act.wait_ge(ach, links[0])

            act.dma_start(h_tok[0:P, 0, :], x_prompt[0, 0:P, :]).then_inc(x_in[0], 16)
            act.dma_start(h_tok[0:P, 1, :], x_prompt[0, P:SEQ, :]).then_inc(x_in[1], 16)
            act.dma_start(h_tok[0:NB, 2, :], x_sample[:, 0, :]).then_inc(x_in[2], 16)
            act.dma_start(h_tok[NB:NB + META, 2, :], meta).then_inc(x_in[2], 16)
            rows8 = "(k p) -> k p"
            act.dma_start(PR[V_NMIX:V_NMIX + 8, 0, :], norm_mix[0].rearrange(rows8, p=P)).then_inc(s.params_in, 16)
            act.dma_start(PR[V_CAW:V_CAW + 32, 0, :], conv_a_w[0].rearrange("j (k p) -> (j k) p", p=P)).then_inc(s.params_in, 16)
            act.dma_start(PR[V_CAB:V_CAB + 8, 0, :], conv_a_b[0].rearrange(rows8, p=P)).then_inc(s.params_in, 16)
            act.dma_start(PR[V_NA:V_NA + 8, 0, :], norm_a[0]).then_inc(s.params_in, 16)
            act.dma_start(PR[V_NB:V_NB + 8, 0, :], norm_b[0].rearrange(rows8, p=P)).then_inc(s.params_in, 16)
            act.dma_start(PR[V_NFF:V_NFF + 8, 0, :], norm_ffn[0].rearrange(rows8, p=P)).then_inc(s.params_in, 16)
            act.dma_start(PR[V_CBB:V_CBB + CB_T, 0, :], conv_b_b[0].rearrange(rows8, p=P)).then_inc(s.params_in, 16)
            act.dma_start(PR[0:4 * CB_T, 1, :], conv_b_w[0].rearrange("j (k p) -> (j k) p", p=P)).then_inc(s.params_in, 16)
            for j, (v, n) in enumerate(((b_i, HA), (b_f, HA), (dt_bias, HB), (a_log, HB), (d_skip, HB))):
                act.dma_start(c16[0:n, j:j + 1], v[0].unsqueeze(1)).then_inc(s.params_in, 16)
            act.dma_start(CPREV[0:PAD * NB, 0:D], conv_a0[0].rearrange("b j c -> (b j) c")).then_inc(s.prev_in, 16)
            act.dma_start(CPREV[0:PAD * NB, D:], conv_b0[0].rearrange("b j c -> (b j) c")).then_inc(s.prev_in, 16)
            act.dma_start(WG[:, :, 0:16], w_in[0, :, O_I:O_I + 16].rearrange("(k p) n -> p k n", p=P)).then_inc(s.gates_in, 16)
            act.dma_start(WG[:, :, 16:32], w_in[0, :, O_DT:O_DT + 16].rearrange("(k p) n -> p k n", p=P)).then_inc(s.gates_in, 16)
            act.dma_start(m0s[:, :], m0[0].rearrange("b h -> h b")).then_inc(s.late_in, 16)
            act.dma_start(N0[:, :], n0[0].rearrange("b h d -> (b h) d")).then_inc(s.late_in, 16)
            act.dma_start(wr[:, :, 0:4], w_r1[0].rearrange("(k p) g -> p k g", p=P)).then_inc(s.late_in, 16)
            act.dma_start(wr[:, :, 4:20], w_r2[0].rearrange("(k p) g e -> p k (g e)", p=P)).then_inc(s.late_in, 16)
            act.dma_start(br[:, 0:4], b_r1).then_inc(s.late_in, 16)
            act.dma_start(br[:, 4:20], b_r2.rearrange("o g e -> o (g e)")).then_inc(s.late_in, 16)

            act.wait_ge(s.consts, 1)
            for i, m in enumerate((P, P, NB + META)):
                act.wait_ge(x_in[i], 16 if i < 2 else 32)
                link(a.activation(xn[0:m, i, :], h_tok[0:m, i, :], ACT.Square, accum_out=st3[0:m, i:i + 1]))
                link(a.activation(st3[0:m, i:i + 1], st3[0:m, i:i + 1], ACT.Ln, bias=epst[0:m, 0:1], scale=1.0 / D))
                a.activation(st3[0:m, 4 + i:5 + i], st3[0:m, i:i + 1], ACT.Exp, scale=-0.5).then_inc(s.rstd_ready, 1)

            act.wait_ge(s.x_abs, 1)
            a.activation(EX[0:HB, :], HN[0:HB, :], ACT.Exp, scale=-1.0).then_inc(s.x_exp, 1)
            a.activation(c16[:, 5:6], c16[:, 3:4], ACT.Exp).then_inc(s.alog_exp, 1)
            act.wait_ge(s.rows_pre, 1)
            a.activation(WSR[0:HA, 0:NP], AC[0:HA, 0:NP], ACT.Exp, bias=c16[0:HA, 6:7])
            a.activation(WSR[0:HA, NP:T], WSR[0:HA, NP:T], ACT.Exp)
            a.activation(EDR[0:HB, 0:NP], AR[0:HB, 0:NP], ACT.Exp, bias=c16[:, 7:8])
            a.activation(RX[:, 0:NB], AR[0:HB, NP:T], ACT.Exp, scale=-1.0)
            a.activation(RS[:, :], RS[:, :], ACT.Exp)
            a.activation(ENM[0:HA, :], MROW[0:HA, :], ACT.Exp, scale=-1.0).then_inc(s.rows_exp, 1)

            def sigmoid_of_conv(n):
                act.wait_ge(s.conv_y, n + 1)
                if n >= 2:
                    act.wait_ge(s.conv_done, n - 1)
                a.activation(CSG[:, n % 2, :], CY[:, n % 2, :], ACT.Sigmoid).then_inc(s.conv_sig, 1)

            for n, (kind, c, _u, _o) in enumerate(UT):
                b = bank[(n + 3) % 4]
                act.wait_ge(s.u_ps, n + 4)
                if kind in ("xa", "xbc"):
                    dst = CA if kind == "xa" else CBX
                    a.activation(dst[:, c, PAD:PAD + NP], b[:, 0:NP], ACT.Copy)
                    a.activation(dst[:, c, SC0 + PAD:SC0 + PAD + TAPS * (NB - 1) + 1:TAPS], b[:, NP:T],
                                 ACT.Copy).then_inc(s.lc_ready, 1)
                    a.activation(LC[:, n, :], b[:, NP - PAD:T], ACT.Copy).then_inc(u_free[(n + 3) % 4], 1)
                    if n >= 1:
                        sigmoid_of_conv(n - 1)
                else:
                    if n == NCONV:
                        sigmoid_of_conv(NCONV - 1)
                    if kind == "za":
                        a.activation(ZA[:, c, :], b[:, 0:T], ACT.Sigmoid).then_inc(u_free[(n + 3) % 4], 1)
                    else:
                        a.activation(ZB[:, c, :], b[:, 0:T], ACT.Sigmoid).then_inc(s.z_sig, 1)
            for q in range(5):
                act.wait_ge(s.lct_ps, q + 1)
                a.activation(LCT[0:LAST, q * 512:(q + 1) * 512], bank[6 + q % 2][0:LAST, :], ACT.Copy).then_inc(s.lct_sb, 1)

            act.wait_ge(s.tm_ready, 1)
            act.wait_ge(s.conv_done, NCONV)
            def head_in(h):
                if h >= 2:
                    act.wait_ge(s.nc_ps, h - 1)
                    act.wait_ge(s.qs_done, h - 1)
                act.wait_ge(s.q_ps, h + 1)
                a.activation(qT[:, h % 2, :], bank[0][:, 0:W], ACT.Copy).then_inc(s.q_sb, 1)
                act.wait_ge(s.k_ps, h + 1)
                a.activation(kT[:, h % 2, :], bank[1][:, 0:W], ACT.Copy, scale=DH ** -0.5).then_inc(s.k_sb, 1)
                act.wait_ge(s.vt_ps, h + 1)
                a.activation(vv[:, h % 2, 0:2, 0:P], bank[3][:, 0:256].rearrange("p (a b) -> p a b", b=P), ACT.Copy)
                a.activation(vv[0:16, h % 2, 2, 0:P], bank[3][0:16, 256:384], ACT.Copy)
                a.activation(VS[:, h * P:(h + 1) * P], bank[3][0:NB, 384:512], ACT.Copy).then_inc(s.v_sb, 1)

            def head_exp(h):
                act.wait_ge(s.arg_done, h + 1)
                a.activation(ARG[:, h % 2, :], ARG[:, h % 2, :], ACT.Exp, scale=-1.0).then_inc(s.exp_done, 1)

            def head_out(h):
                act.wait_ge(s.nc_ps, h + 1)
                if h >= 2:
                    act.wait_ge(cst_out[h % 2], 16 * (h // 2))
                    act.wait_ge(s.nst_ready, h - 1)
                a.activation(NUM[:, h, 0:NP], bank[6][:, 0:NP], ACT.Copy)
                a.activation(CST[:, h % 2, :], bank[6][:, NP:NP + P + 1], ACT.Copy).then_inc(s.num_sb, 1)

            head_in(0)
            for h in range(HA):
                head_exp(h)
                if h + 1 < HA:
                    head_in(h + 1)
                head_out(h)

            act.wait_ge(s.cq_ps, NB)
            a.activation(NUM[:, :, NP:T], bank[4][:, 0:64].rearrange("p (b h) -> p h b", h=HA), ACT.Copy).then_inc(s.cq_sb, 1)

            act.wait_ge(s.bt_ps, 1)
            a.activation(BT[:, 0:2, :], bank[0][:, :].rearrange("p (a b) -> p a b", b=256), ACT.Copy)
            a.activation(BT[0:16, 2, :], bank[1][0:16, 0:256], ACT.Copy)
            a.activation(BCS[:, :], bank[2][0:NB, :], ACT.Copy).then_inc(s.bt_ready, 1)
            for j in range(NG):
                act.wait_ge(s.gt_ps, j + 1)
                a.activation(GT[:, j, 0:BLK[2]], bank[3 + j][:, 0:BLK[2]], ACT.Copy)
                a.activation(GT[0:16, j, BLK[2]:BLKW], bank[3 + j][0:16, BLK[2]:BLKW], ACT.Copy).then_inc(s.gt_ready, 1)
            for h in range(HB):
                act.wait_ge(s.arg2_done, h + 1)
                a.activation(ARG[:, h % 2, :], ARG[:, h % 2, :], ACT.Exp, scale=-1.0).then_inc(s.exp2_done, 1)
            for half in range(2):
                act.wait_ge(s.sst_ps, half + 1)
                a.activation(SST[:, half, :], bank[1 + half][:, :], ACT.Copy).then_inc(s.sst_ready, 1)

            for h in range(HA):
                if h == 0:
                    act.wait_ge(s.cq_sb, 1)
                    act.wait_ge(s.num_sb, HA)
                else:
                    act.wait_ge(s.sq_ps, h)
                a.activation(SQ[:, :], NUM[:, h, :], ACT.Square).then_inc(s.sq_done, 1)
            act.wait_ge(s.rden_ready, 1)
            link(a.activation(SCL[0:HA, :], SCL[0:HA, :], ACT.Ln, bias=epst[0:HA, 0:1], scale=1.0 / DH))
            a.activation(SCL[0:HA, :], SCL[0:HA, :], ACT.Exp, scale=-0.5).then_inc(s.sc_exp, 1)
            act.wait_ge(s.ynorm_in, 1)
            for c in range(KD):
                act.wait_ge(s.sq_ps, HA + c)
                a.activation(SQ[:, :], YB[:, c, :], ACT.Square).then_inc(s.sq_done, 1)
            act.wait_ge(s.sq_ps, HA + KD)
            link(a.activation(YSC[0:NG, :], bank[6][0:NG, 0:T], ACT.Ln, bias=epst[0:NG, 0:1], scale=1.0 / (D // NG)))
            a.activation(YSC[0:NG, :], YSC[0:NG, :], ACT.Exp, scale=-0.5).then_inc(s.ysc_exp, 1)

            for i, (_t0, m) in enumerate(TOK):
                act.wait_ge(s.h_ready, i + 1)
                link(a.activation(xn[0:m, i, :], h_tok[0:m, i, :], ACT.Square, accum_out=st3[0:m, i:i + 1]))
                link(a.activation(st3[0:m, i:i + 1], st3[0:m, i:i + 1], ACT.Ln, bias=epst[0:m, 0:1], scale=1.0 / D))
                a.activation(st3[0:m, 4 + i:5 + i], st3[0:m, i:i + 1], ACT.Exp, scale=-0.5).then_inc(s.h_rstd, 1)
            act.wait_ge(s.lx_ready, 1)
            a.activation(LX[:], LX[:], ACT.Exp).then_inc(s.p1_exp, 1)
            act.wait_ge(s.l2_ready, 1)
            a.activation(r1[:, :, 3:4], r1[:, :, 3:4], ACT.Exp).then_inc(s.e2_exp, 1)

            nr = rounds_of(act)
            with act.Fori(0, nr) as r:
                for k in range(1, KD, 2):
                    act.wait_ge(s.xg_ps, r * KD + (k + 1))
                    a.activation(XG[:, k, :], bank[k][:, :], ACT.Copy, scale=PV[:, V_NFF + k:V_NFF + k + 1])\
                        .then_inc(s.xg_act, 1)
                with act.Fori(0, EG) as q:
                    act.wait_ge(s.gu_ps, (r * EG + q) * (2 * EPG) + 1)
                    act.wait_ge(s.xg_dve, r * 4 + 4)
                    act.wait_ge(s.xg_act, r * 4 + 4)
                    a.activation(XS[:], XG[:, :, bass.ds(q * P, P)], ACT.Copy).then_inc(s.xs_ready, 1)
                    with act.Fori(0, EPG) as e:
                        x2 = ((r * EG + q) * EPG + e) * 2
                        for j in range(2):
                            act.wait_ge(s.gate_ps, x2 + (j + 1))
                            a.activation(SG[:, j * 512:(j + 1) * 512], bank[2 * j][:, :], ACT.Silu)\
                                .then_inc(s.silu_done, 1)
                            if j == 1:
                                turn_hidden(act, x2, 0)
                        turn_hidden(act, x2, 1)

            for i, (_t0, m) in enumerate(TOK):
                act.wait_ge(s.h_add, nr * 6)
                link(a.activation(xn[0:m, i, :], h_tok[0:m, i, :], ACT.Square, accum_out=st3[0:m, i:i + 1]))
                link(a.activation(st3[0:m, i:i + 1], st3[0:m, i:i + 1], ACT.Ln, bias=epst[0:m, 0:1], scale=1.0 / D))
                a.activation(st3[0:m, 4 + i:5 + i], st3[0:m, i:i + 1], ACT.Exp, scale=-0.5).then_inc(s.f_rstd, 1)
            for i, (t0, m) in enumerate(TOK):
                act.wait_ge(s.y_ready, i + 1)
                dst = y_p[0, t0:t0 + m, :] if i < 2 else y_s[:, 0, :]
                act.dma_start(dst, h_tok[0:m, i, :]).then_inc(s.out_y, 16)

        @block.vector
        def _(dve):
            v = nc.vector
            links = [0]

            def link(ins):
                links[0] += 1
                ins.then_inc(dch, 1)
                dve.wait_ge(dch, links[0])

            dve.wait_ge(s.pv_ps, 1)
            v.tensor_copy(PV[:], bank[7][:, 0:132]).then_inc(s.pv_ready, 1)
            dve.wait_ge(s.pv_ready, 1)
            for i, m in enumerate((P, P, NB + META)):
                dve.wait_ge(s.rstd_ready, i + 1)
                v.tensor_scalar(xn[0:m, i, :], h_tok[0:m, i, :], st3[0:m, 4 + i:5 + i], None, ALU.mult).then_inc(s.xn_ready, 1)
            for i, m in enumerate((P, P, NB + META)):
                for half in range(2):
                    q = 2 * i + half
                    dve.wait_ge(s.ht_ps, q + 1)
                    src = bank[q][:, :].rearrange("p (k n) -> p k n", n=P)
                    gain = PV[:, V_NMIX + 4 * half:V_NMIX + 4 * half + 4]
                    ks = slice(4 * half, 4 * half + 4)
                    if i < 2:
                        v.tensor_tensor(hT[:, ks, META + i * P:META + (i + 1) * P], src, bc_last(gain, P), ALU.mult)\
                            .then_inc(s.ht_ready, 1)
                    else:
                        v.tensor_tensor(hT[:, ks, NP:T], src[:, :, 0:NB], bc_last(gain, NB), ALU.mult)
                        v.tensor_tensor(hT[:, ks, 0:META], src[:, :, NB:NB + META], bc_last(gain, META), ALU.mult)\
                            .then_inc(s.ht_ready, 1)
            dve.wait_ge(s.prev_ps, 2)
            for dst, b, n in ((CA, bank[6], KD), (CBX, bank[7], CB_T)):
                for bb in range(NB):
                    last = v.tensor_copy(dst[:, :, SC0 + TAPS * bb:SC0 + TAPS * bb + PAD],
                                         b[:, 0:n * 24].rearrange("p (c q) -> p c q", q=24)[:, :, 3 * bb:3 * bb + 3])
                last.then_inc(s.prev_ready, 1)

            dve.wait_ge(s.params_in, 16 * 13)
            dve.wait_ge(s.u_ps, 3)
            v.tensor_scalar(RI[0:HA, :], bank[0][0:HA, 0:T], c16[0:HA, 0:1], None, ALU.add).then_inc(u_free[0], 1)
            v.tensor_scalar(XR[0:HA, T:2 * T], bank[1][0:HA, 0:T], c16[0:HA, 1:2], -1.0, ALU.add, ALU.mult).then_inc(u_free[1], 1)
            v.tensor_scalar(XR[0:HB, 0:T], bank[2][0:HB, 0:T], c16[:, 2:3], None, ALU.add).then_inc(u_free[2], 1)
            dve.wait_ge(u_free[2], 1)
            dve.wait_ge(u_free[1], 1)
            v.scalar_tensor_tensor(out=HN[0:HB, :], in0=XR[0:HB, :], scalar=-1.0, in1=XR[0:HB, :], op0=ALU.mult, op1=ALU.max).then_inc(s.x_abs, 1)
            dve.wait_ge(s.x_exp, 1)
            link(v.tensor_scalar(SS[0:HB, :], EX[0:HB, :], 2.0, None, ALU.add))
            link(v.reciprocal(SS[0:HB, :], SS[0:HB, :]))
            link(v.tensor_tensor(SS[0:HB, :], SS[0:HB, :], EX[0:HB, :], ALU.mult))
            link(v.tensor_tensor(HN[0:HB, :], SS[0:HB, :], SS[0:HB, :], ALU.mult))
            link(v.tensor_scalar(EX[0:HB, :], HN[0:HB, :], ATANH[-1], None, ALU.mult))
            for cf in reversed(ATANH[:-1]):
                link(v.scalar_tensor_tensor(out=EX[0:HB, :], in0=EX[0:HB, :], scalar=cf, in1=HN[0:HB, :], op0=ALU.add, op1=ALU.mult))
            link(v.scalar_tensor_tensor(out=EX[0:HB, :], in0=EX[0:HB, :], scalar=1.0, in1=SS[0:HB, :], op0=ALU.add, op1=ALU.mult))
            link(v.tensor_scalar(HN[0:HB, :], XR[0:HB, :], 0.0, None, ALU.max))
            link(v.scalar_tensor_tensor(out=XR[0:HB, :], in0=EX[0:HB, :], scalar=2.0, in1=HN[0:HB, :], op0=ALU.mult, op1=ALU.add))
            dve.wait_ge(s.alog_exp, 1)
            link(v.tensor_scalar(SS[0:HB, 0:T], XR[0:HB, 0:T], c16[:, 5:6], None, ALU.mult))
            v.tensor_tensor_scan(AR[0:HB, 0:NP], ENM[0:HB, 0:NP], SS[0:HB, 0:NP], 0.0, ALU.mult, ALU.add)
            link(v.tensor_copy(AR[0:HB, NP:T], SS[0:HB, NP:T]))
            v.tensor_tensor_scan(BN[0:HA, 0:NP], ENM[0:HA, 0:NP], XR[0:HA, T:T + NP], 0.0, ALU.mult, ALU.add)
            link(v.tensor_copy(BN[0:HA, NP:T], XR[0:HA, T + NP:2 * T]))
            link(v.tensor_tensor(AC[0:HA, :], RI[0:HA, :], BN[0:HA, :], ALU.add))
            dve.wait_ge(s.late_in, 16 * 6)
            v.tensor_tensor_scan(MX[0:HA, 0:NP], AC[0:HA, 0:NP], AC[0:HA, 0:NP], 0.0, ALU.max, ALU.max)
            link(v.tensor_tensor(MX[0:HA, NP:T], AC[0:HA, NP:T], m0s[:, :], ALU.max))
            v.tensor_tensor(MROW[0:HA, :], MX[0:HA, :], BN[0:HA, :], ALU.subtract)
            v.tensor_scalar(c16[0:HA, 6:7], MX[0:HA, NP - 1:NP], -1.0, None, ALU.mult)
            v.tensor_scalar(c16[:, 7:8], AR[0:HB, NP - 1:NP], -1.0, None, ALU.mult)
            v.tensor_tensor(WSR[0:HA, NP:T], AC[0:HA, NP:T], MX[0:HA, NP:T], ALU.subtract)
            v.tensor_tensor(RS[:, 0:NB], m0s[:, :], MX[0:HA, NP:T], ALU.subtract)
            v.tensor_tensor(RS[:, NB:2 * NB], AC[0:HA, NP:T], MX[0:HA, NP:T], ALU.subtract)
            v.tensor_copy(RX[:, NB:2 * NB], XR[0:HB, NP:T])
            v.tensor_copy(RX[:, 16:17], c16[:, 4:5]).then_inc(s.rows_pre, 1)

            def conv_taps(n):
                kind, c, _u, _o = UT[n]
                src = CA if kind == "xa" else CBX
                w0, n0_, bcol = (V_CAW, KD, V_CAB) if kind == "xa" else (V_CBW, CB_T, V_CBB)
                y = CY[:, n % 2, :]
                dve.wait_ge(s.lc_ready, n + 1)
                if n >= 2:
                    dve.wait_ge(s.conv_done, n - 1)
                link(v.tensor_scalar(y, src[:, c, 0:W], PV[:, w0 + c:w0 + c + 1], PV[:, bcol + c:bcol + c + 1], ALU.mult, ALU.add))
                for j in range(1, TAPS):
                    wj = w0 + j * n0_ + c
                    ins = v.scalar_tensor_tensor(out=y, in0=src[:, c, j:j + W], scalar=PV[:, wj:wj + 1], in1=y,
                                                 op0=ALU.mult, op1=ALU.add)
                    if j < TAPS - 1:
                        link(ins)
                ins.then_inc(s.conv_y, 1)

            def conv_gate(n):
                kind, c, _u, _o = UT[n]
                dst = XC[:, c, :] if kind == "xa" else CBX[:, c, 0:W]
                dve.wait_ge(s.conv_sig, n + 1)
                v.tensor_tensor(dst, CY[:, n % 2, :], CSG[:, n % 2, :], ALU.mult).then_inc(s.conv_done, 1)

            dve.wait_ge(s.prev_ready, 2)
            for n in range(NCONV):
                conv_taps(n)
                if n >= 1:
                    conv_gate(n - 1)
            conv_gate(NCONV - 1)
            for n, (kind, c, _u, _o) in enumerate(UT):
                if kind == "zb":
                    dve.wait_ge(s.z_sig, c + 1)
                    v.tensor_tensor(ZB[:, c, :], bank[(n + 3) % 4][:, 0:T], ZB[:, c, :], ALU.mult).then_inc(u_free[(n + 3) % 4], 1)

            dve.wait_ge(s.tm_ps, 1)
            v.tensor_copy(TM[:, 0:2, :], bank[4][:, 0:128].rearrange("p (a b) -> p a b", b=64))
            v.tensor_copy(TM[0:16, 2, :], bank[4][0:16, 128:192]).then_inc(s.tm_ready, 1)
            dve.wait_ge(s.bcm_ps, 1)
            v.tensor_copy(BCM[:], bank[5][:, 0:128].rearrange("p (a b) -> p a b", b=16))
            v.tensor_copy(XE[:], bank[5][:, 128:128 + KD * 17].rearrange("p (a b) -> p a b", b=17)).then_inc(s.bcm_ready, 1)

            def decay_args(n, b, key, done, arg_free):
                for j, (t0, m) in enumerate(S_TILES):
                    w = NP - t0
                    last = v.scalar_tensor_tensor(out=ARG[0:m, n % 2, BLK[j]:BLK[j] + w], in0=b[0:m, t0:NP],
                                                  scalar=TM[0:m, j, key:key + 1], in1=mask[0:m, 0:w],
                                                  op0=ALU.subtract, op1=ALU.max)
                last.then_inc(done, 1)

            def head_keys(h):
                if h >= 2:
                    dve.wait_ge(s.nc_ps, h - 1)
                dve.wait_ge(s.kt_ps, h + 1)
                for j, (_t0, m) in enumerate(S_TILES):
                    last = v.tensor_scalar(kw[0:m, h % 2, j, :], bank[2][0:m, j * P:(j + 1) * P],
                                           TM[0:m, j, 8 + h:9 + h], DH ** -0.5, ALU.mult, ALU.mult)
                last.then_inc(s.kw_sb, 1)

            dve.wait_ge(s.tm_ready, 1)
            for h in range(HA):
                dve.wait_ge(s.sc_ps, h + 1)
                if h >= 2:
                    dve.wait_ge(s.nc_ps, h - 1)
                decay_args(h, bank[5], h, s.arg_done, None)
                head_keys(h)
                dve.wait_ge(s.exp_done, h + 1)
                v.tensor_tensor(ARG[:, h % 2, 0:BLK[2]], bank[4][:, 0:BLK[2]], ARG[:, h % 2, 0:BLK[2]], ALU.mult)
                v.tensor_tensor(ARG[0:16, h % 2, BLK[2]:BLKW], bank[4][0:16, BLK[2]:BLKW], ARG[0:16, h % 2, BLK[2]:BLKW],
                                ALU.mult).then_inc(s.st_done, 1)

            dve.wait_ge(s.n0_ps, 1)
            v.tensor_copy(NSTo[:], bank[0][0:HA, 64:64 + P]).then_inc(s.nst_sb, 1)
            bh = "p (b h) -> p h b"
            dve.wait_ge(s.n0_ps, 1)
            dve.wait_ge(s.qs_done, HA)
            dve.wait_ge(s.bcm_ready, 1)
            v.tensor_tensor(NT[:].rearrange(bh, h=HA), bank[0][:, 0:64].rearrange(bh, h=HA), BCM[:, :, 0:NB], ALU.mult)
            link(v.tensor_tensor(KS[:], KS[:], BCM[:, :, NB:2 * NB], ALU.mult))
            link(v.tensor_tensor(N1[:].rearrange(bh, h=HA), NT[:].rearrange(bh, h=HA), KS[:], ALU.add))
            v.tensor_tensor(QN[:].rearrange(bh, h=HA), N1[:].rearrange(bh, h=HA), QS[:], ALU.mult).then_inc(s.n1_ready, 1)
            dve.wait_ge(s.n1_ps, 1)
            v.tensor_copy(N1T[:], bank[5][0:64, 0:P]).then_inc(s.n1_sb, 1)
            tmp3 = TMPS.rearrange("p (a b) -> p a b", b=P)
            for b in range(NB):
                dve.wait_ge(s.vb_ps, b + 1)
                if b >= 1:
                    dve.wait_ge(s.st_new, b)
                for j in range(2):
                    last = v.tensor_tensor(tmp3[:, 4 * j:4 * j + 4, :], bank[2 * (b % 2) + j][:, :].rearrange("p (a b) -> p a b", b=P),
                                           bc_last(KS[:, 4 * j:4 * j + 4, b], P), ALU.mult)
                link(last)
                dve.wait_ge(s.st_dec, b + 1)
                st = stage[:, b % 3, :]
                v.tensor_tensor(st, st, TMPS, ALU.add).then_inc(s.st_new, 1)

            for j, (_t0, m) in enumerate(S_TILES):
                for half in range(2):
                    q = 2 * j + half
                    dve.wait_ge(s.xs_ps, q + 1)
                    v.tensor_tensor(XDT[0:m, j, half * 512:(half + 1) * 512].rearrange("p (h q) -> p h q", q=HD),
                                    bank[q][0:m, :].rearrange("p (h q) -> p h q", q=HD),
                                    bc_last(TM[0:m, j, 32 + 8 * half:40 + 8 * half], HD), ALU.mult).then_inc(s.xdt_ready, 1)
            for h in range(HB):
                dve.wait_ge(s.bc_ps, h + 1)
                if h >= 2:
                    dve.wait_ge(s.y_ps, h - 1)
                decay_args(h, bank[5 - h % 2], 16 + h, s.arg2_done, None)
                if h == 0:
                    dve.wait_ge(s.gt_ready, NG)
                dve.wait_ge(s.exp2_done, h + 1)
                j = h // (HB // NG)
                v.tensor_tensor(ARG[:, h % 2, 0:BLK[2]], GT[:, j, 0:BLK[2]], ARG[:, h % 2, 0:BLK[2]], ALU.mult)
                v.tensor_tensor(ARG[0:16, h % 2, BLK[2]:BLKW], GT[0:16, j, BLK[2]:BLKW], ARG[0:16, h % 2, BLK[2]:BLKW],
                                ALU.mult).then_inc(s.st2_done, 1)
                if h % 2 == 0 and h >= 2:
                    ssd_out(dve, h // 2 - 1)
            ssd_out(dve, KD - 1)

            xs_s = CBX[:, 0:KD, SC0:SC0 + TAPS * (NB - 1) + 1:TAPS]
            v.tensor_tensor(YS2[:], xs_s, XE[:, :, 16:17].to_broadcast([P, KD, NB]), ALU.mult)
            link(v.tensor_tensor(XDS[:], xs_s, XE[:, :, NB:2 * NB], ALU.mult))
            for b in range(NB):
                dve.wait_ge(s.bb_ps, b + 1)
                if b == 0:
                    dve.wait_ge(s.st_new, NB)
                bb = bank[3 + b % 2]
                for j in range(NG):
                    last = v.tensor_tensor(tmp3[:, 4 * j:4 * j + 4, :], bb[:, j * P:(j + 1) * P].unsqueeze(1).to_broadcast([P, 4, P]),
                                           bc_last(XDS[:, 4 * j:4 * j + 4, b], P), ALU.mult)
                link(last)
                dve.wait_ge(s.st_dec, NB + b + 1)
                st = stage[:, (NB + b) % 3, :]
                st3d = st.rearrange("p (a b) -> p a b", b=P)
                v.tensor_tensor(st, st, TMPS, ALU.add).then_inc(s.st_new, 1)
                dve.wait_ge(s.st_new, NB + b + 1)
                for j in range(NG):
                    last = v.tensor_tensor(tmp3[:, 4 * j:4 * j + 4, :], st3d[:, 4 * j:4 * j + 4, :],
                                           bb[:, 256 + j * P:256 + (j + 1) * P].unsqueeze(1).to_broadcast([P, 4, P]), ALU.mult)
                last.then_inc(s.s_y, 1)
                dve.wait_ge(s.s_y, b + 1)
                link(v.tensor_reduce(YS[:, :, b], tmp3, AX, ALU.add))
            link(v.tensor_tensor(YB[:, :, NP:T], YS[:], YS2[:], ALU.add))

            dve.wait_ge(s.conv_done, NCONV)
            v.tensor_tensor(YB, YB, ZB, ALU.mult).then_inc(s.ynorm_in, 1)
            dve.wait_ge(s.sq_ps, HA)
            dve.wait_ge(s.den_ps, 1)
            link(v.tensor_copy(DEN[0:HA, :], bank[7][0:HA, 0:T]))
            link(v.scalar_tensor_tensor(out=DEN[0:HA, :], in0=DEN[0:HA, :], scalar=-1.0, in1=DEN[0:HA, :], op0=ALU.mult, op1=ALU.max))
            link(v.tensor_tensor(DEN[0:HA, :], DEN[0:HA, :], ENM[0:HA, :], ALU.max))
            link(v.reciprocal(DEN[0:HA, :], DEN[0:HA, :]))
            link(v.tensor_tensor(SCL[0:HA, :], bank[0][0:HA, 0:T], DEN[0:HA, :], ALU.mult))
            v.tensor_tensor(SCL[0:HA, :], SCL[0:HA, :], DEN[0:HA, :], ALU.mult).then_inc(s.rden_ready, 1)
            dve.wait_ge(s.sc_exp, 1)
            v.tensor_tensor(SCL[0:HA, :], SCL[0:HA, :], DEN[0:HA, :], ALU.mult).then_inc(s.scale_ready, 1)
            for h in range(HA):
                dve.wait_ge(s.hbc_ps, h + 1)
                link(v.scalar_tensor_tensor(out=NUM[:, h, :], in0=bank[1 + h % 4][:, 0:T], scalar=PV[:, V_NA + h:V_NA + h + 1],
                                            in1=NUM[:, h, :], op0=ALU.mult, op1=ALU.mult))
                v.tensor_tensor(NUM[:, h, :], NUM[:, h, :], ZA[:, h, :], ALU.mult).then_inc(s.num_ready, 1)
            for c in range(KD):
                if c % 4 == 0:
                    dve.wait_ge(s.gbc_ps, c // 4 + 1)
                v.scalar_tensor_tensor(out=YB[:, c, :], in0=bank[7 if c < 4 else 5][:, 0:T],
                                       scalar=PV[:, V_NB + c:V_NB + c + 1], in1=YB[:, c, :],
                                       op0=ALU.mult, op1=ALU.mult).then_inc(s.yb_norm, 1)

            for i, (_t0, m) in enumerate(TOK):
                if i == 0:
                    dve.wait_ge(s.x_again, 16 * 3)
                    dve.wait_ge(s.wo_unit, 4)
                for half in range(2):
                    hv = h_tok[0:m, i, half * 512:(half + 1) * 512]
                    last = v.tensor_tensor(hv, hv, bank[2 * i + half][0:m, :], ALU.add)
                last.then_inc(s.h_ready, 1)
            for i, (_t0, m) in enumerate(TOK):
                dve.wait_ge(s.h_rstd, i + 1)
                v.tensor_scalar(xn[0:m, i, :], h_tok[0:m, i, :], st3[0:m, 4 + i:5 + i], None, ALU.mult).then_inc(s.xn2_ready, 1)
            for i, (t0, m) in enumerate(TOK):
                for half in range(2):
                    q = 2 * i + half
                    dve.wait_ge(s.xt_ps, q + 1)
                    src = bank[q][:, :].rearrange("p (k n) -> p k n", n=P)
                    gain = PV[:, V_NFF + 4 * half:V_NFF + 4 * half + 4]
                    v.tensor_tensor(XT[:, 4 * half:4 * half + 4, t0:t0 + m], src[:, :, 0:m], bc_last(gain, m), ALU.mult)\
                        .then_inc(s.xt_ready, 1)
            dve.wait_ge(s.lg_ps, 1)
            v.tensor_copy(L[:, 0:2, :], bank[6][:, 0:40].rearrange("p (a b) -> p a b", b=20))
            link(v.tensor_copy(L[0:NB, 2, :], bank[6][0:NB, 40:60]))
            LG = L[:, :, 0:4]

            def bc4(c):
                return r1[:, :, c:c + 1].to_broadcast([P, 3, 4])

            ord3 = order[:].unsqueeze(1).to_broadcast([P, 3, 4])

            def first_best(out, vals, c, ck):
                link(v.tensor_tensor(K1[:], vals, bc4(c), ALU.is_equal))
                link(v.tensor_tensor(K1[:], K1[:], ord3, ALU.mult))
                link(v.tensor_reduce(r1[:, :, ck], K1[:], AX, ALU.max))
                link(v.tensor_tensor(out, K1[:], bc4(ck), ALU.is_equal))

            link(v.tensor_reduce(r1[:, :, 0], LG, AX, ALU.max))
            v.tensor_tensor(LX[:], LG, bc4(0), ALU.subtract).then_inc(s.lx_ready, 1)
            first_best(M1[:], LG, 0, 1)
            for i in range(3):
                last = v.tensor_tensor(LP[:, i], L[:, i, 4:20].rearrange("p (g e) -> p e g", g=EG),
                                       M1[:, i, :].unsqueeze(1).to_broadcast([P, EPG, EG]), ALU.mult)
            link(last)
            link(v.tensor_reduce(L2[:], LP[:], AX, ALU.add))
            link(v.tensor_reduce(r1[:, :, 2], L2[:], AX, ALU.max))
            first_best(O1[:], L2[:], 2, 1)
            link(v.scalar_tensor_tensor(out=L2[:], in0=O1[:], scalar=-BIG, in1=L2[:], op0=ALU.mult, op1=ALU.add))
            link(v.tensor_reduce(r1[:, :, 4], L2[:], AX, ALU.max))
            v.tensor_tensor(r1[:, :, 3], r1[:, :, 4], r1[:, :, 2], ALU.subtract).then_inc(s.l2_ready, 1)
            first_best(O2[:], L2[:], 4, 1)
            dve.wait_ge(s.p1_exp, 1)
            link(v.tensor_reduce(r1[:, :, 5], LX[:], AX, ALU.add))
            dve.wait_ge(s.e2_exp, 1)
            link(v.tensor_scalar(r1[:, :, 6], r1[:, :, 3], 1.0, None, ALU.add))
            link(v.tensor_tensor(r1[:, :, 6], r1[:, :, 6], r1[:, :, 5], ALU.mult))
            link(v.reciprocal(r1[:, :, 6], r1[:, :, 6]))
            link(v.tensor_tensor(r1[:, :, 7], r1[:, :, 6], r1[:, :, 3], ALU.mult))
            v.tensor_tensor(O1[:], O1[:], bc4(6), ALU.mult)
            link(v.tensor_tensor(O2[:], O2[:], bc4(7), ALU.mult))
            v.tensor_tensor(GATE[:], O1[:], O2[:], ALU.add).then_inc(s.router, 1)
            dve.wait_ge(s.rank_ps, 1)
            v.tensor_copy(rank[:, 0:2, :], bank[0][:, 0:8].rearrange("p (a b) -> p a b", b=4))
            v.tensor_copy(rank[0:NB, 2, :], bank[0][0:NB, 8:12]).then_inc(s.rank_ready, 1)
            link(v.tensor_reduce(cnt[:, 0:1], bank[0][:, 12:16], AX, ALU.max))
            v.tensor_scalar(cnt[:, 1:2], cnt[:, 0:1], 128.0, 1.0, ALU.is_gt, ALU.add).then_inc(s.yg_done, 1)
            link(v.tensor_scalar(cnt[:, 2:3], cnt[:, 0:1], 256.0, None, ALU.is_gt))
            v.tensor_tensor(rounds[:], cnt[:, 1:2], cnt[:, 2:3], ALU.add).then_inc(s.rounds_ready, 1)

            nr = rounds_of(dve)
            with dve.Fori(0, nr) as r:
                dve.wait_ge(s.rank_ready, r + 1)
                for i, (_t0, m) in enumerate(TOK):
                    for q in range(EG):
                        last = v.tensor_scalar(PG[0:m, i, q * P:(q + 1) * P], iota[0:m, :], rank[0:m, i, q:q + 1],
                                               M1[0:m, i, q:q + 1], ALU.is_equal, ALU.mult)
                last.then_inc(s.p_ready, 1)
                for k in range(0, KD, 2):
                    dve.wait_ge(s.xg_ps, r * KD + (k + 1))
                    v.tensor_scalar(XG[:, k, :], bank[k][:, :], PV[:, V_NFF + k:V_NFF + k + 1], None, ALU.mult)\
                        .then_inc(s.xg_dve, 1)
                dve.wait_ge(s.pt_ps, r + 1)
                v.tensor_copy(GS[:], bank[0][:, 0:16])
                for q in range(EG):
                    last = v.tensor_copy(PT[:, q, :], bank[1 + q][:, 0:NOUT])
                last.then_inc(s.pt_ready, 1)
                v.memset(YG.rearrange("p a b -> p (a b)"), 0.0).then_inc(s.yg_zero, 1)
                with dve.Fori(0, EG) as q:
                    with dve.Fori(0, EPG) as e:
                        x = (r * EG + q) * EPG + e
                        for j in range(2):
                            if j == 0:
                                dve.wait_ge(s.pt_ready, r + 1)
                            dve.wait_ge(s.silu_done, x * 2 + (j + 1))
                            dve.wait_ge(s.gu_ps, x * 2 + (j + 2))
                            v.scalar_tensor_tensor(out=AH[:, j * 512:(j + 1) * 512], in0=bank[2 * j + 1][:, :],
                                                   scalar=GS[:, bass.ds(q * EPG + e, 1)], in1=SG[:, j * 512:(j + 1) * 512],
                                                   op0=ALU.mult, op1=ALU.mult).then_inc(s.a_ready, 1)
                        dve.wait_ge(s.d_ps, x + 1)
                        dve.wait_ge(s.yg_zero, r + 1)
                        dve.wait_ge(s.yg_done, x + 1)
                        yv = YG.rearrange("p a b -> p (a b)")
                        for j in range(2):
                            o = yv[:, bass.ds(q * D + j * 512, 512)]
                            last = v.tensor_tensor(o, o, bank[6 + j][:, :], ALU.add)
                        last.then_inc(s.yg_done, 1)
                for i, (_t0, m) in enumerate(TOK):
                    for half in range(2):
                        dve.wait_ge(s.sc_out_ps, r * 6 + (2 * i + half + 1))
                        hv = h_tok[0:m, i, half * 512:(half + 1) * 512]
                        v.tensor_tensor(hv, hv, bank[2 * i + half][0:m, :], ALU.add).then_inc(s.h_add, 1)
                v.tensor_scalar(rank[:, 0:2, :], rank[:, 0:2, :], float(P), None, ALU.subtract)
                v.tensor_scalar(rank[0:NB, 2, :], rank[0:NB, 2, :], float(P), None, ALU.subtract).then_inc(s.rank_ready, 1)

            dve.wait_ge(s.nf_in, 16)
            for i, (_t0, m) in enumerate(TOK):
                dve.wait_ge(s.f_rstd, i + 1)
                v.scalar_tensor_tensor(out=h_tok[0:m, i, :], in0=h_tok[0:m, i, :], scalar=st3[0:m, 4 + i:5 + i],
                                       in1=NF[0:m, :], op0=ALU.mult, op1=ALU.mult).then_inc(s.y_ready, 1)

        @block.tensor
        def _(pe):
            mm = nc.tensor.matmul
            tr = nc.tensor.transpose

            pe.wait_ge(s.consts, 1)
            pe.wait_ge(s.params_in, 16 * 13)
            tr(bank[7][:, 0:84], PR[0:84, 0, :], ident[0:84, 0:84])
            tr(bank[7][:, 84:132], PR[0:48, 1, :], ident[0:48, 0:48]).then_inc(s.pv_ps, 1)
            for i, m in enumerate((P, P, NB + META)):
                pe.wait_ge(s.xn_ready, i + 1)
                for k in range(KD):
                    last = tr(bank[2 * i + k // 4][:, (k % 4) * P:(k % 4) * P + m], xn[0:m, i, k * P:(k + 1) * P], ident[0:m, 0:m])
                    if k % 4 == 3:
                        last.then_inc(s.ht_ps, 1)
            pe.wait_ge(s.prev_in, 32)
            pe.wait_ge(s.pv_ready, 1)
            for base, b, n in ((0, bank[6], KD), (KD, bank[7], CB_T)):
                for c in range(n):
                    last = tr(b[:, c * 24:(c + 1) * 24], CPREV[0:24, (base + c) * P:(base + c + 1) * P], ident[0:24, 0:24])
                last.then_inc(s.prev_ps, 1)

            pe.wait_ge(s.ht_ready, 6)
            pe.wait_ge(s.gates_in, 32)
            for n, (c0, m) in enumerate(((0, 8), (8, 8), (16, 16))):
                for k in range(KD):
                    last = mm(bank[n][0:m, 0:T], WG[:, k, c0:c0 + m], hT[:, k, :], start=(k == 0), stop=(k == KD - 1))
                last.then_inc(s.u_ps, 1)
            for n0_, (kind, c, u, o) in enumerate(UT):
                n = n0_ + 3
                if o == 0:
                    i, cnt_ = unit_at(u)
                    pe.wait_ge(arrived[i], cnt_)
                if n >= 4:
                    pe.wait_ge(u_free[n % 4], n // 4)
                for k in range(KD):
                    last = mm(bank[n % 4][:, 0:T], slot_k(u % MR, 512)[:, k, o:o + P], hT[:, k, :],
                              start=(k == 0), stop=(k == KD - 1))
                last.then_inc(s.u_ps, 1)

            pe.wait_ge(s.rows_pre, 1)
            pe.wait_ge(s.rows_exp, 1)
            for j, (t0, m) in enumerate(S_TILES):
                for rows, nrow, c0 in ((AC, HA, 0), (WSR, HA, 8), (AR, HB, 16), (XR, HB, 32), (EDR, HB, 48)):
                    last = tr(bank[4][0:m, j * 64 + c0:j * 64 + c0 + nrow], rows[0:nrow, t0:t0 + m], ident[0:nrow, 0:nrow])
            last.then_inc(s.tm_ps, 1)
            for h in range(HA):
                mm(bank[5][:, h * 16:(h + 1) * 16], col(ident[0:HA, :], h), RS[:, :], start=True, stop=True)
            for c in range(KD):
                for j in range(2):
                    last = mm(bank[5][j * HD:(j + 1) * HD, 128 + c * 17:128 + (c + 1) * 17],
                              ident[0:HB, 2 * c + j:2 * c + j + 1].to_broadcast([HB, HD]), RX[:, :], start=True, stop=True)
            last.then_inc(s.bcm_ps, 1)
            for q in range(5):
                if q >= 2:
                    pe.wait_ge(s.lct_sb, q - 1)
                if q == 0:
                    pe.wait_ge(u_free[(NCONV + 2) % 4], (NCONV + 2) // 4 + 1)
                for c in range(4):
                    last = tr(bank[6 + q % 2][0:LAST, c * P:(c + 1) * P], LC[:, 4 * q + c, :], ident[:, :])
                last.then_inc(s.lct_ps, 1)

            iq, cq = unit_at(U_QKV)
            pe.wait_ge(arrived[iq], cq)
            wq, wk, wv = (slot[iq][:, j * D:(j + 1) * D].rearrange("p (h e) -> p h e", e=DH) for j in range(3))
            pe.wait_ge(s.conv_done, NCONV)
            for b, n in enumerate((10, 10, 10, 9)):
                pe.wait_ge(u_free[b], n)

            def head_proj(h):
                if h >= 1:
                    pe.wait_ge(s.q_sb, h)
                    pe.wait_ge(s.k_sb, h)
                    pe.wait_ge(s.kw_sb, h)
                    pe.wait_ge(s.v_sb, h)
                mm(bank[0][:, 0:W], wq[:, h, :], XC[:, h, :], start=True, stop=True).then_inc(s.q_ps, 1)
                mm(bank[1][:, 0:W], wk[:, h, :], XC[:, h, :], start=True, stop=True).then_inc(s.k_ps, 1)
                for j, (t0, m) in enumerate(S_TILES):
                    last = mm(bank[2][0:m, j * P:(j + 1) * P], XC[:, h, t0:t0 + m], wk[:, h, :], start=True, stop=True)
                last.then_inc(s.kt_ps, 1)
                for j, (t0, m) in enumerate(S_TILES):
                    mm(bank[3][0:m, j * P:(j + 1) * P], CA[:, h, PAD + t0:PAD + t0 + m], wv[:, h, :], start=True, stop=True)
                mm(bank[3][0:NB, 384:512], CA[:, h, SC0 + PAD:SC0 + PAD + TAPS * (NB - 1) + 1:TAPS], wv[:, h, :],
                   start=True, stop=True).then_inc(s.vt_ps, 1)

            def block_mm(b, c0, lhs, rhs, key, start, accumulate):
                for j, (t0, m) in enumerate(S_TILES):
                    w = NP - t0
                    if accumulate:
                        o = b[:, c0 + t0:c0 + NP]
                    else:
                        o = b[0:m, BLK[j]:BLK[j] + w]
                    last = mm(o, lhs(j, t0, m), rhs(j, t0, m, w), start=(start and (j == 0 or not accumulate)),
                              stop=(j == 2 or not accumulate))
                return last

            head_proj(0)
            pe.wait_ge(s.tm_ready, 1)
            pe.wait_ge(s.bcm_ready, 1)
            for h in range(HA):
                if h >= 1:
                    pe.wait_ge(s.st_done, h)
                pe.wait_ge(s.q_sb, h + 1)
                pe.wait_ge(s.k_sb, h + 1)
                mm(bank[5][:, 0:NP], col(ident[0:HA, :], h), MX[0:HA, 0:NP], start=True, stop=True)
                block_mm(bank[4], 0, lambda j, t0, m: kT[:, h % 2, t0:t0 + m], lambda j, t0, m, w: qT[:, h % 2, t0:NP],
                         None, True, False).then_inc(s.sc_ps, 1)
                if h + 1 < HA:
                    head_proj(h + 1)
                pe.wait_ge(s.st_done, h + 1)
                pe.wait_ge(s.v_sb, h + 1)
                pe.wait_ge(s.kw_sb, h + 1)
                if h >= 1:
                    pe.wait_ge(s.num_sb, h)
                else:
                    pe.wait_ge(s.lct_sb, 5)
                sc = lambda j, t0, m, w: ARG[0:m, h % 2, BLK[j]:BLK[j] + w]
                block_mm(bank[6], 0, lambda j, t0, m: vv[0:m, h % 2, j, 0:P], sc, None, True, True)
                for j, (t0, m) in enumerate(S_TILES):
                    mm(bank[7][0:HA, t0:NP], strip[0:m, 7 - h:15 - h], sc(j, t0, m, NP - t0),
                       start=(h == 0 and j == 0), stop=(h == HA - 1 and j == 2), skip_group_check=True)
                for j, (t0, m) in enumerate(S_TILES):
                    last = mm(bank[6][:, NP:NP + P + 1], kw[0:m, h % 2, j, :], vv[0:m, h % 2, j, :], start=(j == 0), stop=(j == 2))
                last.then_inc(s.nc_ps, 1)

            pe.wait_ge(s.late_in, 16 * 6)
            pe.wait_ge(s.nst_ready, HA)
            tr(bank[0][:, 0:64], N0[:, :], ident[0:64, 0:64])
            tr(bank[0][0:HA, 64:64 + P], NSTt[:, :], ident[:, :]).then_inc(s.n0_ps, 1)
            pe.wait_ge(s.n1_ready, 1)
            for h in range(HA):
                last = mm(bank[7][0:HA, NP:T], strip[:, 7 - h:15 - h], QN[:].rearrange("p (b h) -> p h b", h=HA)[:, h, :],
                          start=(h == 0), stop=(h == HA - 1), skip_group_check=True)
            last.then_inc(s.den_ps, 1)
            tr(bank[5][0:64, 0:P], N1[:, :], ident[:, :]).then_inc(s.n1_ps, 1)

            for b in range(NB + 1):
                if b < NB:
                    if b == 0:
                        pe.wait_ge(s.nst_sb, 1)
                        pe.wait_ge(s.num_sb, HA)
                    if b >= 2:
                        pe.wait_ge(s.st_new, b - 1)
                    for j in range(2):
                        last = mm(bank[2 * (b % 2) + j][:, :], col(ident[0:NB, :], b), VS[:, j * 512:(j + 1) * 512], start=True, stop=True)
                    last.then_inc(s.vb_ps, 1)
                if b >= 1:
                    pe.wait_ge(s.st_new, b)
                    for h in range(HA):
                        last = mm(bank[4][:, (b - 1) * HA + h:(b - 1) * HA + h + 1],
                                  stage[:, (b - 1) % 3, h * P:(h + 1) * P], QS[:, h, b - 1:b], start=True, stop=True)
                    last.then_inc(s.cq_ps, 1)

            for j, (t0, m) in enumerate(S_TILES):
                for half in range(2):
                    q = 2 * j + half
                    if q == 0:
                        pe.wait_ge(s.cq_sb, 1)
                        pe.wait_ge(s.n1_sb, 1)
                    bq = bank[q]
                    for c in range(4):
                        last = tr(bq[0:m, c * P:(c + 1) * P], CBX[:, 4 * half + c, t0:t0 + m], ident[:, :])
                    last.then_inc(s.xs_ps, 1)
            pe.wait_ge(s.xdt_ready, 6)
            for j, (t0, m) in enumerate(S_TILES):
                for g_ in range(NG):
                    tr(bank[j // 2][0:m, (j % 2) * 256 + g_ * P:(j % 2) * 256 + (g_ + 1) * P], CBX[:, KD + g_, t0:t0 + m], ident[:, :])
            for c in range(4):
                last = tr(bank[2][0:NB, c * P:(c + 1) * P], smp(CBX[:, KD + c, :]), ident[:, :])
            last.then_inc(s.bt_ps, 1)
            for g_ in range(NG):
                block_mm(bank[3 + g_], 0, lambda j, t0, m: CBX[:, KD + g_, t0:t0 + m], lambda j, t0, m, w: CBX[:, KD + NG + g_, t0:NP],
                         None, True, False).then_inc(s.gt_ps, 1)

            def decay_row(h):
                if h >= 2:
                    pe.wait_ge(s.arg2_done, h - 1)
                elif h == 1:
                    pe.wait_ge(s.gt_ready, NG)
                mm(bank[5 - h % 2][:, 0:NP], col(ident[0:HB, :], h), AR[0:HB, 0:NP], start=True, stop=True).then_inc(s.bc_ps, 1)

            decay_row(0)
            for h in range(HB):
                c = h // 2
                if h + 1 < HB:
                    decay_row(h + 1)
                pe.wait_ge(s.st2_done, h + 1)
                if h == 0:
                    pe.wait_ge(s.bt_ready, 1)
                if h % 2 == 0 and c >= 2:
                    pe.wait_ge(y_free[c % 2], c // 2)
                yb = bank[6 if c % 2 == 0 else 0]
                q0 = HD * (h % 2)
                for j, (t0, m) in enumerate(S_TILES):
                    last = mm(yb[q0:q0 + HD, t0:NP], XDT[0:m, j, h * HD:(h + 1) * HD], ARG[0:m, h % 2, BLK[j]:BLK[j] + NP - t0],
                              start=(j == 0), stop=(j == 2))
                last.then_inc(s.y_ps, 1)
            pe.wait_ge(s.xw_ready, 3)
            for half in range(2):
                for c in range(4):
                    ct = 4 * half + c
                    for j, (t0, m) in enumerate(S_TILES):
                        last = mm(bank[1 + half][:, c * P:(c + 1) * P], XWT[0:m, j, ct * P:(ct + 1) * P],
                                  BT[0:m, j, half * P:(half + 1) * P], start=(j == 0), stop=(j == 2))
                last.then_inc(s.sst_ps, 1)
            pe.wait_ge(s.arg2_done, HB)
            for b in range(NB):
                if b >= 2:
                    pe.wait_ge(s.s_y, b - 1)
                mm(bank[3 + b % 2][:, :], col(ident[0:NB, :], b), BCS[:, :], start=True, stop=True).then_inc(s.bb_ps, 1)

            pe.wait_ge(y_free[0], 4)
            pe.wait_ge(y_free[1], 4)
            for h in range(HA):
                pe.wait_ge(s.sq_done, h + 1)
                mm(bank[0][0:HA, 0:T], strip[:, 7 - h:15 - h], SQ[:, :], start=(h == 0), stop=(h == HA - 1)).then_inc(s.sq_ps, 1)
            pe.wait_ge(s.scale_ready, 1)
            pe.wait_ge(s.sst_ready, 2)
            for h in range(HA):
                if h >= 4:
                    pe.wait_ge(s.num_ready, h - 3)
                else:
                    pe.wait_ge(s.s_y, NB)
                mm(bank[1 + h % 4][:, 0:T], col(ident[0:HA, :], h), SCL[0:HA, :], start=True, stop=True).then_inc(s.hbc_ps, 1)
            for c in range(KD):
                pe.wait_ge(s.sq_done, HA + c + 1)
                g_ = c // 4
                mm(bank[6][0:NG, 0:T], strip[:, 7 - g_:9 - g_], SQ[:, :], start=(c == 0), stop=(c == KD - 1)).then_inc(s.sq_ps, 1)
            pe.wait_ge(s.ysc_exp, 1)
            for g_ in range(NG):
                mm(bank[7 if g_ == 0 else 5][:, 0:T], col(ident[0:NG, :], g_), YSC[0:NG, :], start=True, stop=True).then_inc(s.gbc_ps, 1)

            pe.wait_ge(s.num_ready, HA)
            for j in range(4):
                u = U_OUT + j
                i, cnt_ = unit_at(u)
                pe.wait_ge(arrived[i], cnt_)
                if j == 0:
                    pe.wait_ge(s.yb_norm, KD)
                for kk in range(4):
                    kc = 4 * j + kk
                    src = NUM if kc < HA else YB
                    for ti, (t0, m) in enumerate(TOK):
                        for half in range(2):
                            last = mm(bank[2 * ti + half][0:m, :], src[:, kc % 8, META + t0:META + t0 + m],
                                      slot_k(i, D)[:, kk, half * 512:(half + 1) * 512],
                                      start=(kc == 0), stop=(kc == 15), skip_group_check=True)
                last.then_inc(s.wo_unit, 1)

            for i, (t0, m) in enumerate(TOK):
                pe.wait_ge(s.xn2_ready, i + 1)
                if i == 0:
                    pe.wait_ge(s.h_ready, 3)
                for k in range(KD):
                    last = tr(bank[2 * i + k // 4][:, (k % 4) * P:(k % 4) * P + m], xn[0:m, i, k * P:(k + 1) * P], ident[0:m, 0:m])
                    if k % 4 == 3:
                        last.then_inc(s.xt_ps, 1)
            pe.wait_ge(s.late_in, 16 * 6)
            pe.wait_ge(s.xt_ready, 6)
            for i, (t0, m) in enumerate(TOK):
                for k in range(KD):
                    mm(bank[6][0:m, i * 20:(i + 1) * 20], XT[:, k, t0:t0 + m], wr[:, k, :], start=(k == 0), stop=False)
                last = mm(bank[6][0:m, i * 20:(i + 1) * 20], ones[0:1, 0:m], br[:, :], start=False, stop=True)
            last.then_inc(s.lg_ps, 1)
            pe.wait_ge(s.router, 1)
            for i, (_t0, m) in enumerate(TOK):
                for i2 in range(i):
                    mm(bank[0][0:m, 4 * i:4 * i + 4], ones[:, 0:m], M1[:, i2, :], start=(i2 == 0), stop=False)
                last = mm(bank[0][0:m, 4 * i:4 * i + 4], before[0:m, 0:m], M1[0:m, i, :], start=(i == 0), stop=True)
            last.then_inc(s.gu_ps, 1)
            for i, (_t0, m) in enumerate(TOK):
                last = mm(bank[0][:, 12:16], ones[0:m, :], M1[0:m, i, :], start=(i == 0), stop=(i == 2))
            last.then_inc(s.rank_ps, 1)

            nr = rounds_of(pe)
            with pe.Fori(0, nr) as r:
                pe.wait_ge(s.p_ready, r + 1)
                for k in range(KD):
                    for i, (_t0, m) in enumerate(TOK):
                        last = mm(bank[k][:, :], xn[0:m, i, k * P:(k + 1) * P], PG[0:m, i, :], start=(i == 0), stop=(i == 2))
                    last.then_inc(s.xg_ps, 1)
                pe.wait_ge(s.xg_dve, r * 4 + 4)
                pe.wait_ge(s.xg_act, r * 4 + 4)
                for q in range(EG):
                    for i, (_t0, m) in enumerate(TOK):
                        last = mm(bank[0][:, 4 * q:4 * q + 4], PG[0:m, i, q * P:(q + 1) * P], GATE[0:m, i, :], start=(i == 0), stop=(i == 2))
                for q in range(EG):
                    for i, (t0, m) in enumerate(TOK):
                        last = tr(bank[1 + q][:, t0:t0 + m], PG[0:m, i, q * P:(q + 1) * P], ident[0:m, 0:m])
                last.then_inc(s.pt_ps, 1)
                with pe.Fori(0, EG) as q:
                    with pe.Fori(0, EPG) as e:
                        x = (r * EG + q) * EPG + e
                        pe.wait_ge(s.pt_ready, r + 1)
                        pe.wait_ge(s.xs_ready, r * EG + q + 1)

                        def weights(c):
                            i = EXP_SLOT[c]
                            pe.wait_ge(arrived[i], x * 16 + (mix_in[i] + 16))
                            return slot_k(i, 512 if c < 4 else D)

                        def project(j, up):
                            w = weights(2 * j + up)
                            for k in range(KD):
                                last = mm(bank[2 * j + up][:, :], XS[:, k, :], w[:, k, :], start=(k == 0), stop=(k == KD - 1))
                            return last

                        def turn(j):
                            pe.wait_ge(s.a_ready, x * 2 + (j + 1))
                            for k in range(4):
                                last = tr(bank[4 + j][:, k * P:(k + 1) * P], AH[:, (4 * j + k) * P:(4 * j + k + 1) * P], ident[:, :])
                            last.then_inc(s.ft_ps, 1)

                        def down(j, half, w):
                            for k in range(4):
                                last = mm(bank[6 + half][:, :], HT[:, 4 * j + k, :], w[:, k, half * 512:(half + 1) * 512],
                                          start=(j == 0 and k == 0), stop=(j == 1 and k == 3), skip_group_check=True)
                            return last

                        project(0, 0).then_inc(s.gate_ps, 1)
                        project(0, 1).then_inc(s.gu_ps, 1)
                        project(1, 0).then_inc(s.gate_ps, 1)
                        turn(0)
                        project(1, 1).then_inc(s.gu_ps, 1)
                        pe.wait_ge(s.yg_done, x + 1)
                        pe.wait_ge(s.ht_sb, x * 2 + 1)
                        w = weights(4)
                        down(0, 0, w)
                        turn(1)
                        down(0, 1, w).then_inc(s.down_ps, 1)
                        pe.wait_ge(s.ht_sb, x * 2 + 2)
                        w = weights(5)
                        down(1, 0, w)
                        down(1, 1, w).then_inc(s.d_ps, 1)
                pe.wait_ge(s.yg_done, (r + 1) * (EG * EPG) + 1)
                for i, (t0, m) in enumerate(TOK):
                    for half in range(2):
                        for q in range(EG):
                            last = mm(bank[2 * i + half][0:m, :], PT[:, q, t0:t0 + m], YG[:, q, half * 512:(half + 1) * 512],
                                      start=(q == 0), stop=(q == EG - 1))
                        last.then_inc(s.sc_out_ps, 1)
                pe.wait_ge(s.h_add, r * 6 + 6)


_INS = ["x_prompt", "x_sample", "state_mlstm_C", "state_mlstm_n", "state_mlstm_m", "state_mlstm_conv",
        "state_ssm", "state_ssm_conv", "meta_tokens", "norm_mix", "w_in", "conv_a_w", "conv_a_b", "w_q",
        "w_k", "w_v", "b_i", "b_f", "norm_a", "conv_b_w", "conv_b_b", "dt_bias", "a_log", "d_skip",
        "norm_b", "w_out", "norm_ffn", "w_r1", "b_r1", "w_r2", "b_r2", "w_gate", "w_up", "w_down",
        "norm_final"]
_OUTS = [(1, SEQ, D), (NB, 1, D),
         (1, 1, HA, DH, DH), (1, 1, HA, DH), (1, 1, HA), (1, 1, PAD, D), (1, 1, HB, HD, NST), (1, 1, PAD, CB_T * P),
         (1, NB, HA, DH, DH), (1, NB, HA, DH), (1, NB, HA), (1, NB, PAD, D), (1, NB, HB, HD, NST), (1, NB, PAD, CB_T * P)]


def kernel(**inputs):
    import numpy as _np
    import concourse.bacc as _bacc
    from concourse.bass_utils import run_bass_kernel_spmd as _run

    nc = _bacc.Bacc("TRN2", target_bir_lowering=False, num_devices=1)
    arrays, args = {}, []
    for name in _INS:
        a = _np.ascontiguousarray(inputs[name])
        arrays[f"in_{name}"] = a
        args.append(nc.dram_tensor(f"in_{name}", a.shape, mybir.dt.from_np(a.dtype), kind="ExternalInput").ap())
    for i, shape in enumerate(_OUTS):
        args.append(nc.dram_tensor(f"out_{i}", shape, F32, kind="ExternalOutput").ap())
    program(nc, *args)
    r = _run(nc, [arrays], core_ids=[0])
    return tuple(r.results[0][f"out_{i}"] for i in range(len(_OUTS)))
```

```python
from contextlib import ExitStack

import concourse.bass as bass
from concourse import mybir

F32 = mybir.dt.float32
I32 = mybir.dt.int32
ALU = mybir.AluOpType
ACT = mybir.ActivationFunctionType
AX = mybir.AxisListType.X

P = 128
D = 1024
KD = D // P
META, SEQ, NB = 16, 256, 8
NP = META + SEQ
T = NP + NB
TAPS = 4
PAD = TAPS - 1
SC0 = NP + PAD
CW = SC0 + NB * TAPS
W = CW - PAD
LAST = PAD + NB
HA, DH = 8, 128
HB, HD, NG, NST = 16, 64, 2, 128
CB_T = (D + 2 * NG * NST) // P
QT = W
S_TILES = [(0, 128), (128, 128), (256, 16)]
BLK = [0, NP, NP + NP - 128]
BLKW = BLK[2] + NP - 256
TOK = [(0, 128), (128, 128), (256, 8)]
NOUT = SEQ + NB
EG, EPG, FF = 4, 4, 1024
SLOT = 4 * 1024
BIG = 1e30
EPS = 1e-6
ATANH = [1.0 / (2 * i + 1) for i in range(1, 9)]

O_XA, O_ZA, O_I, O_F = 0, 1024, 2048, 2056
O_ZB, O_XBC, O_DT = 2064, 3088, 4624
WIN = [O_XA, O_XA + 512, O_XBC, O_XBC + 512, O_XBC + 1024, O_ZA, O_ZA + 512, O_ZB, O_ZB + 512]
U_QKV = len(WIN)
U_OUT = U_QKV + 1
N_MIX = U_OUT + 4
MR = 3
EXP_SLOT = [3, 4, 5, 2, 0, 1]
EXP_FREE = [1, 1, 1, 2, 3]

V_NMIX, V_CAW, V_CAB, V_NA, V_NB, V_NFF, V_CBB, V_CBW = 0, 8, 40, 48, 56, 64, 72, 84


class Signals:

    def __init__(self, sem):
        self.params_in = sem("params_in")
        self.prev_in = sem("prev_in")
        self.gates_in = sem("gates_in")
        self.late_in = sem("late_in")
        self.x_again = sem("x_again")
        self.nf_in = sem("nf_in")
        self.pv_ps = sem("pv_ps")
        self.ht_ps = sem("ht_ps")
        self.prev_ps = sem("prev_ps")
        self.u_ps = sem("u_ps")
        self.tm_ps = sem("tm_ps")
        self.bcm_ps = sem("bcm_ps")
        self.lct_ps = sem("lct_ps")
        self.q_ps = sem("q_ps")
        self.k_ps = sem("k_ps")
        self.kt_ps = sem("kt_ps")
        self.vt_ps = sem("vt_ps")
        self.sc_ps = sem("sc_ps")
        self.nc_ps = sem("nc_ps")
        self.n0_ps = sem("n0_ps")
        self.down_ps = sem("down_ps")
        self.cq_ps = sem("cq_ps")
        self.den_ps = sem("den_ps")
        self.n1_ps = sem("n1_ps")
        self.xs_ps = sem("xs_ps")
        self.bt_ps = sem("bt_ps")
        self.gt_ps = sem("gt_ps")
        self.bc_ps = sem("bc_ps")
        self.y_ps = sem("y_ps")
        self.sst_ps = sem("sst_ps")
        self.sq_ps = sem("sq_ps")
        self.hbc_ps = sem("hbc_ps")
        self.gbc_ps = sem("gbc_ps")
        self.wo_unit = sem("wo_unit")
        self.mo_ps = sem("mo_ps")
        self.wt_ps = sem("wt_ps")
        self.xt_ps = sem("xt_ps")
        self.lg_ps = sem("lg_ps")
        self.rank_ps = sem("rank_ps")
        self.xg_ps = sem("xg_ps")
        self.pt_ps = sem("pt_ps")
        self.gate_ps = sem("gate_ps")
        self.gu_ps = sem("gu_ps")
        self.ft_ps = sem("ft_ps")
        self.d_ps = sem("d_ps")
        self.sc_out_ps = sem("sc_out_ps")
        self.consts = sem("consts")
        self.pv_ready = sem("pv_ready")
        self.rstd_ready = sem("rstd_ready")
        self.xn_ready = sem("xn_ready")
        self.ht_ready = sem("ht_ready")
        self.prev_ready = sem("prev_ready")
        self.x_abs = sem("x_abs")
        self.x_exp = sem("x_exp")
        self.rows_pre = sem("rows_pre")
        self.rows_exp = sem("rows_exp")
        self.lc_ready = sem("lc_ready")
        self.conv_y = sem("conv_y")
        self.conv_sig = sem("conv_sig")
        self.conv_done = sem("conv_done")
        self.z_sig = sem("z_sig")
        self.tm_ready = sem("tm_ready")
        self.bcm_ready = sem("bcm_ready")
        self.lct_sb = sem("lct_sb")
        self.q_sb = sem("q_sb")
        self.k_sb = sem("k_sb")
        self.v_sb = sem("v_sb")
        self.kw_sb = sem("kw_sb")
        self.arg_done = sem("arg_done")
        self.exp_done = sem("exp_done")
        self.st_done = sem("st_done")
        self.num_sb = sem("num_sb")
        self.qs_done = sem("qs_done")
        self.nst_ready = sem("nst_ready")
        self.n1_ready = sem("n1_ready")
        self.n1_sb = sem("n1_sb")
        self.st_dec = sem("st_dec")
        self.st_new = sem("st_new")
        self.cq_sb = sem("cq_sb")
        self.xdt_ready = sem("xdt_ready")
        self.xw_ready = sem("xw_ready")
        self.bcs_ps = sem("bcs_ps")
        self.rows_out = sem("rows_out")
        self.mt_sb = sem("mt_sb")
        self.den_sb = sem("den_sb")
        self.za_done = sem("za_done")
        self.yz_ready = sem("yz_ready")
        self.bcs_ready = sem("bcs_ready")
        self.bt_ready = sem("bt_ready")
        self.gt_ready = sem("gt_ready")
        self.arg2_done = sem("arg2_done")
        self.exp2_done = sem("exp2_done")
        self.st2_done = sem("st2_done")
        self.sst_ready = sem("sst_ready")
        self.s_y = sem("s_y")
        self.sq_done = sem("sq_done")
        self.rden_ready = sem("rden_ready")
        self.sc_exp = sem("sc_exp")
        self.scale_ready = sem("scale_ready")
        self.num_ready = sem("num_ready")
        self.ysc_exp = sem("ysc_exp")
        self.yb_norm = sem("yb_norm")
        self.h_ready = sem("h_ready")
        self.h_rstd = sem("h_rstd")
        self.xn2_ready = sem("xn2_ready")
        self.xt_ready = sem("xt_ready")
        self.lx_ready = sem("lx_ready")
        self.p1_exp = sem("p1_exp")
        self.router = sem("router")
        self.rank_ready = sem("rank_ready")
        self.rounds_ready = sem("rounds_ready")
        self.p_ready = sem("p_ready")
        self.xg_ready = sem("xg_ready")
        self.pt_ready = sem("pt_ready")
        self.xs_ready = sem("xs_ready")
        self.silu_done = sem("silu_done")
        self.a_ready = sem("a_ready")
        self.ht_sb = sem("ht_sb")
        self.yg_done = sem("yg_done")
        self.h_add = sem("h_add")
        self.f_rstd = sem("f_rstd")
        self.y_ready = sem("y_ready")
        self.out_conv = sem("out_conv")
        self.out_mn = sem("out_mn")
        self.out_S = sem("out_S")
        self.out_y = sem("out_y")


def program(nc, x_prompt, x_sample, C0, n0, m0, conv_a0, S0, conv_b0, meta, norm_mix, w_in,
            conv_a_w, conv_a_b, w_q, w_k, w_v, b_i, b_f, norm_a, conv_b_w, conv_b_b, dt_bias, a_log,
            d_skip, norm_b, w_out, norm_ffn, w_r1, b_r1, w_r2, b_r2, w_gate, w_up, w_down, norm_final,
            y_p, y_s, p_C, p_n, p_m, p_ca, p_S, p_cb, s_C, s_n, s_m, s_ca, s_S, s_cb, rows_dram):
    ctx = ExitStack()
    with ctx:
        def sb(name, shape, dt=F32):
            return ctx.enter_context(nc.sbuf_tensor(name, shape, dt))

        def sem(name):
            return ctx.enter_context(nc.semaphore(name))

        def carve(t, start, *dims):
            n = 1
            for d in dims:
                n *= d
            v = t[:, start:start + n]
            if len(dims) == 2:
                v = v.rearrange("p (a b) -> p a b", b=dims[1])
            if len(dims) == 3:
                v = v.rearrange("p (a b c) -> p a b c", b=dims[1], c=dims[2])
            return v

        ring = sb("ring", [P, 6 * SLOT])
        tmp0 = 3 * SLOT
        XDT = carve(ring, tmp0, 3, D)
        XWT = carve(ring, tmp0 + 3072, 3, D)
        CPREV = carve(ring, tmp0, (KD + CB_T) * P)
        LCT = carve(ring, tmp0 + 3072, (KD + CB_T) * P)
        kw = carve(ring, tmp0 + 6144, 2, 3, P)
        vv = carve(ring, tmp0 + 6912, 2, 3, P + 1)
        SST = carve(ring, tmp0 + 6144, 2, 512)
        BCS = ring[0:NB, tmp0 + 5632:tmp0 + 6144]
        assert (KD + CB_T) * P == 5632 - 3072 and D <= 2 * 3 * (2 * P + 1)
        TMPS = carve(ring, tmp0 + 7686, D)
        BB = carve(ring, tmp0, 2, 512)
        VB = [carve(ring, tmp0 + 6144, D), TMPS]
        rows0 = tmp0 + 8710

        def rowt(i, w=T):
            return ring[:, rows0 + i * T:rows0 + i * T + w]

        XR = ring[:, rows0:rows0 + 2 * T]
        EX = ring[:, rows0 + 2 * T:rows0 + 4 * T]
        SS = ring[:, rows0 + 4 * T:rows0 + 6 * T]
        HN = ring[:, rows0 + 6 * T:rows0 + 8 * T]
        RI, AC, AR = rowt(8), rowt(9), rowt(10)
        MX = rowt(11)
        WSR, EDR = rowt(2), rowt(3)
        BN, MROW = rowt(4), rowt(5)
        DEN, SCL, YSC = rowt(6), rowt(7), rowt(8)[32:32 + NG]
        assert rows0 + 12 * T <= 6 * SLOT

        h_tok = sb("h_tok", [P, 3, D])
        stage = h_tok
        xn = sb("xn", [P, 3, D])
        xnf = xn[:, :, :].rearrange("p a b -> p (a b)")
        qT = carve(xnf, 0, 2, QT)
        kT = carve(xnf, 2 * QT, 2, QT)
        GT = carve(xnf, 4 * QT, 2, BLKW)
        BT = carve(xnf, 4 * QT + 2 * BLKW, 3, NG * NST)
        SDEN = 4 * QT + 2 * BLKW + 3 * NG * NST
        assert SDEN <= 3 * D

        arena = sb("arena", [P, 15304])
        CA = carve(arena, 0, KD, CW)
        CBX = carve(arena, 2456, CB_T, CW)
        ZA = carve(arena, 6140, KD, T)
        ZB = carve(arena, 8380, KD, T)
        hT = carve(arena, 10620, KD, T)
        NUM = hT
        SQA = carve(arena, 0, KD, T)
        MT = carve(arena, 2456, KD, NOUT)
        XC = carve(arena, 12860, KD, W)
        YB = carve(arena, 12860, KD, T)
        XG = carve(arena, 0, KD, EG * P)
        YG = carve(arena, 4096, EG, D)
        XT = carve(arena, 4096, KD, NOUT)
        PT = carve(arena, 8192, EG, NOUT)
        PG = carve(arena, 9248, 3, EG * P)
        XS = carve(arena, 10784, KD, P)
        SG = carve(arena, 11808, D)
        AH = carve(arena, 12832, D)
        HT = carve(arena, 13856, KD, P)

        shared = sb("shared", [P, 1216])
        CY = carve(shared, 0, 2, W)
        CSG = carve(shared, 2 * W, 2, W)
        ARG = carve(shared, 0, 2, BLKW)
        NF = carve(shared, 0, D)

        ident = sb("ident", [P, P])
        mask = sb("mask", [P, NP])
        before = sb("before", [P, P])
        ones = sb("ones", [P, P])
        iota_i = sb("iota_i", [P, P], I32)
        iota = sb("iota", [P, P])
        strip = sb("strip", [P, 15])
        PR = sb("PR", [84, 2, P])
        PV = sb("PV", [P, 132])
        c16 = sb("c16", [HB, 8])
        WG = sb("WG", [P, KD, 80])
        LC = sb("LC", [P, KD + CB_T, LAST])
        TM = sb("TM", [P, 3, 64])
        VS = sb("VS", [NB, D])
        RS = sb("RS", [HA, 16])
        RX = sb("RX", [HB, 17])
        BCM = sb("BCM", [P, HA, 16])
        XE = sb("XE", [P, KD, 17])
        m0s = sb("m0s", [HA, NB])
        N0 = sb("N0", [64, P])
        N1 = sb("N1", [P, 64])
        NT = sb("NT", [P, 64])
        QN = sb("QN", [P, 64])
        N1T = sb("N1T", [64, P])
        QS = sb("QS", [P, HA, NB])
        KS = sb("KS", [P, HA, NB])
        XDS = sb("XDS", [P, KD, NB])
        YS = sb("YS", [P, KD, NB])
        CST = sb("CST", [P, 2, P + 1])
        NSTt = sb("NSTt", [P, HA])
        NSTo = sb("NSTo", [HA, P])
        ENM = sb("ENM", [HB, T])
        YS2 = sb("YS2", [P, KD, NB])
        st3 = sb("st3", [P, 8])
        wr = sb("wr", [P, KD, 20])
        br = sb("br", [1, 20])
        epst = sb("epst", [P, 2])

        bank = [ctx.enter_context(nc.psum_tensor(f"bank{i}", [P, 512], F32)) for i in range(8)]

        L = sb("L", [P, 3, 20])
        LX = sb("LX", [P, 3, 4])
        M1 = sb("M1", [P, 3, 4])
        K1 = sb("K1", [P, 3, 4])
        L2 = sb("L2", [P, 3, 4])
        O1 = sb("O1", [P, 3, 4])
        O2 = sb("O2", [P, 3, 4])
        LP = sb("LP", [P, 3, 4, 4])
        r1 = sb("r1", [P, 3, 8])
        GATE = sb("GATE", [P, 3, 4])
        rank = sb("rank", [P, 3, 4])
        order = sb("order", [P, 4])
        GS = sb("GS", [P, EG * EPG])
        cnt = sb("cnt", [P, 8])
        rounds = sb("rounds", [P, 1], I32)

        s = Signals(sem)
        x_in = [sem(f"x_in{i}") for i in range(3)]
        u_free = [sem(f"u_free{b}") for b in range(4)]
        y_free = [sem(f"y_free{b}") for b in range(2)]
        arrived = [sem(f"arrived{i}") for i in range(6)]
        st_in = [sem(f"st_in{i}") for i in range(3)]
        bb_in = [sem(f"bb_in{i}") for i in range(2)]
        vb_in = [sem(f"vb_in{i}") for i in range(2)]
        st_out = [sem(f"st_out{i}") for i in range(3)]
        cst_out = [sem(f"cst_out{i}") for i in range(2)]
        dch, ach, gch = sem("dve_chain"), sem("act_chain"), sem("pool_chain")

        slot = [ring[:, i * SLOT:(i + 1) * SLOT] for i in range(6)]

        def slot_k(i, n):
            return slot[i].rearrange("p (k n) -> p k n", n=n)

        def unit_at(u):
            return u % MR, 16 * (u // MR + 1) + (32 if u % MR == U_QKV % MR and u >= U_QKV else 0)

        mix_in = [0] * 6
        for u in range(N_MIX):
            mix_in[u % MR] += 48 if u == U_QKV else 16

        UT = [("xa", c, c // 4, (c % 4) * P) for c in range(KD)]
        UT += [("xbc", c, 2 + c // 4, (c % 4) * P) for c in range(CB_T)]
        UT += [("za", c, 5 + c // 4, (c % 4) * P) for c in range(KD)]
        UT += [("zb", c, 7 + c // 4, (c % 4) * P) for c in range(KD)]
        NCONV = KD + CB_T

        def col(t, n):
            return t[:, n:n + 1].to_broadcast([t.shape[0], P])

        def bc_last(v, n):
            return v.unsqueeze(len(v.shape)).to_broadcast(list(v.shape) + [n])

        def smp(v):
            return v[:, SC0:SC0 + TAPS * (NB - 1) + 1:TAPS]

        def rounds_of(eng):
            eng.wait_ge(s.rounds_ready, 1)
            return eng.value_load(rounds[0:1, 0:1], min_val=1, max_val=3)

        def head_state_out(pool, h):
            pool.wait_ge(s.num_sb, h + 1)
            pool.dma_start(p_C[0, 0, h], CST[:, h % 2, 0:P]).then_inc(cst_out[h % 2], 16)
            nc.gpsimd.tensor_copy(NSTt[:, h:h + 1], CST[:, h % 2, P:P + 1]).then_inc(s.nst_ready, 1)

        def state_buf(n):
            return stage[:, n % 3, :].rearrange("p (a b) -> p a b", b=P)

        def state_dram(n, old):
            if n >= NB:
                t = C0 if old else s_C
                return t[0, n - NB].rearrange("h d e -> d h e")
            t = S0 if old else s_S
            return t[0, n].rearrange("h q n -> (h q) n").rearrange("(c p) n -> p c n", p=P)

        def state_free(pool, n):
            pool.wait_ge(st_out[n % 3], 16 * (n // 3 + 1))
            if n < NB:
                pool.wait_ge(s.s_y, n + 1)
            else:
                pool.wait_ge(s.cq_ps, n - NB + 1)

        def turn_hidden(act, x2, j):
            act.wait_ge(s.ft_ps, x2 + (j + 1))
            nc.scalar.activation(HT[:, 4 * j:4 * j + 4, :], bank[4 + j][:, :].rearrange("p (k n) -> p k n", n=P),
                                 ACT.Copy).then_inc(s.ht_sb, 1)

        def ssd_out(dve, c):
            dve.wait_ge(s.y_ps, 2 * c + 2)
            nc.vector.scalar_tensor_tensor(out=YB[:, c, 0:NP], in0=CBX[:, c, 0:NP], scalar=XE[:, c, 16:17],
                                           in1=bank[6 if c % 2 == 0 else 0][:, 0:NP], op0=ALU.mult, op1=ALU.add)\
                .then_inc(y_free[c % 2], 1)

        ctx.enter_context(nc.allow_non_contiguous_dma(reason="small [sample, head] tables, transposed"))
        block = ctx.enter_context(nc.Block())

        @block.sync
        def _(sp):
            def mixer_unit(u):
                if u >= MR:
                    before_u = u - MR
                    if before_u < U_QKV:
                        sp.wait_ge(s.u_ps, 3 + 4 * (before_u + 1))
                    elif before_u == U_QKV:
                        sp.wait_ge(s.vt_ps, HA)
                    else:
                        sp.wait_ge(s.wo_unit, before_u - U_QKV)
                i = u % MR
                if u < U_QKV:
                    src = w_in[0, :, WIN[u]:WIN[u] + 512].rearrange("(k p) n -> p k n", p=P)
                    sp.dma_start(slot_k(i, 512), src).then_inc(arrived[i], 16)
                elif u == U_QKV:
                    for j, wt in enumerate((w_q, w_k, w_v)):
                        dst = slot[i][:, j * D:(j + 1) * D].rearrange("p (h e) -> p h e", e=DH)
                        sp.dma_start(dst, wt[0].rearrange("h d e -> d h e")).then_inc(arrived[i], 16)
                else:
                    r0 = 512 * (u - U_OUT)
                    src = w_out[0, r0:r0 + 512, :].rearrange("(k p) n -> p k n", p=P)
                    sp.dma_start(slot_k(i, D), src).then_inc(arrived[i], 16)

            sp.dma_start(h_tok[0:P, 0, :], x_prompt[0, 0:P, :]).then_inc(x_in[0], 16)
            sp.dma_start(h_tok[0:P, 1, :], x_prompt[0, P:SEQ, :]).then_inc(x_in[1], 16)
            sp.dma_start(h_tok[0:NB, 2, :], x_sample[:, 0, :]).then_inc(x_in[2], 16)
            sp.dma_start(h_tok[NB:NB + META, 2, :], meta).then_inc(x_in[2], 16)
            for c0, o, n in ((0, O_I, HA), (32, O_F, HA), (64, O_DT, HB)):
                sp.dma_start(WG[:, :, c0:c0 + n], w_in[0, :, o:o + n].rearrange("(k p) n -> p k n", p=P)).then_inc(s.gates_in, 16)
            mixer_unit(0)
            sp.wait_ge(s.params_in, 16 * 13)
            for u in range(1, MR):
                mixer_unit(u)
            sp.wait_ge(s.xn_ready, 3)
            for n in range(3):
                sp.dma_start(state_buf(n), state_dram(n, True)).then_inc(st_in[n % 3], 16)
            for u in range(MR, U_OUT + 2):
                mixer_unit(u)

            def state_step(n):
                if n >= 1:
                    sp.wait_ge(s.st_new, n)
                    sp.dma_start(state_dram(n - 1, False), state_buf(n - 1)).then_inc(st_out[(n - 1) % 3], 16)
                if n >= 2 and n + 1 < 2 * NB:
                    state_free(sp, n - 2)
                    sp.dma_start(state_buf(n + 1), state_dram(n + 1, True)).then_inc(st_in[(n + 1) % 3], 16)

            sp.wait_ge(s.bcs_ready, 1)
            sp.dma_start(rows_dram[:, 0:512], BCS).then_inc(s.rows_out, 16)
            for b in range(NB):
                if b == 0:
                    sp.wait_ge(s.rows_out, 16)
                if b >= 2:
                    sp.wait_ge(s.s_y, b - 1)
                sp.dma_start(BB[:, b % 2, :], rows_dram[b:b + 1, 0:512].to_broadcast([P, 512])).then_inc(bb_in[b % 2], 16)
                state_step(b)
            mixer_unit(U_OUT + 2)
            sp.wait_ge(s.v_sb, HA)
            sp.dma_start(rows_dram[:, 512:512 + D], VS[:, :]).then_inc(s.rows_out, 16)
            for b in range(NB):
                if b == 0:
                    sp.wait_ge(s.rows_out, 32)
                    sp.wait_ge(s.nc_ps, HA)
                    sp.wait_ge(s.n1_ready, 1)
                if b >= 2:
                    sp.wait_ge(s.st_new, NB + b - 1)
                sp.dma_start(VB[b % 2], rows_dram[b:b + 1, 512:512 + D].to_broadcast([P, D])).then_inc(vb_in[b % 2], 16)
                state_step(NB + b)
            state_step(2 * NB)
            mixer_unit(U_OUT + 3)

            gate_v = w_gate[0].rearrange("e (k p) n -> e p k n", p=P)
            up_v = w_up[0].rearrange("e (k p) n -> e p k n", p=P)
            down_v = w_down[0].rearrange("e (k p) n -> e p k n", p=P)

            def expert_units(e, free):
                for c in range(6):
                    sp.wait_ge(*free[c])
                    i = EXP_SLOT[c]
                    if c < 4:
                        v = gate_v if c % 2 == 0 else up_v
                        src = v[bass.ds(e, 1), :, :, (c // 2) * 512:(c // 2 + 1) * 512]
                        dst = slot_k(i, 512)
                    else:
                        src = down_v[bass.ds(e, 1), :, (c - 4) * 4:(c - 3) * 4, :]
                        dst = slot_k(i, D)
                    src = src.rearrange("o p k n -> (o p) k n")
                    sp.dma_start(dst, src).then_inc(arrived[i], 16)

            def read_by(x):
                return [(s.gate_ps, x * 2 - 1), (s.gu_ps, x * 2), (s.gate_ps, x * 2), (s.gu_ps, x * 2 + 1),
                        (s.down_ps, x), (s.d_ps, x)]

            sp.wait_ge(s.out_S, 16 * 2)
            expert_units(0, [(s.wo_unit, n) for n in EXP_FREE] + [(s.mo_ps, KD)])
            with sp.Fori(1, EG * EPG) as e:
                expert_units(e, read_by(e))
            again = rounds_of(sp)
            with sp.If(again > 1):
                with sp.Fori(1, again) as r:
                    with sp.Fori(0, EG * EPG) as e:
                        expert_units(e, read_by(r * (EG * EPG) + e))
            sp.wait_ge(s.out_y, 16 * 3)
            sp.wait_ge(s.out_conv, 16 * 6)
            sp.wait_ge(s.out_mn, 16 * 4)
            sp.wait_ge(s.out_S, 16 * 2)
            for i in range(2):
                sp.wait_ge(cst_out[i], 16 * 4)
            for i in range(3):
                sp.wait_ge(st_out[i], 16 * len(range(i, 2 * NB, 3)))

        @block.gpsimd
        def _(pool):
            g = nc.gpsimd
            links = [0]

            def link(ins):
                links[0] += 1
                ins.then_inc(gch, 1)
                pool.wait_ge(gch, links[0])

            g.memset(ones[:], 1.0)
            g.memset(ident[:], 0.0)
            g.memset(mask[:], 0.0)
            g.memset(strip[:], 0.0)
            g.memset(epst[:, 0:1], EPS)
            g.memset(st3[:], 0.0)
            g.memset(WG[:, :, HA:32], 0.0)
            g.memset(WG[:, :, 32 + HA:64], 0.0)
            g.iota(iota_i[:], pattern=[[1, P]], base=0, channel_multiplier=0)
            link(g.memset(epst[:, 1:2], 1.0))
            g.memset(strip[:, 7:8], 1.0)
            g.affine_select(out=ident[:], in_=ident[:], compare_op=ALU.not_equal, fill=1.0, base=0,
                            pattern=[[-1, P]], channel_multiplier=1)
            g.affine_select(out=mask[:], in_=mask[:], compare_op=ALU.is_ge, fill=BIG, base=0,
                            pattern=[[1, NP]], channel_multiplier=-1)
            g.affine_select(out=before[:], in_=ones[:], compare_op=ALU.is_gt, fill=0.0, base=0,
                            pattern=[[1, P]], channel_multiplier=-1)
            g.tensor_copy(iota[:], iota_i[:])
            for j in range(4):
                g.memset(order[:, j:j + 1], 4.0 - j)
            g.memset(CA[:, :, 0:PAD], 0.0)
            g.memset(CBX[:, :, 0:PAD], 0.0)
            g.memset(vv[:, :, :, P:P + 1].rearrange("p a b c -> p (a b) c"), 1.0)
            g.memset(XR[0:HB, T:2 * T], 0.0)
            g.memset(ENM[0:HB, :], 1.0)
            g.memset(L[:], 0.0).then_inc(s.consts, 1)

            pool.dma_start(s_ca[0, :, 0:2, :], conv_a0[0, :, 1:3, :]).then_inc(s.out_conv, 16)
            pool.dma_start(s_cb[0, :, 0:2, :], conv_b0[0, :, 1:3, :]).then_inc(s.out_conv, 16)
            pool.wait_ge(s.rows_pre, 1)
            pool.dma_start(p_m[0, 0, :].unsqueeze(1), MROW[0:HA, NP - 1:NP]).then_inc(s.out_mn, 16)
            pool.dma_start(s_m[0].rearrange("b h -> h b"), MROW[0:HA, NP:T]).then_inc(s.out_mn, 16)
            pool.wait_ge(s.lct_sb, 5)
            pool.dma_start(p_ca[0, 0], LCT[0:PAD, 0:D]).then_inc(s.out_conv, 16)
            pool.dma_start(p_cb[0, 0], LCT[0:PAD, D:]).then_inc(s.out_conv, 16)
            pool.dma_start(s_ca[0, :, 2, :], LCT[PAD:LAST, 0:D]).then_inc(s.out_conv, 16)
            pool.dma_start(s_cb[0, :, 2, :], LCT[PAD:LAST, D:]).then_inc(s.out_conv, 16)

            def decay_state(n):
                pool.wait_ge(st_in[n % 3], 16 * (n // 3 + 1))
                if n == 0:
                    pool.wait_ge(s.bcm_ready, 1)
                w = XE[:, :, n] if n < NB else BCM[:, :, n - NB]
                g.tensor_tensor(state_buf(n), state_buf(n), bc_last(w, P), ALU.mult).then_inc(s.st_dec, 1)

            for h in range(HA):
                decay_state(h)
                pool.wait_ge(s.q_sb, h + 1)
                pool.wait_ge(s.k_sb, h + 1)
                g.tensor_copy(QS[:, h, :], smp(qT[:, h % 2, :]))
                g.tensor_copy(KS[:, h, :], smp(kT[:, h % 2, :])).then_inc(s.qs_done, 1)
                if h > 0:
                    head_state_out(pool, h - 1)
            head_state_out(pool, HA - 1)
            decay_state(NB)
            pool.wait_ge(s.n1_sb, 1)
            pool.dma_start(p_n[0, 0], NSTo[:, :]).then_inc(s.out_mn, 16)
            pool.dma_start(s_n[0].rearrange("b h d -> (b h) d"), N1T[:, :]).then_inc(s.out_mn, 16)
            pool.wait_ge(s.out_conv, 16 * 6)
            for i, (_t0, m) in enumerate(S_TILES):
                pool.wait_ge(s.xdt_ready, 2 * (i + 1))
                g.tensor_tensor(XWT[0:m, i, :].rearrange("p (h q) -> p h q", q=HD),
                                XDT[0:m, i, :].rearrange("p (h q) -> p h q", q=HD),
                                bc_last(TM[0:m, i, 48:64], HD), ALU.mult).then_inc(s.xw_ready, 1)
            for n in range(NB + 1, 2 * NB):
                decay_state(n)
                h = n - NB - 1
                pool.wait_ge(s.sq_done, h + 1)
                g.tensor_tensor(NUM[:, h, 0:NP], NUM[:, h, 0:NP], ZA[:, h, 0:NP], ALU.mult).then_inc(s.za_done, 1)
            pool.wait_ge(s.sq_done, HA)
            g.tensor_tensor(NUM[:, HA - 1, 0:NP], NUM[:, HA - 1, 0:NP], ZA[:, HA - 1, 0:NP], ALU.mult).then_inc(s.za_done, 1)
            for half in range(2):
                pool.wait_ge(s.sst_ready, half + 1)
                dst = p_S[0, 0].rearrange("h q n -> (h q) n").rearrange("(c p) n -> p c n", p=P)
                pool.dma_start(dst[:, 4 * half:4 * half + 4, :],
                               SST[:, half, :].rearrange("p (c n) -> p c n", n=NST)).then_inc(s.out_S, 16)
            for n in range(2 * NB - 3, 2 * NB):
                state_free(pool, n)
            for i, (t0, m) in enumerate(TOK):
                src = x_prompt[0, t0:t0 + m, :] if i < 2 else x_sample[:, 0, :]
                pool.dma_start(h_tok[0:m, i, :], src).then_inc(s.x_again, 16)
            pool.wait_ge(s.h_ready, 1)
            pool.dma_start(NF, norm_final.rearrange("(o n) -> o n", o=1).to_broadcast([P, D]))\
                .then_inc(s.nf_in, 16)

        @block.scalar
        def _(act):
            a = nc.scalar
            links = [0]

            def link(ins):
                links[0] += 1
                ins.then_inc(ach, 1)
                act.wait_ge(ach, links[0])

            def root_of_mean(done):
                link(a.activation(st3[:, 4:7], st3[:, 0:3], ACT.Ln, bias=epst[:, 0:1], scale=1.0 / D))
                a.activation(st3[:, 4:7], st3[:, 4:7], ACT.Exp, scale=-0.5).then_inc(done, 1)

            rows8 = "(k p) -> k p"
            act.dma_start(PR[V_NMIX:V_NMIX + 8, 0, :], norm_mix[0].rearrange(rows8, p=P)).then_inc(s.params_in, 16)
            act.dma_start(PR[V_CAW:V_CAW + 32, 0, :], conv_a_w[0].rearrange("j (k p) -> (j k) p", p=P)).then_inc(s.params_in, 16)
            act.dma_start(PR[V_CAB:V_CAB + 8, 0, :], conv_a_b[0].rearrange(rows8, p=P)).then_inc(s.params_in, 16)
            act.dma_start(PR[V_NA:V_NA + 8, 0, :], norm_a[0]).then_inc(s.params_in, 16)
            act.dma_start(PR[V_NB:V_NB + 8, 0, :], norm_b[0].rearrange(rows8, p=P)).then_inc(s.params_in, 16)
            act.dma_start(PR[V_NFF:V_NFF + 8, 0, :], norm_ffn[0].rearrange(rows8, p=P)).then_inc(s.params_in, 16)
            act.dma_start(PR[V_CBB:V_CBB + CB_T, 0, :], conv_b_b[0].rearrange(rows8, p=P)).then_inc(s.params_in, 16)
            act.dma_start(PR[0:4 * CB_T, 1, :], conv_b_w[0].rearrange("j (k p) -> (j k) p", p=P)).then_inc(s.params_in, 16)
            for j, (v, n) in enumerate(((b_i, HA), (b_f, HA), (dt_bias, HB), (a_log, HB), (d_skip, HB))):
                act.dma_start(c16[0:n, j:j + 1], v[0].unsqueeze(1)).then_inc(s.params_in, 16)
            act.dma_start(CPREV[0:PAD * NB, 0:D], conv_a0[0].rearrange("b j c -> (b j) c")).then_inc(s.prev_in, 16)
            act.dma_start(CPREV[0:PAD * NB, D:], conv_b0[0].rearrange("b j c -> (b j) c")).then_inc(s.prev_in, 16)
            act.dma_start(m0s[:, :], m0[0].rearrange("b h -> h b")).then_inc(s.late_in, 16)
            act.dma_start(N0[:, :], n0[0].rearrange("b h d -> (b h) d")).then_inc(s.late_in, 16)
            act.dma_start(wr[:, :, 0:4], w_r1[0].rearrange("(k p) g -> p k g", p=P)).then_inc(s.late_in, 16)
            act.dma_start(wr[:, :, 4:20], w_r2[0].rearrange("(k p) g e -> p k (g e)", p=P)).then_inc(s.late_in, 16)
            act.dma_start(br[:, 0:4], b_r1).then_inc(s.late_in, 16)
            act.dma_start(br[:, 4:20], b_r2.rearrange("o g e -> o (g e)")).then_inc(s.late_in, 16)

            act.wait_ge(s.consts, 1)
            for i, m in enumerate((P, P, NB + META)):
                act.wait_ge(x_in[i], 16 if i < 2 else 32)
                link(a.activation(xn[0:m, i, :], h_tok[0:m, i, :], ACT.Square, accum_out=st3[0:m, i:i + 1]))
            root_of_mean(s.rstd_ready)

            act.wait_ge(s.x_abs, 1)
            a.activation(EX[0:HB, :], HN[0:HB, :], ACT.Exp, scale=-1.0).then_inc(s.x_exp, 1)
            a.activation(c16[:, 5:6], c16[:, 3:4], ACT.Exp).then_inc(s.x_exp, 1)
            act.wait_ge(s.rows_pre, 1)
            a.activation(WSR[0:HA, 0:NP], AC[0:HA, 0:NP], ACT.Exp, bias=c16[0:HA, 6:7])
            a.activation(WSR[0:HA, NP:T], WSR[0:HA, NP:T], ACT.Exp)
            a.activation(EDR[0:HB, 0:NP], AR[0:HB, 0:NP], ACT.Exp, bias=c16[:, 7:8])
            a.activation(RX[:, 0:NB], AR[0:HB, NP:T], ACT.Exp, scale=-1.0)
            a.activation(RS[:, :], RS[:, :], ACT.Exp)
            a.activation(ENM[0:HA, :], MROW[0:HA, :], ACT.Exp, scale=-1.0).then_inc(s.rows_exp, 1)

            def sigmoid_of_conv(n):
                act.wait_ge(s.conv_y, n + 1)
                if n >= 2:
                    act.wait_ge(s.conv_done, n - 1)
                a.activation(CSG[:, n % 2, :], CY[:, n % 2, :], ACT.Sigmoid).then_inc(s.conv_sig, 1)

            for n, (kind, c, _u, _o) in enumerate(UT):
                b = bank[(n + 3) % 4]
                act.wait_ge(s.u_ps, n + 4)
                if kind in ("xa", "xbc"):
                    dst = CA if kind == "xa" else CBX
                    a.activation(dst[:, c, PAD:PAD + NP], b[:, 0:NP], ACT.Copy)
                    a.activation(dst[:, c, SC0 + PAD:SC0 + PAD + TAPS * (NB - 1) + 1:TAPS], b[:, NP:T],
                                 ACT.Copy).then_inc(s.lc_ready, 1)
                    a.activation(LC[:, n, :], b[:, NP - PAD:T], ACT.Copy).then_inc(u_free[(n + 3) % 4], 1)
                    if n >= 1:
                        sigmoid_of_conv(n - 1)
                else:
                    if n == NCONV:
                        sigmoid_of_conv(NCONV - 1)
                    if kind == "za":
                        a.activation(ZA[:, c, :], b[:, 0:T], ACT.Sigmoid).then_inc(u_free[(n + 3) % 4], 1)
                    else:
                        a.activation(ZB[:, c, :], b[:, 0:T], ACT.Sigmoid).then_inc(s.z_sig, 1)
            for q in range(5):
                act.wait_ge(s.lct_ps, q + 1)
                a.activation(LCT[0:LAST, q * 512:(q + 1) * 512], bank[6 + q % 2][0:LAST, :], ACT.Copy).then_inc(s.lct_sb, 1)

            act.wait_ge(s.bcs_ps, 1)
            a.activation(BCS, bank[7][0:NB, :], ACT.Copy).then_inc(s.bcs_ready, 1)

            act.wait_ge(s.tm_ready, 1)
            act.wait_ge(s.conv_done, NCONV)
            def head_in(h):
                if h >= 2:
                    act.wait_ge(s.nc_ps, h - 1)
                    act.wait_ge(s.qs_done, h - 1)
                act.wait_ge(s.q_ps, h + 1)
                a.activation(qT[:, h % 2, :], bank[0][:, 0:W], ACT.Copy).then_inc(s.q_sb, 1)
                act.wait_ge(s.k_ps, h + 1)
                a.activation(kT[:, h % 2, :], bank[1][:, 0:W], ACT.Copy, scale=DH ** -0.5).then_inc(s.k_sb, 1)
                act.wait_ge(s.vt_ps, h + 1)
                a.activation(vv[:, h % 2, 0:2, 0:P], bank[3][:, 0:256].rearrange("p (a b) -> p a b", b=P), ACT.Copy)
                a.activation(vv[0:16, h % 2, 2, 0:P], bank[3][0:16, 256:384], ACT.Copy)
                a.activation(VS[:, h * P:(h + 1) * P], bank[3][0:NB, 384:512], ACT.Copy).then_inc(s.v_sb, 1)

            def head_exp(h):
                act.wait_ge(s.arg_done, h + 1)
                a.activation(ARG[:, h % 2, :], ARG[:, h % 2, :], ACT.Exp, scale=-1.0).then_inc(s.exp_done, 1)

            def head_out(h):
                act.wait_ge(s.nc_ps, h + 1)
                if h >= 2:
                    act.wait_ge(cst_out[h % 2], 16 * (h // 2))
                    act.wait_ge(s.nst_ready, h - 1)
                a.activation(NUM[:, h, 0:NP], bank[6][:, 0:NP], ACT.Copy)
                a.activation(CST[:, h % 2, :], bank[6][:, NP:NP + P + 1], ACT.Copy).then_inc(s.num_sb, 1)

            head_in(0)
            for h in range(HA):
                head_exp(h)
                if h + 1 < HA:
                    head_in(h + 1)
                head_out(h)

            for h in range(HA):
                act.wait_ge(s.num_sb, h + 1)
                a.activation(SQA[:, h, 0:NP], NUM[:, h, 0:NP], ACT.Square).then_inc(s.sq_done, 1)

            act.wait_ge(s.bt_ps, 1)
            a.activation(BT[:, 0:2, :], bank[0][:, :].rearrange("p (a b) -> p a b", b=256), ACT.Copy)
            a.activation(BT[0:16, 2, :], bank[1][0:16, 0:256], ACT.Copy).then_inc(s.bt_ready, 1)
            for j in range(NG):
                act.wait_ge(s.gt_ps, j + 1)
                a.activation(GT[:, j, 0:BLK[2]], bank[3 + j][:, 0:BLK[2]], ACT.Copy)
                a.activation(GT[0:16, j, BLK[2]:BLKW], bank[3 + j][0:16, BLK[2]:BLKW], ACT.Copy).then_inc(s.gt_ready, 1)
            def y_square(c):
                act.wait_ge(s.yz_ready, c + 1)
                act.wait_ge(s.sq_ps, c + 1)
                a.activation(SQA[:, c, :], YB[:, c, :], ACT.Square).then_inc(s.sq_done, 1)

            for h in range(HB):
                act.wait_ge(s.arg2_done, h + 1)
                a.activation(ARG[:, h % 2, :], ARG[:, h % 2, :], ACT.Exp, scale=-1.0).then_inc(s.exp2_done, 1)
                if h % 2 == 1 and h >= 3:
                    y_square((h - 3) // 2)
            y_square(KD - 1)
            act.wait_ge(s.cq_ps, NB)
            a.activation(NUM[:, :, NP:T], bank[3][:, 0:64].rearrange("p (b h) -> p h b", h=HA), ACT.Copy)
            a.activation(QN[:], bank[3][:, 0:64], ACT.Square).then_inc(s.cq_sb, 1)
            for half in range(2):
                act.wait_ge(s.sst_ps, half + 1)
                a.activation(SST[:, half, :], bank[1 + half][:, :], ACT.Copy).then_inc(s.sst_ready, 1)

            act.wait_ge(s.sq_ps, HA + KD)
            a.activation(YSC, bank[7][32:32 + NG, 0:T], ACT.Ln, bias=epst[32:32 + NG, 0:1], scale=1.0 / (D // NG))
            act.wait_ge(s.rden_ready, 1)
            link(a.activation(SCL[0:HA, :], SCL[0:HA, :], ACT.Ln, bias=epst[0:HA, 0:1], scale=1.0 / DH))
            a.activation(SCL[0:HA, :], SCL[0:HA, :], ACT.Exp, scale=-0.5).then_inc(s.sc_exp, 1)
            a.activation(YSC, YSC, ACT.Exp, scale=-0.5).then_inc(s.ysc_exp, 1)

            for c in range(KD):
                act.wait_ge(s.mo_ps, c + 1)
                a.activation(MT[:, c, :], bank[c][:, 0:NOUT], ACT.Copy).then_inc(s.mt_sb, 1)

            for i, (_t0, m) in enumerate(TOK):
                act.wait_ge(s.h_ready, i + 1)
                link(a.activation(xn[0:m, i, :], h_tok[0:m, i, :], ACT.Square, accum_out=st3[0:m, i:i + 1]))
            root_of_mean(s.h_rstd)
            act.wait_ge(s.lx_ready, 1)
            a.activation(LX[:], LX[:], ACT.Exp).then_inc(s.p1_exp, 1)
            act.wait_ge(s.lx_ready, 2)
            a.activation(r1[:, :, 3:4], r1[:, :, 3:4], ACT.Exp).then_inc(s.p1_exp, 1)

            nr = rounds_of(act)
            with act.Fori(0, nr) as r:
                for k in range(1, KD, 2):
                    act.wait_ge(s.xg_ps, r * KD + (k + 1))
                    a.activation(XG[:, k, :], bank[k][:, :], ACT.Copy, scale=PV[:, V_NFF + k:V_NFF + k + 1])\
                        .then_inc(s.xg_ready, 1)
                with act.Fori(0, EG) as q:
                    act.wait_ge(s.gu_ps, (r * EG + q) * (2 * EPG) + 1)
                    act.wait_ge(s.xg_ready, r * KD + KD)
                    a.activation(XS[:], XG[:, :, bass.ds(q * P, P)], ACT.Copy).then_inc(s.xs_ready, 1)
                    with act.Fori(0, EPG) as e:
                        x2 = ((r * EG + q) * EPG + e) * 2
                        for j in range(2):
                            act.wait_ge(s.gate_ps, x2 + (j + 1))
                            a.activation(SG[:, j * 512:(j + 1) * 512], bank[2 * j][:, :], ACT.Silu)\
                                .then_inc(s.silu_done, 1)
                            if j == 1:
                                turn_hidden(act, x2, 0)
                        turn_hidden(act, x2, 1)

            for i, (_t0, m) in enumerate(TOK):
                act.wait_ge(s.h_add, nr * 6)
                link(a.activation(xn[0:m, i, :], h_tok[0:m, i, :], ACT.Square, accum_out=st3[0:m, i:i + 1]))
            root_of_mean(s.f_rstd)
            for i, (t0, m) in enumerate(TOK):
                act.wait_ge(s.y_ready, i + 1)
                dst = y_p[0, t0:t0 + m, :] if i < 2 else y_s[:, 0, :]
                act.dma_start(dst, h_tok[0:m, i, :]).then_inc(s.out_y, 16)

        @block.vector
        def _(dve):
            v = nc.vector
            links = [0]

            def link(ins):
                links[0] += 1
                ins.then_inc(dch, 1)
                dve.wait_ge(dch, links[0])

            dve.wait_ge(s.pv_ps, 1)
            v.tensor_copy(PV[:], bank[7][:, 0:132]).then_inc(s.pv_ready, 1)
            dve.wait_ge(s.pv_ready, 1)
            for i, m in enumerate((P, P, NB + META)):
                dve.wait_ge(s.rstd_ready, 1)
                v.tensor_scalar(xn[0:m, i, :], h_tok[0:m, i, :], st3[0:m, 4 + i:5 + i], None, ALU.mult).then_inc(s.xn_ready, 1)
            for i, m in enumerate((P, P, NB + META)):
                for half in range(2):
                    q = 2 * i + half
                    dve.wait_ge(s.ht_ps, q + 1)
                    src = bank[q][:, :].rearrange("p (k n) -> p k n", n=P)
                    gain = PV[:, V_NMIX + 4 * half:V_NMIX + 4 * half + 4]
                    ks = slice(4 * half, 4 * half + 4)
                    if i < 2:
                        v.tensor_tensor(hT[:, ks, META + i * P:META + (i + 1) * P], src, bc_last(gain, P), ALU.mult)\
                            .then_inc(s.ht_ready, 1)
                    else:
                        v.tensor_tensor(hT[:, ks, NP:T], src[:, :, 0:NB], bc_last(gain, NB), ALU.mult)
                        v.tensor_tensor(hT[:, ks, 0:META], src[:, :, NB:NB + META], bc_last(gain, META), ALU.mult)\
                            .then_inc(s.ht_ready, 1)
            dve.wait_ge(s.prev_ps, 2)
            for dst, b, n in ((CA, bank[6], KD), (CBX, bank[7], CB_T)):
                for bb in range(NB):
                    last = v.tensor_copy(dst[:, :, SC0 + TAPS * bb:SC0 + TAPS * bb + PAD],
                                         b[:, 0:n * 24].rearrange("p (c q) -> p c q", q=24)[:, :, 3 * bb:3 * bb + 3])
                last.then_inc(s.prev_ready, 1)

            dve.wait_ge(s.params_in, 16 * 13)
            dve.wait_ge(s.u_ps, 3)
            v.tensor_scalar(RI[0:HA, :], bank[0][0:HA, 0:T], c16[0:HA, 0:1], None, ALU.add).then_inc(u_free[1], 1)
            v.tensor_scalar(XR[0:HA, T:2 * T], bank[0][32:32 + HA, 0:T], c16[0:HA, 1:2], -1.0, ALU.add, ALU.mult).then_inc(u_free[2], 1)
            v.tensor_scalar(XR[0:HB, 0:T], bank[0][64:64 + HB, 0:T], c16[:, 2:3], None, ALU.add).then_inc(u_free[0], 1)
            dve.wait_ge(u_free[0], 1)
            v.scalar_tensor_tensor(out=HN[0:HB, :], in0=XR[0:HB, :], scalar=-1.0, in1=XR[0:HB, :], op0=ALU.mult, op1=ALU.max).then_inc(s.x_abs, 1)
            dve.wait_ge(s.x_exp, 1)
            link(v.tensor_scalar(SS[0:HB, :], EX[0:HB, :], 2.0, None, ALU.add))
            link(v.reciprocal(SS[0:HB, :], SS[0:HB, :]))
            link(v.tensor_tensor(SS[0:HB, :], SS[0:HB, :], EX[0:HB, :], ALU.mult))
            link(v.tensor_tensor(HN[0:HB, :], SS[0:HB, :], SS[0:HB, :], ALU.mult))
            link(v.tensor_scalar(EX[0:HB, :], HN[0:HB, :], ATANH[-1], None, ALU.mult))
            for cf in reversed(ATANH[:-1]):
                link(v.scalar_tensor_tensor(out=EX[0:HB, :], in0=EX[0:HB, :], scalar=cf, in1=HN[0:HB, :], op0=ALU.add, op1=ALU.mult))
            link(v.scalar_tensor_tensor(out=EX[0:HB, :], in0=EX[0:HB, :], scalar=1.0, in1=SS[0:HB, :], op0=ALU.add, op1=ALU.mult))
            link(v.tensor_scalar(HN[0:HB, :], XR[0:HB, :], 0.0, None, ALU.max))
            link(v.scalar_tensor_tensor(out=XR[0:HB, :], in0=EX[0:HB, :], scalar=2.0, in1=HN[0:HB, :], op0=ALU.mult, op1=ALU.add))
            dve.wait_ge(s.x_exp, 2)
            link(v.tensor_scalar(SS[0:HB, 0:T], XR[0:HB, 0:T], c16[:, 5:6], None, ALU.mult))
            v.tensor_tensor_scan(AR[0:HB, 0:NP], ENM[0:HB, 0:NP], SS[0:HB, 0:NP], 0.0, ALU.mult, ALU.add)
            link(v.tensor_copy(AR[0:HB, NP:T], SS[0:HB, NP:T]))
            v.tensor_tensor_scan(BN[0:HA, 0:NP], ENM[0:HA, 0:NP], XR[0:HA, T:T + NP], 0.0, ALU.mult, ALU.add)
            link(v.tensor_copy(BN[0:HA, NP:T], XR[0:HA, T + NP:2 * T]))
            link(v.tensor_tensor(AC[0:HA, :], RI[0:HA, :], BN[0:HA, :], ALU.add))
            dve.wait_ge(s.late_in, 16 * 6)
            v.tensor_tensor_scan(MX[0:HA, 0:NP], AC[0:HA, 0:NP], AC[0:HA, 0:NP], 0.0, ALU.max, ALU.max)
            link(v.tensor_tensor(MX[0:HA, NP:T], AC[0:HA, NP:T], m0s[:, :], ALU.max))
            v.tensor_tensor(MROW[0:HA, :], MX[0:HA, :], BN[0:HA, :], ALU.subtract)
            v.tensor_scalar(c16[0:HA, 6:7], MX[0:HA, NP - 1:NP], -1.0, None, ALU.mult)
            v.tensor_scalar(c16[:, 7:8], AR[0:HB, NP - 1:NP], -1.0, None, ALU.mult)
            v.tensor_tensor(WSR[0:HA, NP:T], AC[0:HA, NP:T], MX[0:HA, NP:T], ALU.subtract)
            v.tensor_tensor(RS[:, 0:NB], m0s[:, :], MX[0:HA, NP:T], ALU.subtract)
            v.tensor_tensor(RS[:, NB:2 * NB], AC[0:HA, NP:T], MX[0:HA, NP:T], ALU.subtract)
            v.tensor_copy(RX[:, NB:2 * NB], XR[0:HB, NP:T])
            v.tensor_copy(RX[:, 16:17], c16[:, 4:5]).then_inc(s.rows_pre, 1)

            def conv_taps(n):
                kind, c, _u, _o = UT[n]
                src = CA if kind == "xa" else CBX
                w0, n0_, bcol = (V_CAW, KD, V_CAB) if kind == "xa" else (V_CBW, CB_T, V_CBB)
                y = CY[:, n % 2, :]
                dve.wait_ge(s.lc_ready, n + 1)
                if n >= 2:
                    dve.wait_ge(s.conv_done, n - 1)
                link(v.tensor_scalar(y, src[:, c, 0:W], PV[:, w0 + c:w0 + c + 1], PV[:, bcol + c:bcol + c + 1], ALU.mult, ALU.add))
                for j in range(1, TAPS):
                    wj = w0 + j * n0_ + c
                    ins = v.scalar_tensor_tensor(out=y, in0=src[:, c, j:j + W], scalar=PV[:, wj:wj + 1], in1=y,
                                                 op0=ALU.mult, op1=ALU.add)
                    if j < TAPS - 1:
                        link(ins)
                ins.then_inc(s.conv_y, 1)

            def conv_gate(n):
                kind, c, _u, _o = UT[n]
                dst = XC[:, c, :] if kind == "xa" else CBX[:, c, 0:W]
                dve.wait_ge(s.conv_sig, n + 1)
                v.tensor_tensor(dst, CY[:, n % 2, :], CSG[:, n % 2, :], ALU.mult).then_inc(s.conv_done, 1)

            dve.wait_ge(s.prev_ready, 2)
            for n in range(NCONV):
                conv_taps(n)
                if n >= 1:
                    conv_gate(n - 1)
            conv_gate(NCONV - 1)
            for n, (kind, c, _u, _o) in enumerate(UT):
                if kind == "zb":
                    dve.wait_ge(s.z_sig, c + 1)
                    v.tensor_tensor(ZB[:, c, :], bank[(n + 3) % 4][:, 0:T], ZB[:, c, :], ALU.mult).then_inc(u_free[(n + 3) % 4], 1)

            dve.wait_ge(s.tm_ps, 1)
            v.tensor_copy(TM[:, 0:2, :], bank[4][:, 0:128].rearrange("p (a b) -> p a b", b=64))
            v.tensor_copy(TM[0:16, 2, :], bank[4][0:16, 128:192]).then_inc(s.tm_ready, 1)
            dve.wait_ge(s.bcm_ps, 1)
            v.tensor_copy(BCM[:], bank[5][:, 0:128].rearrange("p (a b) -> p a b", b=16))
            v.tensor_copy(XE[:], bank[5][:, 128:128 + KD * 17].rearrange("p (a b) -> p a b", b=17)).then_inc(s.bcm_ready, 1)

            def decay_args(n, b, key, done, arg_free):
                for j, (t0, m) in enumerate(S_TILES):
                    w = NP - t0
                    last = v.scalar_tensor_tensor(out=ARG[0:m, n % 2, BLK[j]:BLK[j] + w], in0=b[0:m, t0:NP],
                                                  scalar=TM[0:m, j, key:key + 1], in1=mask[0:m, 0:w],
                                                  op0=ALU.subtract, op1=ALU.max)
                last.then_inc(done, 1)

            def head_keys(h):
                if h >= 2:
                    dve.wait_ge(s.nc_ps, h - 1)
                dve.wait_ge(s.kt_ps, h + 1)
                for j, (_t0, m) in enumerate(S_TILES):
                    last = v.tensor_scalar(kw[0:m, h % 2, j, :], bank[2][0:m, j * P:(j + 1) * P],
                                           TM[0:m, j, 8 + h:9 + h], DH ** -0.5, ALU.mult, ALU.mult)
                last.then_inc(s.kw_sb, 1)

            tmp3 = TMPS.rearrange("p (a b) -> p a b", b=P)
            xs_s = CBX[:, 0:KD, SC0:SC0 + TAPS * (NB - 1) + 1:TAPS]
            dve.wait_ge(s.bcm_ready, 1)
            v.tensor_tensor(YS2[:], xs_s, XE[:, :, 16:17].to_broadcast([P, KD, NB]), ALU.mult)
            link(v.tensor_tensor(XDS[:], xs_s, XE[:, :, NB:2 * NB], ALU.mult))

            def s_update(b):
                dve.wait_ge(bb_in[b % 2], 16 * (b // 2 + 1))
                for j in range(NG):
                    last = v.tensor_tensor(tmp3[:, 4 * j:4 * j + 4, :], BB[:, b % 2, j * P:(j + 1) * P].unsqueeze(1).to_broadcast([P, 4, P]),
                                           bc_last(XDS[:, 4 * j:4 * j + 4, b], P), ALU.mult)
                link(last)
                dve.wait_ge(s.st_dec, b + 1)
                st = stage[:, b % 3, :]
                st3d = st.rearrange("p (a b) -> p a b", b=P)
                v.tensor_tensor(st, st, TMPS, ALU.add).then_inc(s.st_new, 1)
                dve.wait_ge(s.st_new, b + 1)
                for j in range(NG):
                    last = v.tensor_tensor(tmp3[:, 4 * j:4 * j + 4, :], st3d[:, 4 * j:4 * j + 4, :],
                                           BB[:, b % 2, (2 + j) * P:(3 + j) * P].unsqueeze(1).to_broadcast([P, 4, P]), ALU.mult)
                last.then_inc(s.s_y, 1)
                dve.wait_ge(s.s_y, b + 1)
                link(v.tensor_reduce(YS[:, :, b], tmp3, AX, ALU.add))

            dve.wait_ge(s.tm_ready, 1)
            for h in range(HA):
                head_keys(h)
                dve.wait_ge(s.sc_ps, h + 1)
                if h >= 2:
                    dve.wait_ge(s.nc_ps, h - 1)
                decay_args(h, bank[5], h, s.arg_done, None)
                dve.wait_ge(s.exp_done, h + 1)
                v.tensor_tensor(ARG[:, h % 2, 0:BLK[2]], bank[4][:, 0:BLK[2]], ARG[:, h % 2, 0:BLK[2]], ALU.mult)
                v.tensor_tensor(ARG[0:16, h % 2, BLK[2]:BLKW], bank[4][0:16, BLK[2]:BLKW], ARG[0:16, h % 2, BLK[2]:BLKW],
                                ALU.mult).then_inc(s.st_done, 1)
                s_update(h)

            dve.wait_ge(s.n0_ps, 1)
            v.tensor_copy(NSTo[:], bank[0][0:HA, 64:64 + P])
            bh = "p (b h) -> p h b"
            dve.wait_ge(s.n0_ps, 1)
            dve.wait_ge(s.qs_done, HA)
            dve.wait_ge(s.bcm_ready, 1)
            v.tensor_tensor(NT[:].rearrange(bh, h=HA), bank[0][:, 0:64].rearrange(bh, h=HA), BCM[:, :, 0:NB], ALU.mult)
            link(v.tensor_tensor(KS[:], KS[:], BCM[:, :, NB:2 * NB], ALU.mult))
            link(v.tensor_tensor(N1[:].rearrange(bh, h=HA), NT[:].rearrange(bh, h=HA), KS[:], ALU.add))
            v.tensor_tensor(QN[:].rearrange(bh, h=HA), N1[:].rearrange(bh, h=HA), QS[:], ALU.mult).then_inc(s.n1_ready, 1)
            dve.wait_ge(s.n1_ps, 1)
            v.tensor_copy(N1T[:], bank[5][0:64, 0:P]).then_inc(s.n1_sb, 1)
            link(v.tensor_tensor(YB[:, :, NP:T], YS[:], YS2[:], ALU.add))
            dve.wait_ge(s.den_ps, 1)
            v.tensor_copy(DEN[0:HA, :], bank[7][0:HA, 0:T]).then_inc(s.den_sb, 1)
            dve.wait_ge(s.den_sb, 1)
            link(v.scalar_tensor_tensor(out=DEN[0:HA, :], in0=DEN[0:HA, :], scalar=-1.0, in1=DEN[0:HA, :], op0=ALU.mult, op1=ALU.max))
            link(v.tensor_tensor(DEN[0:HA, :], DEN[0:HA, :], ENM[0:HA, :], ALU.max))
            link(v.reciprocal(DEN[0:HA, :], DEN[0:HA, :]))

            def c_update(b):
                dve.wait_ge(vb_in[b % 2], 16 * (b // 2 + 1))
                kv = VB[b % 2].rearrange("p (a b) -> p a b", b=P)
                link(v.tensor_tensor(kv, kv, bc_last(KS[:, :, b], P), ALU.mult))
                dve.wait_ge(s.st_dec, NB + b + 1)
                st = stage[:, (NB + b) % 3, :]
                v.tensor_tensor(st, st, VB[b % 2], ALU.add).then_inc(s.st_new, 1)

            for j, (_t0, m) in enumerate(S_TILES):
                for half in range(2):
                    q = 2 * j + half
                    dve.wait_ge(s.xs_ps, q + 1)
                    v.tensor_tensor(XDT[0:m, j, half * 512:(half + 1) * 512].rearrange("p (h q) -> p h q", q=HD),
                                    bank[q][0:m, :].rearrange("p (h q) -> p h q", q=HD),
                                    bc_last(TM[0:m, j, 32 + 8 * half:40 + 8 * half], HD), ALU.mult).then_inc(s.xdt_ready, 1)
            def gate_y(c):
                dve.wait_ge(y_free[c % 2], c // 2 + 1)
                v.tensor_tensor(YB[:, c, :], YB[:, c, :], ZB[:, c, :], ALU.mult).then_inc(s.yz_ready, 1)

            for h in range(HB):
                dve.wait_ge(s.bc_ps, h + 1)
                if h >= 2:
                    dve.wait_ge(s.y_ps, h - 1)
                decay_args(h, bank[5 - h % 2], 16 + h, s.arg2_done, None)
                if h == 0:
                    dve.wait_ge(s.gt_ready, NG)
                dve.wait_ge(s.exp2_done, h + 1)
                j = h // (HB // NG)
                v.tensor_tensor(ARG[:, h % 2, 0:BLK[2]], GT[:, j, 0:BLK[2]], ARG[:, h % 2, 0:BLK[2]], ALU.mult)
                v.tensor_tensor(ARG[0:16, h % 2, BLK[2]:BLKW], GT[0:16, j, BLK[2]:BLKW], ARG[0:16, h % 2, BLK[2]:BLKW],
                                ALU.mult).then_inc(s.st2_done, 1)
                if h % 2 == 0 and h >= 2:
                    ssd_out(dve, h // 2 - 1)
                    gate_y(h // 2 - 1)
                if h % 2 == 0:
                    c_update(h // 2)
            ssd_out(dve, KD - 1)
            gate_y(KD - 1)
            dve.wait_ge(s.sq_ps, HA + KD + 1)
            link(v.tensor_tensor(SCL[0:HA, :], bank[7][0:HA, 0:T], DEN[0:HA, :], ALU.mult))
            v.tensor_tensor(SCL[0:HA, :], SCL[0:HA, :], DEN[0:HA, :], ALU.mult).then_inc(s.rden_ready, 1)
            dve.wait_ge(s.za_done, HA)
            dve.wait_ge(s.cq_sb, 1)
            v.tensor_tensor(NUM[:, :, NP:T], NUM[:, :, NP:T], ZA[:, :, NP:T], ALU.mult)
            dve.wait_ge(s.sc_exp, 1)
            v.tensor_tensor(SCL[0:HA, :], SCL[0:HA, :], DEN[0:HA, :], ALU.mult).then_inc(s.scale_ready, 1)
            for h in range(HA):
                if h == 0:
                    dve.wait_ge(s.scale_ready, 1)
                dve.wait_ge(s.hbc_ps, h + 1)
                v.scalar_tensor_tensor(out=NUM[:, h, :], in0=bank[1 + h % 4][:, 0:T], scalar=PV[:, V_NA + h:V_NA + h + 1],
                                       in1=NUM[:, h, :], op0=ALU.mult, op1=ALU.mult).then_inc(s.num_ready, 1)
            for c in range(KD):
                if c % 4 == 0:
                    dve.wait_ge(s.gbc_ps, c // 4 + 1)
                v.scalar_tensor_tensor(out=YB[:, c, :], in0=bank[6 if c < 4 else 0][:, 0:T],
                                       scalar=PV[:, V_NB + c:V_NB + c + 1], in1=YB[:, c, :],
                                       op0=ALU.mult, op1=ALU.mult).then_inc(s.yb_norm, 1)

            for half in range(2):
                for i, (_t0, m) in enumerate(TOK):
                    if half == 0 and i == 0:
                        dve.wait_ge(s.x_again, 16 * 3)
                    dve.wait_ge(s.wt_ps, half + 1)
                    hv = h_tok[0:m, i, half * 512:(half + 1) * 512]
                    ins = v.tensor_tensor(hv, hv, bank[i + 3 * half][0:m, :], ALU.add)
                    if half == 1:
                        ins.then_inc(s.h_ready, 1)
            for i, (_t0, m) in enumerate(TOK):
                dve.wait_ge(s.h_rstd, 1)
                v.tensor_scalar(xn[0:m, i, :], h_tok[0:m, i, :], st3[0:m, 4 + i:5 + i], None, ALU.mult).then_inc(s.xn2_ready, 1)
            for i, (t0, m) in enumerate(TOK):
                for half in range(2):
                    q = 2 * i + half
                    dve.wait_ge(s.xt_ps, q + 1)
                    src = bank[q][:, :].rearrange("p (k n) -> p k n", n=P)
                    gain = PV[:, V_NFF + 4 * half:V_NFF + 4 * half + 4]
                    v.tensor_tensor(XT[:, 4 * half:4 * half + 4, t0:t0 + m], src[:, :, 0:m], bc_last(gain, m), ALU.mult)\
                        .then_inc(s.xt_ready, 1)
            dve.wait_ge(s.lg_ps, 1)
            v.tensor_copy(L[:, 0:2, :], bank[6][:, 0:40].rearrange("p (a b) -> p a b", b=20))
            link(v.tensor_copy(L[0:NB, 2, :], bank[6][0:NB, 40:60]))
            LG = L[:, :, 0:4]

            def bc4(c):
                return r1[:, :, c:c + 1].to_broadcast([P, 3, 4])

            ord3 = order[:].unsqueeze(1).to_broadcast([P, 3, 4])

            def first_best(out, vals, c, ck):
                link(v.tensor_tensor(K1[:], vals, bc4(c), ALU.is_equal))
                link(v.tensor_tensor(K1[:], K1[:], ord3, ALU.mult))
                link(v.tensor_reduce(r1[:, :, ck], K1[:], AX, ALU.max))
                link(v.tensor_tensor(out, K1[:], bc4(ck), ALU.is_equal))

            link(v.tensor_reduce(r1[:, :, 0], LG, AX, ALU.max))
            v.tensor_tensor(LX[:], LG, bc4(0), ALU.subtract).then_inc(s.lx_ready, 1)
            first_best(M1[:], LG, 0, 1)
            for i in range(3):
                last = v.tensor_tensor(LP[:, i], L[:, i, 4:20].rearrange("p (g e) -> p e g", g=EG),
                                       M1[:, i, :].unsqueeze(1).to_broadcast([P, EPG, EG]), ALU.mult)
            link(last)
            link(v.tensor_reduce(L2[:], LP[:], AX, ALU.add))
            link(v.tensor_reduce(r1[:, :, 2], L2[:], AX, ALU.max))
            first_best(O1[:], L2[:], 2, 1)
            link(v.scalar_tensor_tensor(out=L2[:], in0=O1[:], scalar=-BIG, in1=L2[:], op0=ALU.mult, op1=ALU.add))
            link(v.tensor_reduce(r1[:, :, 4], L2[:], AX, ALU.max))
            v.tensor_tensor(r1[:, :, 3], r1[:, :, 4], r1[:, :, 2], ALU.subtract).then_inc(s.lx_ready, 1)
            first_best(O2[:], L2[:], 4, 1)
            dve.wait_ge(s.p1_exp, 1)
            link(v.tensor_reduce(r1[:, :, 5], LX[:], AX, ALU.add))
            dve.wait_ge(s.p1_exp, 2)
            link(v.tensor_scalar(r1[:, :, 6], r1[:, :, 3], 1.0, None, ALU.add))
            link(v.tensor_tensor(r1[:, :, 6], r1[:, :, 6], r1[:, :, 5], ALU.mult))
            link(v.reciprocal(r1[:, :, 6], r1[:, :, 6]))
            link(v.tensor_tensor(r1[:, :, 7], r1[:, :, 6], r1[:, :, 3], ALU.mult))
            v.tensor_tensor(O1[:], O1[:], bc4(6), ALU.mult)
            link(v.tensor_tensor(O2[:], O2[:], bc4(7), ALU.mult))
            v.tensor_tensor(GATE[:], O1[:], O2[:], ALU.add).then_inc(s.router, 1)
            dve.wait_ge(s.rank_ps, 1)
            v.tensor_copy(rank[:, 0:2, :], bank[0][:, 0:8].rearrange("p (a b) -> p a b", b=4))
            v.tensor_copy(rank[0:NB, 2, :], bank[0][0:NB, 8:12]).then_inc(s.rank_ready, 1)
            link(v.tensor_reduce(cnt[:, 0:1], bank[0][:, 12:16], AX, ALU.max))
            v.tensor_scalar(cnt[:, 1:2], cnt[:, 0:1], 128.0, 1.0, ALU.is_gt, ALU.add).then_inc(s.yg_done, 1)
            link(v.tensor_scalar(cnt[:, 2:3], cnt[:, 0:1], 256.0, None, ALU.is_gt))
            v.tensor_tensor(rounds[:], cnt[:, 1:2], cnt[:, 2:3], ALU.add).then_inc(s.rounds_ready, 1)

            nr = rounds_of(dve)
            with dve.Fori(0, nr) as r:
                dve.wait_ge(s.rank_ready, r + 1)
                for i, (_t0, m) in enumerate(TOK):
                    for q in range(EG):
                        last = v.tensor_scalar(PG[0:m, i, q * P:(q + 1) * P], iota[0:m, :], rank[0:m, i, q:q + 1],
                                               M1[0:m, i, q:q + 1], ALU.is_equal, ALU.mult)
                last.then_inc(s.p_ready, 1)
                for k in range(0, KD, 2):
                    dve.wait_ge(s.xg_ps, r * KD + (k + 1))
                    v.tensor_scalar(XG[:, k, :], bank[k][:, :], PV[:, V_NFF + k:V_NFF + k + 1], None, ALU.mult)\
                        .then_inc(s.xg_ready, 1)
                v.memset(YG.rearrange("p a b -> p (a b)"), 0.0)
                dve.wait_ge(s.pt_ps, r + 1)
                v.tensor_copy(GS[:], bank[0][:, 0:16])
                for q in range(EG):
                    last = v.tensor_copy(PT[:, q, :], bank[1 + q][:, 0:NOUT])
                last.then_inc(s.pt_ready, 1)
                with dve.Fori(0, EG) as q:
                    with dve.Fori(0, EPG) as e:
                        x = (r * EG + q) * EPG + e
                        for j in range(2):
                            if j == 0:
                                dve.wait_ge(s.pt_ready, r + 1)
                            dve.wait_ge(s.silu_done, x * 2 + (j + 1))
                            dve.wait_ge(s.gu_ps, x * 2 + (j + 2))
                            v.scalar_tensor_tensor(out=AH[:, j * 512:(j + 1) * 512], in0=bank[2 * j + 1][:, :],
                                                   scalar=GS[:, bass.ds(q * EPG + e, 1)], in1=SG[:, j * 512:(j + 1) * 512],
                                                   op0=ALU.mult, op1=ALU.mult).then_inc(s.a_ready, 1)
                        dve.wait_ge(s.d_ps, x + 1)
                        dve.wait_ge(s.yg_done, x + 1)
                        yv = YG.rearrange("p a b -> p (a b)")
                        for j in range(2):
                            o = yv[:, bass.ds(q * D + j * 512, 512)]
                            last = v.tensor_tensor(o, o, bank[6 + j][:, :], ALU.add)
                        last.then_inc(s.yg_done, 1)
                for i, (_t0, m) in enumerate(TOK):
                    for half in range(2):
                        dve.wait_ge(s.sc_out_ps, r * 6 + (2 * i + half + 1))
                        hv = h_tok[0:m, i, half * 512:(half + 1) * 512]
                        v.tensor_tensor(hv, hv, bank[2 * i + half][0:m, :], ALU.add).then_inc(s.h_add, 1)
                v.tensor_scalar(rank[:, 0:2, :], rank[:, 0:2, :], float(P), None, ALU.subtract)
                v.tensor_scalar(rank[0:NB, 2, :], rank[0:NB, 2, :], float(P), None, ALU.subtract).then_inc(s.rank_ready, 1)

            dve.wait_ge(s.nf_in, 16)
            for i, (_t0, m) in enumerate(TOK):
                dve.wait_ge(s.f_rstd, 1)
                v.scalar_tensor_tensor(out=h_tok[0:m, i, :], in0=h_tok[0:m, i, :], scalar=st3[0:m, 4 + i:5 + i],
                                       in1=NF[0:m, :], op0=ALU.mult, op1=ALU.mult).then_inc(s.y_ready, 1)

        @block.tensor
        def _(pe):
            mm = nc.tensor.matmul
            tr = nc.tensor.transpose

            pe.wait_ge(s.consts, 1)
            pe.wait_ge(s.params_in, 16 * 13)
            tr(bank[7][:, 0:84], PR[0:84, 0, :], ident[0:84, 0:84])
            tr(bank[7][:, 84:132], PR[0:48, 1, :], ident[0:48, 0:48]).then_inc(s.pv_ps, 1)
            for i, m in enumerate((P, P, NB + META)):
                pe.wait_ge(s.xn_ready, i + 1)
                for k in range(KD):
                    last = tr(bank[2 * i + k // 4][:, (k % 4) * P:(k % 4) * P + m], xn[0:m, i, k * P:(k + 1) * P], ident[0:m, 0:m])
                    if k % 4 == 3:
                        last.then_inc(s.ht_ps, 1)
            pe.wait_ge(s.prev_in, 32)
            pe.wait_ge(s.pv_ready, 1)
            for base, b, n in ((0, bank[6], KD), (KD, bank[7], CB_T)):
                for c in range(n):
                    last = tr(b[:, c * 24:(c + 1) * 24], CPREV[0:24, (base + c) * P:(base + c + 1) * P], ident[0:24, 0:24])
                last.then_inc(s.prev_ps, 1)

            pe.wait_ge(s.ht_ready, 6)
            pe.wait_ge(s.gates_in, 48)
            for k in range(KD):
                last = mm(bank[0][0:80, 0:T], WG[:, k, :], hT[:, k, :], start=(k == 0), stop=(k == KD - 1))
            last.then_inc(s.u_ps, 3)
            for n0_, (kind, c, u, o) in enumerate(UT):
                n = n0_ + 3
                if o == 0:
                    i, cnt_ = unit_at(u)
                    pe.wait_ge(arrived[i], cnt_)
                if n >= 4:
                    pe.wait_ge(u_free[n % 4], n // 4)
                for k in range(KD):
                    last = mm(bank[n % 4][:, 0:T], slot_k(u % MR, 512)[:, k, o:o + P], hT[:, k, :],
                              start=(k == 0), stop=(k == KD - 1))
                last.then_inc(s.u_ps, 1)

            pe.wait_ge(s.rows_pre, 1)
            pe.wait_ge(s.rows_exp, 1)
            for j, (t0, m) in enumerate(S_TILES):
                for rows, nrow, c0 in ((AC, HA, 0), (WSR, HA, 8), (AR, HB, 16), (XR, HB, 32), (EDR, HB, 48)):
                    last = tr(bank[4][0:m, j * 64 + c0:j * 64 + c0 + nrow], rows[0:nrow, t0:t0 + m], ident[0:nrow, 0:nrow])
            last.then_inc(s.tm_ps, 1)
            for h in range(HA):
                mm(bank[5][:, h * 16:(h + 1) * 16], col(ident[0:HA, :], h), RS[:, :], start=True, stop=True)
            for c in range(KD):
                for j in range(2):
                    last = mm(bank[5][j * HD:(j + 1) * HD, 128 + c * 17:128 + (c + 1) * 17],
                              ident[0:HB, 2 * c + j:2 * c + j + 1].to_broadcast([HB, HD]), RX[:, :], start=True, stop=True)
            last.then_inc(s.bcm_ps, 1)
            for q in range(5):
                if q >= 2:
                    pe.wait_ge(s.lct_sb, q - 1)
                if q == 0:
                    pe.wait_ge(u_free[(NCONV + 2) % 4], (NCONV + 2) // 4 + 1)
                for c in range(4):
                    last = tr(bank[6 + q % 2][0:LAST, c * P:(c + 1) * P], LC[:, 4 * q + c, :], ident[:, :])
                last.then_inc(s.lct_ps, 1)

            pe.wait_ge(s.conv_done, NCONV)
            pe.wait_ge(s.lct_sb, 5)
            for c in range(4):
                last = tr(bank[7][0:NB, c * P:(c + 1) * P], smp(CBX[:, KD + c, :]), ident[:, :])
            last.then_inc(s.bcs_ps, 1)

            iq, cq = unit_at(U_QKV)
            pe.wait_ge(arrived[iq], cq)
            wq, wk, wv = (slot[iq][:, j * D:(j + 1) * D].rearrange("p (h e) -> p h e", e=DH) for j in range(3))
            for b, n in enumerate((10, 10, 10, 9)):
                pe.wait_ge(u_free[b], n)

            def head_proj(h):
                if h >= 1:
                    pe.wait_ge(s.q_sb, h)
                    pe.wait_ge(s.k_sb, h)
                    pe.wait_ge(s.kw_sb, h)
                    pe.wait_ge(s.v_sb, h)
                mm(bank[0][:, 0:W], wq[:, h, :], XC[:, h, :], start=True, stop=True).then_inc(s.q_ps, 1)
                mm(bank[1][:, 0:W], wk[:, h, :], XC[:, h, :], start=True, stop=True).then_inc(s.k_ps, 1)
                for j, (t0, m) in enumerate(S_TILES):
                    last = mm(bank[2][0:m, j * P:(j + 1) * P], XC[:, h, t0:t0 + m], wk[:, h, :], start=True, stop=True)
                last.then_inc(s.kt_ps, 1)
                for j, (t0, m) in enumerate(S_TILES):
                    mm(bank[3][0:m, j * P:(j + 1) * P], CA[:, h, PAD + t0:PAD + t0 + m], wv[:, h, :], start=True, stop=True)
                mm(bank[3][0:NB, 384:512], CA[:, h, SC0 + PAD:SC0 + PAD + TAPS * (NB - 1) + 1:TAPS], wv[:, h, :],
                   start=True, stop=True).then_inc(s.vt_ps, 1)

            def block_mm(b, c0, lhs, rhs, key, start, accumulate):
                for j, (t0, m) in enumerate(S_TILES):
                    w = NP - t0
                    if accumulate:
                        o = b[:, c0 + t0:c0 + NP]
                    else:
                        o = b[0:m, BLK[j]:BLK[j] + w]
                    last = mm(o, lhs(j, t0, m), rhs(j, t0, m, w), start=(start and (j == 0 or not accumulate)),
                              stop=(j == 2 or not accumulate))
                return last

            head_proj(0)
            pe.wait_ge(s.tm_ready, 1)
            pe.wait_ge(s.bcm_ready, 1)
            for h in range(HA):
                if h >= 1:
                    pe.wait_ge(s.st_done, h)
                pe.wait_ge(s.q_sb, h + 1)
                pe.wait_ge(s.k_sb, h + 1)
                mm(bank[5][:, 0:NP], col(ident[0:HA, :], h), MX[0:HA, 0:NP], start=True, stop=True)
                block_mm(bank[4], 0, lambda j, t0, m: kT[:, h % 2, t0:t0 + m], lambda j, t0, m, w: qT[:, h % 2, t0:NP],
                         None, True, False).then_inc(s.sc_ps, 1)
                if h + 1 < HA:
                    head_proj(h + 1)
                pe.wait_ge(s.st_done, h + 1)
                pe.wait_ge(s.v_sb, h + 1)
                pe.wait_ge(s.kw_sb, h + 1)
                if h >= 1:
                    pe.wait_ge(s.num_sb, h)
                else:
                    pe.wait_ge(s.bcs_ready, 1)
                sc = lambda j, t0, m, w: ARG[0:m, h % 2, BLK[j]:BLK[j] + w]
                block_mm(bank[6], 0, lambda j, t0, m: vv[0:m, h % 2, j, 0:P], sc, None, True, True)
                for j, (t0, m) in enumerate(S_TILES):
                    mm(bank[7][0:HA, t0:NP], strip[0:m, 7 - h:15 - h], sc(j, t0, m, NP - t0),
                       start=(h == 0 and j == 0), stop=(h == HA - 1 and j == 2), skip_group_check=True)
                for j, (t0, m) in enumerate(S_TILES):
                    last = mm(bank[6][:, NP:NP + P + 1], kw[0:m, h % 2, j, :], vv[0:m, h % 2, j, :], start=(j == 0), stop=(j == 2))
                last.then_inc(s.nc_ps, 1)
            pe.wait_ge(s.late_in, 16 * 6)
            pe.wait_ge(s.nst_ready, HA)
            tr(bank[0][:, 0:64], N0[:, :], ident[0:64, 0:64])
            tr(bank[0][0:HA, 64:64 + P], NSTt[:, :], ident[:, :]).then_inc(s.n0_ps, 1)
            pe.wait_ge(s.n1_ready, 1)
            for h in range(HA):
                last = mm(bank[7][0:HA, NP:T], strip[:, 7 - h:15 - h], QN[:].rearrange("p (b h) -> p h b", h=HA)[:, h, :],
                          start=(h == 0), stop=(h == HA - 1), skip_group_check=True)
            last.then_inc(s.den_ps, 1)
            tr(bank[5][0:64, 0:P], N1[:, :], ident[:, :]).then_inc(s.n1_ps, 1)

            for j, (t0, m) in enumerate(S_TILES):
                for half in range(2):
                    q = 2 * j + half
                    if q == 0:
                        pe.wait_ge(s.n1_sb, 1)
                        pe.wait_ge(s.s_y, NB)
                    bq = bank[q]
                    for c in range(4):
                        last = tr(bq[0:m, c * P:(c + 1) * P], CBX[:, 4 * half + c, t0:t0 + m], ident[:, :])
                    last.then_inc(s.xs_ps, 1)
            pe.wait_ge(s.xdt_ready, 6)
            for j, (t0, m) in enumerate(S_TILES):
                for g_ in range(NG):
                    last = tr(bank[j // 2][0:m, (j % 2) * 256 + g_ * P:(j % 2) * 256 + (g_ + 1) * P], CBX[:, KD + g_, t0:t0 + m], ident[:, :])
            last.then_inc(s.bt_ps, 1)
            for g_ in range(NG):
                block_mm(bank[3 + g_], 0, lambda j, t0, m: CBX[:, KD + g_, t0:t0 + m], lambda j, t0, m, w: CBX[:, KD + NG + g_, t0:NP],
                         None, True, False).then_inc(s.gt_ps, 1)

            def decay_row(h):
                if h >= 2:
                    pe.wait_ge(s.arg2_done, h - 1)
                elif h == 1:
                    pe.wait_ge(s.gt_ready, NG)
                mm(bank[5 - h % 2][:, 0:NP], col(ident[0:HB, :], h), AR[0:HB, 0:NP], start=True, stop=True).then_inc(s.bc_ps, 1)

            def c_read(b):
                pe.wait_ge(s.st_new, NB + b + 1)
                for h in range(HA):
                    last = mm(bank[3][:, b * HA + h:b * HA + h + 1], stage[:, (NB + b) % 3, h * P:(h + 1) * P],
                              QS[:, h, b:b + 1], start=True, stop=True)
                last.then_inc(s.cq_ps, 1)

            summed = [0]

            def group_sum():
                c = summed[0]
                summed[0] += 1
                g_ = c // 4
                pe.wait_ge(s.sq_done, HA + c + 1)
                mm(bank[7][32:32 + NG, 0:T], strip[:, 7 - g_:9 - g_], SQA[:, c, :], start=(c == 0), stop=(c == KD - 1)).then_inc(s.sq_ps, 1)

            decay_row(0)
            for h in range(HB):
                c = h // 2
                if h + 1 < HB:
                    decay_row(h + 1)
                if h == 0:
                    pe.wait_ge(s.bt_ready, 1)
                    pe.wait_ge(s.gt_ready, NG)
                if h % 2 == 0 and c >= 1:
                    c_read(c - 1)
                if h == 0:
                    pe.wait_ge(s.den_sb, 1)
                if h == 1:
                    pe.wait_ge(s.xw_ready, 3)
                if h % 2 == 1:
                    for j, (t0, m) in enumerate(S_TILES):
                        last = mm(bank[1 + c // 4][:, (c % 4) * P:(c % 4 + 1) * P], XWT[0:m, j, c * P:(c + 1) * P],
                                  BT[0:m, j, (c // 4) * P:(c // 4 + 1) * P], start=(j == 0), stop=(j == 2))
                    if c % 4 == 3:
                        last.then_inc(s.sst_ps, 1)
                if h < HA:
                    pe.wait_ge(s.sq_done, h + 1)
                    mm(bank[7][0:HA, 0:NP], strip[:, 7 - h:15 - h], SQA[:, h, 0:NP], start=(h == 0), stop=(h == HA - 1)).then_inc(s.sq_ps, 1)
                if h >= HA and h % 2 == 0:
                    for cc in range({8: 3, 10: 1, 12: 1, 14: 1}[h]):
                        group_sum()
                pe.wait_ge(s.st2_done, h + 1)
                if h % 2 == 0 and c >= 2:
                    pe.wait_ge(y_free[c % 2], c // 2)
                yb = bank[6 if c % 2 == 0 else 0]
                q0 = HD * (h % 2)
                for j, (t0, m) in enumerate(S_TILES):
                    last = mm(yb[q0:q0 + HD, t0:NP], XDT[0:m, j, h * HD:(h + 1) * HD], ARG[0:m, h % 2, BLK[j]:BLK[j] + NP - t0],
                              start=(j == 0), stop=(j == 2))
                last.then_inc(s.y_ps, 1)
            c_read(NB - 1)
            group_sum()
            group_sum()
            pe.wait_ge(s.cq_sb, 1)
            for h in range(HA):
                last = mm(bank[7][0:HA, NP:T], strip[:, 7 - h:15 - h], QN[:].rearrange("p (b h) -> p h b", h=HA)[:, h, :],
                          start=(h == 0), stop=(h == HA - 1), skip_group_check=True)
            last.then_inc(s.sq_ps, 1)
            pe.wait_ge(s.sst_ready, 2)
            pe.wait_ge(s.arg2_done, HB)
            pe.wait_ge(y_free[0], 4)
            pe.wait_ge(y_free[1], 4)
            pe.wait_ge(s.scale_ready, 1)
            for h in range(HA):
                if h >= 4:
                    pe.wait_ge(s.num_ready, h - 3)
                mm(bank[1 + h % 4][:, 0:T], col(ident[0:HA, :], h), SCL[0:HA, :], start=True, stop=True).then_inc(s.hbc_ps, 1)
                if h < NG:
                    pe.wait_ge(s.ysc_exp, 1)
                    mm(bank[6 if h == 0 else 0][:, 0:T], col(ident[32:32 + NG, :], 32 + h), YSC, start=True, stop=True).then_inc(s.gbc_ps, 1)

            pe.wait_ge(s.num_ready, HA)
            pe.wait_ge(s.yb_norm, KD)

            def out_part(kc, dt):
                w = slot_k(unit_at(U_OUT + kc // 4)[0], D)
                src = NUM if kc < HA else YB
                return mm(bank[dt][:, 0:NOUT], w[:, kc % 4, dt * P:(dt + 1) * P], src[:, kc % 8, META:T],
                          start=(kc == 0), stop=(kc == 15), skip_group_check=True)

            def out_turn(dt):
                if dt == 0:
                    pe.wait_ge(s.mt_sb, 3)
                if dt == 4:
                    pe.wait_ge(s.mt_sb, 6)
                pe.wait_ge(s.mt_sb, dt + 1)
                for i, (t0, m) in enumerate(TOK):
                    last = tr(bank[i + 3 * (dt // 4)][0:m, (dt % 4) * P:(dt % 4 + 1) * P], MT[:, dt, t0:t0 + m], ident[:, :])
                if dt % 4 == 3:
                    last.then_inc(s.wt_ps, 1)

            for j in range(4):
                i, cnt_ = unit_at(U_OUT + j)
                pe.wait_ge(arrived[i], cnt_)
                if j < 3:
                    for kk in range(4):
                        for dt in range(KD):
                            last = out_part(4 * j + kk, dt)
                    last.then_inc(s.wo_unit, 1)
                else:
                    for dt in range(KD):
                        for kk in range(4):
                            last = out_part(4 * j + kk, dt)
                        last.then_inc(s.mo_ps, 1)
                        if dt >= 3:
                            out_turn(dt - 3)
                    for dt in range(5, 8):
                        out_turn(dt)

            for i, (t0, m) in enumerate(TOK):
                pe.wait_ge(s.xn2_ready, i + 1)
                if i == 0:
                    pe.wait_ge(s.h_ready, 3)
                for k in range(KD):
                    last = tr(bank[2 * i + k // 4][:, (k % 4) * P:(k % 4) * P + m], xn[0:m, i, k * P:(k + 1) * P], ident[0:m, 0:m])
                    if k % 4 == 3:
                        last.then_inc(s.xt_ps, 1)
            pe.wait_ge(s.late_in, 16 * 6)
            pe.wait_ge(s.xt_ready, 6)
            for i, (t0, m) in enumerate(TOK):
                for k in range(KD):
                    mm(bank[6][0:m, i * 20:(i + 1) * 20], XT[:, k, t0:t0 + m], wr[:, k, :], start=(k == 0), stop=False)
                last = mm(bank[6][0:m, i * 20:(i + 1) * 20], ones[0:1, 0:m], br[:, :], start=False, stop=True)
            last.then_inc(s.lg_ps, 1)
            pe.wait_ge(s.router, 1)
            for i, (_t0, m) in enumerate(TOK):
                for i2 in range(i):
                    mm(bank[0][0:m, 4 * i:4 * i + 4], ones[:, 0:m], M1[:, i2, :], start=(i2 == 0), stop=False)
                last = mm(bank[0][0:m, 4 * i:4 * i + 4], before[0:m, 0:m], M1[0:m, i, :], start=(i == 0), stop=True)
            last.then_inc(s.gu_ps, 1)
            for i, (_t0, m) in enumerate(TOK):
                last = mm(bank[0][:, 12:16], ones[0:m, :], M1[0:m, i, :], start=(i == 0), stop=(i == 2))
            last.then_inc(s.rank_ps, 1)

            nr = rounds_of(pe)
            with pe.Fori(0, nr) as r:
                pe.wait_ge(s.p_ready, r + 1)
                for k in range(KD):
                    for i, (_t0, m) in enumerate(TOK):
                        last = mm(bank[k][:, :], xn[0:m, i, k * P:(k + 1) * P], PG[0:m, i, :], start=(i == 0), stop=(i == 2))
                    last.then_inc(s.xg_ps, 1)
                pe.wait_ge(s.xg_ready, r * KD + KD)
                for q in range(EG):
                    for i, (_t0, m) in enumerate(TOK):
                        last = mm(bank[0][:, 4 * q:4 * q + 4], PG[0:m, i, q * P:(q + 1) * P], GATE[0:m, i, :], start=(i == 0), stop=(i == 2))
                for q in range(EG):
                    for i, (t0, m) in enumerate(TOK):
                        last = tr(bank[1 + q][:, t0:t0 + m], PG[0:m, i, q * P:(q + 1) * P], ident[0:m, 0:m])
                last.then_inc(s.pt_ps, 1)
                with pe.Fori(0, EG) as q:
                    with pe.Fori(0, EPG) as e:
                        x = (r * EG + q) * EPG + e
                        pe.wait_ge(s.pt_ready, r + 1)
                        pe.wait_ge(s.xs_ready, r * EG + q + 1)

                        def weights(c):
                            i = EXP_SLOT[c]
                            pe.wait_ge(arrived[i], x * 16 + (mix_in[i] + 16))
                            return slot_k(i, 512 if c < 4 else D)

                        def project(j, up):
                            w = weights(2 * j + up)
                            for k in range(KD):
                                last = mm(bank[2 * j + up][:, :], XS[:, k, :], w[:, k, :], start=(k == 0), stop=(k == KD - 1))
                            return last

                        def turn(j):
                            pe.wait_ge(s.a_ready, x * 2 + (j + 1))
                            for k in range(4):
                                last = tr(bank[4 + j][:, k * P:(k + 1) * P], AH[:, (4 * j + k) * P:(4 * j + k + 1) * P], ident[:, :])
                            last.then_inc(s.ft_ps, 1)

                        def down(j, half, w):
                            for k in range(4):
                                last = mm(bank[6 + half][:, :], HT[:, 4 * j + k, :], w[:, k, half * 512:(half + 1) * 512],
                                          start=(j == 0 and k == 0), stop=(j == 1 and k == 3), skip_group_check=True)
                            return last

                        project(0, 0).then_inc(s.gate_ps, 1)
                        project(0, 1).then_inc(s.gu_ps, 1)
                        project(1, 0).then_inc(s.gate_ps, 1)
                        turn(0)
                        project(1, 1).then_inc(s.gu_ps, 1)
                        pe.wait_ge(s.yg_done, x + 1)
                        pe.wait_ge(s.ht_sb, x * 2 + 1)
                        w = weights(4)
                        down(0, 0, w)
                        turn(1)
                        down(0, 1, w).then_inc(s.down_ps, 1)
                        pe.wait_ge(s.ht_sb, x * 2 + 2)
                        w = weights(5)
                        down(1, 0, w)
                        down(1, 1, w).then_inc(s.d_ps, 1)
                pe.wait_ge(s.yg_done, (r + 1) * (EG * EPG) + 1)
                for i, (t0, m) in enumerate(TOK):
                    for half in range(2):
                        for q in range(EG):
                            last = mm(bank[2 * i + half][0:m, :], PT[:, q, t0:t0 + m], YG[:, q, half * 512:(half + 1) * 512],
                                      start=(q == 0), stop=(q == EG - 1))
                        last.then_inc(s.sc_out_ps, 1)
                pe.wait_ge(s.h_add, r * 6 + 6)


_INS = ["x_prompt", "x_sample", "state_mlstm_C", "state_mlstm_n", "state_mlstm_m", "state_mlstm_conv",
        "state_ssm", "state_ssm_conv", "meta_tokens", "norm_mix", "w_in", "conv_a_w", "conv_a_b", "w_q",
        "w_k", "w_v", "b_i", "b_f", "norm_a", "conv_b_w", "conv_b_b", "dt_bias", "a_log", "d_skip",
        "norm_b", "w_out", "norm_ffn", "w_r1", "b_r1", "w_r2", "b_r2", "w_gate", "w_up", "w_down",
        "norm_final"]
_OUTS = [(1, SEQ, D), (NB, 1, D),
         (1, 1, HA, DH, DH), (1, 1, HA, DH), (1, 1, HA), (1, 1, PAD, D), (1, 1, HB, HD, NST), (1, 1, PAD, CB_T * P),
         (1, NB, HA, DH, DH), (1, NB, HA, DH), (1, NB, HA), (1, NB, PAD, D), (1, NB, HB, HD, NST), (1, NB, PAD, CB_T * P)]


def kernel(**inputs):
    import numpy as _np
    import concourse.bacc as _bacc
    from concourse.bass_utils import run_bass_kernel_spmd as _run

    nc = _bacc.Bacc("TRN2", target_bir_lowering=False, num_devices=1)
    arrays, args = {}, []
    for name in _INS:
        a = _np.ascontiguousarray(inputs[name])
        arrays[f"in_{name}"] = a
        args.append(nc.dram_tensor(f"in_{name}", a.shape, mybir.dt.from_np(a.dtype), kind="ExternalInput").ap())
    for i, shape in enumerate(_OUTS):
        args.append(nc.dram_tensor(f"out_{i}", shape, F32, kind="ExternalOutput").ap())
    args.append(nc.dram_tensor("rows_dram", (NB, 512 + D), F32, kind="Internal").ap())
    program(nc, *args)
    r = _run(nc, [arrays], core_ids=[0])
    return tuple(r.results[0][f"out_{i}"] for i in range(len(_OUTS)))
```

```python
from contextlib import ExitStack

import concourse.bass as bass
from concourse import mybir

F32 = mybir.dt.float32
I32 = mybir.dt.int32
ALU = mybir.AluOpType
ACT = mybir.ActivationFunctionType
AX = mybir.AxisListType.X

P = 128
D = 1024
KD = D // P
META, SEQ, NB = 16, 256, 8
NP = META + SEQ
T = NP + NB
TAPS = 4
PAD = TAPS - 1
SC0 = NP + PAD
CW = SC0 + NB * TAPS
W = CW - PAD
LAST = PAD + NB
HA, DH = 8, 128
HB, HD, NG, NST = 16, 64, 2, 128
CB_T = (D + 2 * NG * NST) // P
QT = W
S_TILES = [(0, 128), (128, 128), (256, 16)]
BLK = [0, NP, NP + NP - 128]
BLKW = BLK[2] + NP - 256
TOK = [(0, 128), (128, 128), (256, 8)]
NOUT = SEQ + NB
EG, EPG, FF = 4, 4, 1024
SLOT = 4 * 1024
BIG = 1e30
EPS = 1e-6
ATANH = [1.0 / (2 * i + 1) for i in range(1, 9)]

O_XA, O_ZA, O_I, O_F = 0, 1024, 2048, 2056
O_ZB, O_XBC, O_DT = 2064, 3088, 4624
WIN = [O_XA, O_XA + 512, O_XBC, O_XBC + 512, O_XBC + 1024, O_ZA, O_ZA + 512, O_ZB, O_ZB + 512]
U_QKV = len(WIN)
U_OUT = U_QKV + 1
N_MIX = U_OUT + 4
MR = 3
EXP_SLOT = [3, 4, 5, 2, 0, 1]
EXP_FREE = [1, 1, 1, 2, 3]

V_NMIX, V_CAW, V_CAB, V_NA, V_NB, V_NFF, V_CBB, V_CBW = 0, 8, 40, 48, 56, 64, 72, 84


class Signals:

    def __init__(self, sem):
        self.params_in = sem("params_in")
        self.prev_in = sem("prev_in")
        self.gates_in = sem("gates_in")
        self.late_in = sem("late_in")
        self.x_again = sem("x_again")
        self.nf_in = sem("nf_in")
        self.pv_ps = sem("pv_ps")
        self.ht_ps = sem("ht_ps")
        self.prev_ps = sem("prev_ps")
        self.u_ps = sem("u_ps")
        self.tm_ps = sem("tm_ps")
        self.bcm_ps = sem("bcm_ps")
        self.lct_ps = sem("lct_ps")
        self.q_ps = sem("q_ps")
        self.k_ps = sem("k_ps")
        self.kt_ps = sem("kt_ps")
        self.vt_ps = sem("vt_ps")
        self.sc_ps = sem("sc_ps")
        self.nc_ps = sem("nc_ps")
        self.n0_ps = sem("n0_ps")
        self.down_ps = sem("down_ps")
        self.cq_ps = sem("cq_ps")
        self.den_ps = sem("den_ps")
        self.n1_ps = sem("n1_ps")
        self.xs_ps = sem("xs_ps")
        self.bt_ps = sem("bt_ps")
        self.gt_ps = sem("gt_ps")
        self.y_ps = sem("y_ps")
        self.sst_ps = sem("sst_ps")
        self.sq_ps = sem("sq_ps")
        self.hbc_ps = sem("hbc_ps")
        self.gbc_ps = sem("gbc_ps")
        self.wo_unit = sem("wo_unit")
        self.mo_ps = sem("mo_ps")
        self.wt_ps = sem("wt_ps")
        self.xt_ps = sem("xt_ps")
        self.lg_ps = sem("lg_ps")
        self.rank_ps = sem("rank_ps")
        self.xg_ps = sem("xg_ps")
        self.pt_ps = sem("pt_ps")
        self.gate_ps = sem("gate_ps")
        self.gu_ps = sem("gu_ps")
        self.ft_ps = sem("ft_ps")
        self.d_ps = sem("d_ps")
        self.sc_out_ps = sem("sc_out_ps")
        self.consts = sem("consts")
        self.pv_ready = sem("pv_ready")
        self.rstd_ready = sem("rstd_ready")
        self.xn_ready = sem("xn_ready")
        self.ht_ready = sem("ht_ready")
        self.prev_ready = sem("prev_ready")
        self.x_abs = sem("x_abs")
        self.x_exp = sem("x_exp")
        self.rows_pre = sem("rows_pre")
        self.rows_exp = sem("rows_exp")
        self.lc_ready = sem("lc_ready")
        self.conv_y = sem("conv_y")
        self.conv_sig = sem("conv_sig")
        self.conv_done = sem("conv_done")
        self.z_sig = sem("z_sig")
        self.tm_ready = sem("tm_ready")
        self.bcm_ready = sem("bcm_ready")
        self.lct_sb = sem("lct_sb")
        self.q_sb = sem("q_sb")
        self.k_sb = sem("k_sb")
        self.v_sb = sem("v_sb")
        self.kw_sb = sem("kw_sb")
        self.arg_done = sem("arg_done")
        self.exp_done = sem("exp_done")
        self.st_done = sem("st_done")
        self.num_sb = sem("num_sb")
        self.qs_done = sem("qs_done")
        self.nst_ready = sem("nst_ready")
        self.n1_ready = sem("n1_ready")
        self.n1_sb = sem("n1_sb")
        self.st_dec = sem("st_dec")
        self.st_new = sem("st_new")
        self.cq_half = sem("cq_half")
        self.cq_sb = sem("cq_sb")
        self.xdt_ready = sem("xdt_ready")
        self.xw_ready = sem("xw_ready")
        self.bcs_ps = sem("bcs_ps")
        self.rows_out = sem("rows_out")
        self.mt_sb = sem("mt_sb")
        self.den_sb = sem("den_sb")
        self.za_done = sem("za_done")
        self.yz_ready = sem("yz_ready")
        self.bcs_ready = sem("bcs_ready")
        self.bt_ready = sem("bt_ready")
        self.gt_ready = sem("gt_ready")
        self.sst_ready = sem("sst_ready")
        self.s_y = sem("s_y")
        self.sq_done = sem("sq_done")
        self.rden_ready = sem("rden_ready")
        self.sc_exp = sem("sc_exp")
        self.scale_ready = sem("scale_ready")
        self.num_ready = sem("num_ready")
        self.ysc_exp = sem("ysc_exp")
        self.yb_norm = sem("yb_norm")
        self.h_ready = sem("h_ready")
        self.h_rstd = sem("h_rstd")
        self.xn2_ready = sem("xn2_ready")
        self.xt_ready = sem("xt_ready")
        self.lx_ready = sem("lx_ready")
        self.p1_exp = sem("p1_exp")
        self.router = sem("router")
        self.rank_ready = sem("rank_ready")
        self.rounds_ready = sem("rounds_ready")
        self.p_ready = sem("p_ready")
        self.xg_ready = sem("xg_ready")
        self.pt_ready = sem("pt_ready")
        self.xs_ready = sem("xs_ready")
        self.silu_done = sem("silu_done")
        self.a_ready = sem("a_ready")
        self.ht_sb = sem("ht_sb")
        self.yg_done = sem("yg_done")
        self.h_add = sem("h_add")
        self.f_rstd = sem("f_rstd")
        self.y_ready = sem("y_ready")
        self.out_conv = sem("out_conv")
        self.out_mn = sem("out_mn")
        self.out_S = sem("out_S")
        self.out_y = sem("out_y")


def program(nc, x_prompt, x_sample, C0, n0, m0, conv_a0, S0, conv_b0, meta, norm_mix, w_in,
            conv_a_w, conv_a_b, w_q, w_k, w_v, b_i, b_f, norm_a, conv_b_w, conv_b_b, dt_bias, a_log,
            d_skip, norm_b, w_out, norm_ffn, w_r1, b_r1, w_r2, b_r2, w_gate, w_up, w_down, norm_final,
            y_p, y_s, p_C, p_n, p_m, p_ca, p_S, p_cb, s_C, s_n, s_m, s_ca, s_S, s_cb, rows_dram, heads_dram):
    ctx = ExitStack()
    with ctx:
        def sb(name, shape, dt=F32):
            return ctx.enter_context(nc.sbuf_tensor(name, shape, dt))

        def sem(name):
            return ctx.enter_context(nc.semaphore(name))

        def carve(t, start, *dims):
            n = 1
            for d in dims:
                n *= d
            v = t[:, start:start + n]
            if len(dims) == 2:
                v = v.rearrange("p (a b) -> p a b", b=dims[1])
            if len(dims) == 3:
                v = v.rearrange("p (a b c) -> p a b c", b=dims[1], c=dims[2])
            return v

        ring = sb("ring", [P, 6 * SLOT])
        tmp0 = 3 * SLOT
        XDT = carve(ring, tmp0, 3, D)
        XWT = carve(ring, tmp0 + 3072, 3, D)
        CPREV = carve(ring, tmp0, (KD + CB_T) * P)
        LCT = carve(ring, tmp0 + 3072, (KD + CB_T) * P)
        kw = carve(ring, tmp0 + 6144, 2, 3, P)
        vv = carve(ring, tmp0 + 6912, 2, 3, P + 1)
        SST = carve(ring, tmp0 + 6144, 2, 512)
        BCS = ring[0:NB, tmp0 + 5632:tmp0 + 6144]
        assert (KD + CB_T) * P == 5632 - 3072 and D <= 2 * 3 * (2 * P + 1)
        TMPS = carve(ring, tmp0 + 7686, D)
        BB = carve(ring, tmp0, 2, 512)
        VB = [carve(ring, tmp0 + 6144, D), TMPS]
        rows0 = tmp0 + 8710

        def rowt(i, w=T):
            return ring[:, rows0 + i * T:rows0 + i * T + w]

        ROWB = [rowt(i, NP) for i in range(4)]
        XR = ring[:, rows0:rows0 + 2 * T]
        EX = ring[:, rows0 + 2 * T:rows0 + 4 * T]
        SS = ring[:, rows0 + 4 * T:rows0 + 6 * T]
        HN = ring[:, rows0 + 6 * T:rows0 + 8 * T]
        RI, AC, AR = rowt(8), rowt(9), rowt(10)
        MX = rowt(11)
        WSR, EDR = rowt(2), rowt(3)
        BN, MROW = rowt(4), rowt(5)
        DEN, SCL, YSC = rowt(6), rowt(7), rowt(8)[32:32 + NG]
        assert rows0 + 12 * T <= 6 * SLOT

        h_tok = sb("h_tok", [P, 3, D])
        stage = h_tok
        xnf = sb("xn", [P, 3 * D])
        xn = carve(xnf, 0, 3, D)
        qT = carve(xnf, 0, 2, QT)
        kT = carve(xnf, 2 * QT, 2, QT)
        GT = carve(xnf, 4 * QT, 2, BLKW)
        BT = carve(xnf, 4 * QT + 2 * BLKW, 3, NG * NST)
        SDEN = 4 * QT + 2 * BLKW + 3 * NG * NST
        assert SDEN <= 3 * D

        arena = sb("arena", [P, 15304])
        CA = carve(arena, 0, KD, CW)
        CBX = carve(arena, 2456, CB_T, CW)
        ZA = carve(arena, 6140, KD, T)
        ZB = carve(arena, 8380, KD, T)
        hT = carve(arena, 10620, KD, T)
        NUM = hT
        SQA = carve(arena, 0, KD, T)
        MT = carve(arena, 2456, KD, NOUT)
        XC = carve(arena, 12860, KD, W)
        YB = carve(arena, 12860, KD, T)
        XG = carve(arena, 0, KD, EG * P)
        YN = XG.rearrange("p k n -> p (k n)")[:, 0:3 * D].rearrange("p (i d) -> p i d", d=D)
        YG = carve(arena, 4096, EG, D)
        XT = carve(arena, 4096, KD, NOUT)
        PT = carve(arena, 8192, EG, NOUT)
        PG = carve(arena, 9248, 3, EG * P)
        XS = carve(arena, 10784, KD, P)
        SG = carve(arena, 11808, D)
        AH = carve(arena, 12832, D)
        HT = carve(arena, 13856, KD, P)

        shared = sb("shared", [P, 1216])
        NF = carve(shared, 0, D)
        CY = carve(shared, 0, 2, W)
        CSG = carve(shared, 2 * W, 2, W)
        ARG = carve(shared, 0, 2, BLKW)

        ident = sb("ident", [P, P])
        mask = sb("mask", [P, NP])
        before = sb("before", [P, P])
        ones = sb("ones", [P, P])
        iota_i = sb("iota_i", [P, P], I32)
        iota = sb("iota", [P, P])
        strip = sb("strip", [P, 15])
        PR = sb("PR", [84, 2, P])
        PV = sb("PV", [P, 132])
        c16 = sb("c16", [HB, 8])
        WG = sb("WG", [P, KD, 80])
        LC = sb("LC", [P, KD + CB_T, LAST])
        TM = sb("TM", [P, 3, 64])
        VS = sb("VS", [NB, D])
        RS = sb("RS", [HA, 16])
        RX = sb("RX", [HB, 17])
        BCM = sb("BCM", [P, HA, 16])
        XE = sb("XE", [P, KD, 17])
        m0s = sb("m0s", [HA, NB])
        N0 = sb("N0", [64, P])
        N1 = sb("N1", [P, 64])
        NT = sb("NT", [P, 64])
        QN = sb("QN", [P, 64])
        N1T = sb("N1T", [64, P])
        QS = sb("QS", [P, HA, NB])
        QZ = carve(WG[:, :, :].rearrange("p k n -> p (k n)"), 0, HA, NB, HA)
        KS = sb("KS", [P, HA, NB])
        XDS = sb("XDS", [P, KD, NB])
        YS = sb("YS", [P, KD, NB])
        CST = sb("CST", [P, 2, P + 1])
        NSTt = sb("NSTt", [P, HA])
        NSTo = sb("NSTo", [HA, P])
        ENM = sb("ENM", [HB, T])
        YS2 = sb("YS2", [P, KD, NB])
        st3 = sb("st3", [P, 8])
        wr = sb("wr", [P, KD, 20])
        br = sb("br", [1, 20])
        epst = sb("epst", [P, 2])

        bank = [ctx.enter_context(nc.psum_tensor(f"bank{i}", [P, 512], F32)) for i in range(8)]

        L = sb("L", [P, 3, 20])
        LX = sb("LX", [P, 3, 4])
        M1 = sb("M1", [P, 3, 4])
        K1 = sb("K1", [P, 3, 4])
        L2 = sb("L2", [P, 3, 4])
        O1 = sb("O1", [P, 3, 4])
        O2 = sb("O2", [P, 3, 4])
        LP = sb("LP", [P, 3, 4, 4])
        r1 = sb("r1", [P, 3, 8])
        GATE = sb("GATE", [P, 3, 4])
        rank = sb("rank", [P, 3, 4])
        order = sb("order", [P, 4])
        GS = sb("GS", [P, EG * EPG])
        cnt = sb("cnt", [P, 8])
        rounds = sb("rounds", [P, 1], I32)

        s = Signals(sem)
        x_in = [sem(f"x_in{i}") for i in range(3)]
        u_free = [sem(f"u_free{b}") for b in range(4)]
        y_free = [sem(f"y_free{b}") for b in range(2)]
        arrived = [sem(f"arrived{i}") for i in range(6)]
        st_in = [sem(f"st_in{i}") for i in range(3)]
        row_in = [sem(f"row_in{i}") for i in range(4)]
        bb_in = [sem(f"bb_in{i}") for i in range(2)]
        vb_in = [sem(f"vb_in{i}") for i in range(2)]
        st_out = [sem(f"st_out{i}") for i in range(3)]
        cst_out = [sem(f"cst_out{i}") for i in range(2)]
        dch, ach, gch = sem("dve_chain"), sem("act_chain"), sem("pool_chain")

        slot = [ring[:, i * SLOT:(i + 1) * SLOT] for i in range(6)]

        def slot_k(i, n):
            return slot[i].rearrange("p (k n) -> p k n", n=n)

        def unit_at(u):
            return u % MR, 16 * (u // MR + 1) + (32 if u % MR == U_QKV % MR and u >= U_QKV else 0)

        mix_in = [0] * 6
        for u in range(N_MIX):
            mix_in[u % MR] += 48 if u == U_QKV else 16

        UT = [("xa", c, c // 4, (c % 4) * P) for c in range(KD)]
        UT += [("xbc", c, 2 + c // 4, (c % 4) * P) for c in range(CB_T)]
        UT += [("za", c, 5 + c // 4, (c % 4) * P) for c in range(KD)]
        UT += [("zb", c, 7 + c // 4, (c % 4) * P) for c in range(KD)]
        NCONV = KD + CB_T

        def col(t, n):
            return t[:, n:n + 1].to_broadcast([t.shape[0], P])

        def bc_last(v, n):
            return v.unsqueeze(len(v.shape)).to_broadcast(list(v.shape) + [n])

        def smp(v):
            return v[:, SC0:SC0 + TAPS * (NB - 1) + 1:TAPS]

        def rounds_of(eng):
            eng.wait_ge(s.rounds_ready, 1)
            return eng.value_load(rounds[0:1, 0:1], min_val=1, max_val=3)

        def head_state_out(pool, h):
            pool.wait_ge(s.num_sb, h + 1)
            nc.gpsimd.tensor_copy(NSTt[:, h:h + 1], CST[:, h % 2, P:P + 1]).then_inc(s.nst_ready, 1)
            pool.dma_start(p_C[0, 0, h], CST[:, h % 2, 0:P]).then_inc(cst_out[h % 2], 16)

        def state_buf(n):
            return stage[:, n % 3, :].rearrange("p (a b) -> p a b", b=P)

        def state_dram(n, old):
            if n >= NB:
                t = C0 if old else s_C
                return t[0, n - NB].rearrange("h d e -> d h e")
            t = S0 if old else s_S
            return t[0, n].rearrange("h q n -> (h q) n").rearrange("(c p) n -> p c n", p=P)

        def state_free(pool, n):
            pool.wait_ge(st_out[n % 3], 16 * (n // 3 + 1))
            if n < NB:
                pool.wait_ge(s.s_y, n + 1)
            else:
                pool.wait_ge(s.cq_ps, n - NB + 1)

        def turn_hidden(act, x2, j):
            act.wait_ge(s.ft_ps, x2 + (j + 1))
            nc.scalar.activation(HT[:, 4 * j:4 * j + 4, :], bank[4 + j][:, :].rearrange("p (k n) -> p k n", n=P),
                                 ACT.Copy).then_inc(s.ht_sb, 1)

        def ssd_out(dve, c):
            dve.wait_ge(s.y_ps, 2 * c + 2)
            nc.vector.scalar_tensor_tensor(out=YB[:, c, 0:NP], in0=CBX[:, c, 0:NP], scalar=XE[:, c, 16:17],
                                           in1=bank[6 if c % 2 == 0 else 0][:, 0:NP], op0=ALU.mult, op1=ALU.add)\
                .then_inc(y_free[c % 2], 1)

        ctx.enter_context(nc.allow_non_contiguous_dma(reason="small [sample, head] tables, transposed"))
        block = ctx.enter_context(nc.Block())

        @block.sync
        def _(sp):
            def mixer_unit(u):
                if u >= MR:
                    before_u = u - MR
                    if before_u < U_QKV:
                        sp.wait_ge(s.u_ps, 3 + 4 * (before_u + 1))
                    elif before_u == U_QKV:
                        sp.wait_ge(s.vt_ps, HA)
                    else:
                        sp.wait_ge(s.wo_unit, before_u - U_QKV)
                i = u % MR
                if u < U_QKV:
                    src = w_in[0, :, WIN[u]:WIN[u] + 512].rearrange("(k p) n -> p k n", p=P)
                    sp.dma_start(slot_k(i, 512), src).then_inc(arrived[i], 16)
                elif u == U_QKV:
                    for j, wt in enumerate((w_q, w_k, w_v)):
                        dst = slot[i][:, j * D:(j + 1) * D].rearrange("p (h e) -> p h e", e=DH)
                        sp.dma_start(dst, wt[0].rearrange("h d e -> d h e")).then_inc(arrived[i], 16)
                else:
                    r0 = 512 * (u - U_OUT)
                    src = w_out[0, r0:r0 + 512, :].rearrange("(k p) n -> p k n", p=P)
                    sp.dma_start(slot_k(i, D), src).then_inc(arrived[i], 16)

            sp.dma_start(h_tok[0:P, 0, :], x_prompt[0, 0:P, :]).then_inc(x_in[0], 16)
            sp.dma_start(h_tok[0:P, 1, :], x_prompt[0, P:SEQ, :]).then_inc(x_in[1], 16)
            sp.dma_start(h_tok[0:NB, 2, :], x_sample[:, 0, :]).then_inc(x_in[2], 16)
            sp.dma_start(h_tok[NB:NB + META, 2, :], meta).then_inc(x_in[2], 16)
            for c0, o, n in ((0, O_I, HA), (32, O_F, HA), (64, O_DT, HB)):
                sp.dma_start(WG[:, :, c0:c0 + n], w_in[0, :, o:o + n].rearrange("(k p) n -> p k n", p=P)).then_inc(s.gates_in, 16)
            sp.wait_ge(s.params_in, 16 * 8)
            mixer_unit(0)
            sp.wait_ge(s.prev_in, 32)
            sp.wait_ge(s.late_in, 16 * 11)
            for u in range(1, MR):
                mixer_unit(u)
            sp.wait_ge(s.xn_ready, 3)
            for n in range(3):
                sp.dma_start(state_buf(n), state_dram(n, True)).then_inc(st_in[n % 3], 16)
            for u in range(MR, U_OUT + 2):
                mixer_unit(u)

            def state_step(n):
                if n >= 1:
                    sp.wait_ge(s.st_new, n)
                    sp.dma_start(state_dram(n - 1, False), state_buf(n - 1)).then_inc(st_out[(n - 1) % 3], 16)
                if n >= 2 and n + 1 < 2 * NB:
                    state_free(sp, n - 2)
                    sp.dma_start(state_buf(n + 1), state_dram(n + 1, True)).then_inc(st_in[(n + 1) % 3], 16)

            sp.wait_ge(s.rows_pre, 1)
            sp.dma_start(heads_dram[0:HA, :], MX[0:HA, 0:NP]).then_inc(s.rows_out, 16)
            sp.dma_start(heads_dram[HA:, :], AR[0:HB, 0:NP]).then_inc(s.rows_out, 16)

            def row_load(n):
                if n < HA + HB:
                    if n >= 4:
                        sp.wait_ge(s.arg_done, n - 3)
                    sp.dma_start(ROWB[n % 4], heads_dram[n:n + 1, :].to_broadcast([P, NP])).then_inc(row_in[n % 4], 16)

            sp.wait_ge(s.rows_out, 32)
            sp.wait_ge(s.tm_ps, 1)
            sp.wait_ge(s.rows_exp, 1)
            for n in range(4):
                row_load(n)
            sp.wait_ge(s.bcs_ready, 1)
            sp.dma_start(rows_dram[:, 0:512], BCS).then_inc(s.rows_out, 16)
            for b in range(NB):
                if b == 0:
                    sp.wait_ge(s.rows_out, 48)
                if b >= 2:
                    sp.wait_ge(s.s_y, b - 1)
                sp.dma_start(BB[:, b % 2, :], rows_dram[b:b + 1, 0:512].to_broadcast([P, 512])).then_inc(bb_in[b % 2], 16)
                state_step(b)
                row_load(b + 4)
            mixer_unit(U_OUT + 2)
            sp.wait_ge(s.v_sb, HA)
            sp.dma_start(rows_dram[:, 512:512 + D], VS[:, :]).then_inc(s.rows_out, 16)
            for b in range(NB):
                if b == 0:
                    sp.wait_ge(s.rows_out, 64)
                    sp.wait_ge(s.nc_ps, HA)
                    sp.wait_ge(s.xdt_ready, 1)
                if b >= 2:
                    sp.wait_ge(s.st_new, NB + b - 1)
                sp.dma_start(VB[b % 2], rows_dram[b:b + 1, 512:512 + D].to_broadcast([P, D])).then_inc(vb_in[b % 2], 16)
                state_step(NB + b)
                row_load(HA + 4 + 2 * b)
                row_load(HA + 5 + 2 * b)
            state_step(2 * NB)
            mixer_unit(U_OUT + 3)

            gate_v = w_gate[0].rearrange("e (k p) n -> e p k n", p=P)
            up_v = w_up[0].rearrange("e (k p) n -> e p k n", p=P)
            down_v = w_down[0].rearrange("e (k p) n -> e p k n", p=P)

            def expert_units(e, free):
                for c in range(6):
                    sp.wait_ge(*free[c])
                    i = EXP_SLOT[c]
                    if c < 4:
                        v = gate_v if c % 2 == 0 else up_v
                        src = v[bass.ds(e, 1), :, :, (c // 2) * 512:(c // 2 + 1) * 512]
                        dst = slot_k(i, 512)
                    else:
                        src = down_v[bass.ds(e, 1), :, (c - 4) * 4:(c - 3) * 4, :]
                        dst = slot_k(i, D)
                    src = src.rearrange("o p k n -> (o p) k n")
                    sp.dma_start(dst, src).then_inc(arrived[i], 16)

            def read_by(x):
                return [(s.gate_ps, x * 2 - 1), (s.gu_ps, x * 2), (s.gate_ps, x * 2), (s.gu_ps, x * 2 + 1),
                        (s.down_ps, x), (s.d_ps, x)]

            sp.wait_ge(s.out_S, 16 * 2)
            expert_units(0, [(s.wo_unit, n) for n in EXP_FREE] + [(s.mo_ps, KD)])
            with sp.Fori(1, EG * EPG) as e:
                expert_units(e, read_by(e))
            again = rounds_of(sp)
            with sp.If(again > 1):
                with sp.Fori(1, again) as r:
                    with sp.Fori(0, EG * EPG) as e:
                        expert_units(e, read_by(r * (EG * EPG) + e))
            sp.wait_ge(s.out_y, 16 * 3)
            sp.wait_ge(s.out_conv, 16 * 6)
            sp.wait_ge(s.out_mn, 16 * 4)
            sp.wait_ge(s.out_S, 16 * 2)
            for i in range(2):
                sp.wait_ge(cst_out[i], 16 * 4)
            for i in range(3):
                sp.wait_ge(st_out[i], 16 * len(range(i, 2 * NB, 3)))

        @block.gpsimd
        def _(pool):
            g = nc.gpsimd
            links = [0]

            def link(ins):
                links[0] += 1
                ins.then_inc(gch, 1)
                pool.wait_ge(gch, links[0])

            g.memset(st3[:], 0.0)
            g.memset(epst[:, 0:1], EPS)
            link(g.memset(epst[:, 1:2], 1.0))
            g.memset(ones[:], 1.0)
            g.memset(ident[:], 0.0)
            g.memset(mask[:], 0.0)
            g.memset(strip[:], 0.0)
            g.memset(WG[:, :, HA:32], 0.0)
            g.memset(WG[:, :, 32 + HA:64], 0.0)
            g.iota(iota_i[:], pattern=[[1, P]], base=0, channel_multiplier=0)
            link(g.memset(NSTt[:], 0.0))
            g.memset(strip[:, 7:8], 1.0)
            g.affine_select(out=ident[:], in_=ident[:], compare_op=ALU.not_equal, fill=1.0, base=0,
                            pattern=[[-1, P]], channel_multiplier=1)
            g.affine_select(out=mask[:], in_=mask[:], compare_op=ALU.is_ge, fill=BIG, base=0,
                            pattern=[[1, NP]], channel_multiplier=-1)
            g.affine_select(out=before[:], in_=ones[:], compare_op=ALU.is_gt, fill=0.0, base=0,
                            pattern=[[1, P]], channel_multiplier=-1)
            g.tensor_copy(iota[:], iota_i[:])
            for j in range(4):
                g.memset(order[:, j:j + 1], 4.0 - j)
            g.memset(CA[:, :, 0:PAD], 0.0)
            g.memset(CBX[:, :, 0:PAD], 0.0)
            g.memset(vv[:, :, :, P:P + 1].rearrange("p a b c -> p (a b) c"), 1.0)
            g.memset(XR[0:HB, T:2 * T], 0.0)
            g.memset(ENM[0:HB, :], 1.0)
            g.memset(L[:], 0.0).then_inc(s.consts, 1)

            pool.dma_start(CPREV[0:PAD * NB, 0:D], conv_a0[0].rearrange("b j c -> (b j) c")).then_inc(s.prev_in, 16)
            pool.dma_start(CPREV[0:PAD * NB, D:], conv_b0[0].rearrange("b j c -> (b j) c")).then_inc(s.prev_in, 16)
            for j, (v, n) in enumerate(((b_i, HA), (b_f, HA), (dt_bias, HB), (a_log, HB), (d_skip, HB))):
                pool.dma_start(c16[0:n, j:j + 1], v[0].unsqueeze(1)).then_inc(s.late_in, 16)
            pool.dma_start(m0s[:, :], m0[0].rearrange("b h -> h b")).then_inc(s.late_in, 16)
            pool.dma_start(N0[:, :], n0[0].rearrange("b h d -> (b h) d")).then_inc(s.late_in, 16)
            pool.dma_start(wr[:, :, 0:4], w_r1[0].rearrange("(k p) g -> p k g", p=P)).then_inc(s.late_in, 16)
            pool.dma_start(wr[:, :, 4:20], w_r2[0].rearrange("(k p) g e -> p k (g e)", p=P)).then_inc(s.late_in, 16)
            pool.dma_start(br[:, 0:4], b_r1).then_inc(s.late_in, 16)
            pool.dma_start(br[:, 4:20], b_r2.rearrange("o g e -> o (g e)")).then_inc(s.late_in, 16)

            pool.dma_start(s_ca[0, :, 0:2, :], conv_a0[0, :, 1:3, :]).then_inc(s.out_conv, 16)
            pool.dma_start(s_cb[0, :, 0:2, :], conv_b0[0, :, 1:3, :]).then_inc(s.out_conv, 16)
            pool.wait_ge(s.rows_pre, 1)
            pool.dma_start(p_m[0, 0, :].unsqueeze(1), MROW[0:HA, NP - 1:NP]).then_inc(s.out_mn, 16)
            pool.dma_start(s_m[0].rearrange("b h -> h b"), MROW[0:HA, NP:T]).then_inc(s.out_mn, 16)
            pool.wait_ge(s.lct_sb, 5)
            pool.dma_start(p_ca[0, 0], LCT[0:PAD, 0:D]).then_inc(s.out_conv, 16)
            pool.dma_start(p_cb[0, 0], LCT[0:PAD, D:]).then_inc(s.out_conv, 16)
            pool.dma_start(s_ca[0, :, 2, :], LCT[PAD:LAST, 0:D]).then_inc(s.out_conv, 16)
            pool.dma_start(s_cb[0, :, 2, :], LCT[PAD:LAST, D:]).then_inc(s.out_conv, 16)

            def decay_state(n):
                pool.wait_ge(st_in[n % 3], 16 * (n // 3 + 1))
                if n == 0:
                    pool.wait_ge(s.bcm_ready, 1)
                w = XE[:, :, n] if n < NB else BCM[:, :, n - NB]
                ins = g.tensor_tensor(state_buf(n), state_buf(n), bc_last(w, P), ALU.mult)
                if n >= NB:
                    b = n - NB
                    if b == 0:
                        pool.wait_ge(s.n1_ready, 1)
                    pool.wait_ge(vb_in[b % 2], 16 * (b // 2 + 1))
                    kv = VB[b % 2].rearrange("p (a b) -> p a b", b=P)
                    ins = g.tensor_tensor(kv, kv, bc_last(KS[:, :, b], P), ALU.mult)
                ins.then_inc(s.st_dec, 1)

            pool.wait_ge(s.u_ps, 3)
            link(g.memset(QZ, 0.0))
            for h in range(HA):
                decay_state(h)
                pool.wait_ge(s.q_sb, h + 1)
                pool.wait_ge(s.k_sb, h + 1)
                g.tensor_copy(QS[:, h, :], smp(qT[:, h % 2, :]))
                g.tensor_copy(QZ[:, h, :, h], smp(qT[:, h % 2, :]))
                g.tensor_copy(KS[:, h, :], smp(kT[:, h % 2, :])).then_inc(s.qs_done, 1)
                if h > 0:
                    head_state_out(pool, h - 1)
            head_state_out(pool, HA - 1)
            pool.wait_ge(s.out_conv, 16 * 6)
            for i, (_t0, m) in enumerate(S_TILES):
                pool.wait_ge(s.xdt_ready, 2 * (i + 1))
                g.tensor_tensor(XWT[0:m, i, :].rearrange("p (h q) -> p h q", q=HD),
                                XDT[0:m, i, :].rearrange("p (h q) -> p h q", q=HD),
                                bc_last(TM[0:m, i, 48:64], HD), ALU.mult).then_inc(s.xw_ready, 1)
            for n in range(NB, 2 * NB):
                decay_state(n)
                h = n - NB - 1
                if h < 0:
                    continue
                pool.wait_ge(s.sq_done, h + 1)
                g.tensor_tensor(NUM[:, h, 0:NP], NUM[:, h, 0:NP], ZA[:, h, 0:NP], ALU.mult).then_inc(s.za_done, 1)
            pool.wait_ge(s.sq_done, HA)
            g.tensor_tensor(NUM[:, HA - 1, 0:NP], NUM[:, HA - 1, 0:NP], ZA[:, HA - 1, 0:NP], ALU.mult).then_inc(s.za_done, 1)
            pool.wait_ge(s.n1_sb, 1)
            pool.dma_start(p_n[0, 0], NSTo[:, :]).then_inc(s.out_mn, 16)
            pool.dma_start(s_n[0].rearrange("b h d -> (b h) d"), N1T[:, :]).then_inc(s.out_mn, 16)
            for half in range(2):
                pool.wait_ge(s.sst_ready, half + 1)
                dst = p_S[0, 0].rearrange("h q n -> (h q) n").rearrange("(c p) n -> p c n", p=P)
                pool.dma_start(dst[:, 4 * half:4 * half + 4, :],
                               SST[:, half, :].rearrange("p (c n) -> p c n", n=NST)).then_inc(s.out_S, 16)
            for n in range(2 * NB - 3, 2 * NB):
                state_free(pool, n)
            for i, (t0, m) in enumerate(TOK):
                src = x_prompt[0, t0:t0 + m, :] if i < 2 else x_sample[:, 0, :]
                pool.dma_start(h_tok[0:m, i, :], src).then_inc(s.x_again, 16)
            pool.wait_ge(s.h_ready, 1)
            pool.dma_start(NF, norm_final.rearrange("(o n) -> o n", o=1).to_broadcast([P, D]))\
                .then_inc(s.nf_in, 16)

        @block.scalar
        def _(act):
            a = nc.scalar
            links = [0]

            def link(ins):
                links[0] += 1
                ins.then_inc(ach, 1)
                act.wait_ge(ach, links[0])

            def load_ln_table():
                link(a.activation(st3[:, 3:4], epst[:, 1:2], ACT.Ln))

            def root_of_mean(done):
                link(a.activation(st3[:, 4:7], st3[:, 0:3], ACT.Ln, bias=epst[:, 0:1], scale=1.0 / D))
                a.activation(st3[:, 4:7], st3[:, 4:7], ACT.Exp, scale=-0.5).then_inc(done, 1)

            act.wait_ge(gch, 1)
            load_ln_table()
            rows8 = "(k p) -> k p"
            act.dma_start(PR[V_NMIX:V_NMIX + 8, 0, :], norm_mix[0].rearrange(rows8, p=P)).then_inc(s.params_in, 16)
            act.dma_start(PR[V_CAW:V_CAW + 32, 0, :], conv_a_w[0].rearrange("j (k p) -> (j k) p", p=P)).then_inc(s.params_in, 16)
            act.dma_start(PR[V_CAB:V_CAB + 8, 0, :], conv_a_b[0].rearrange(rows8, p=P)).then_inc(s.params_in, 16)
            act.dma_start(PR[V_NA:V_NA + 8, 0, :], norm_a[0]).then_inc(s.params_in, 16)
            act.dma_start(PR[V_NB:V_NB + 8, 0, :], norm_b[0].rearrange(rows8, p=P)).then_inc(s.params_in, 16)
            act.dma_start(PR[V_NFF:V_NFF + 8, 0, :], norm_ffn[0].rearrange(rows8, p=P)).then_inc(s.params_in, 16)
            act.dma_start(PR[V_CBB:V_CBB + CB_T, 0, :], conv_b_b[0].rearrange(rows8, p=P)).then_inc(s.params_in, 16)
            act.dma_start(PR[0:4 * CB_T, 1, :], conv_b_w[0].rearrange("j (k p) -> (j k) p", p=P)).then_inc(s.params_in, 16)

            for i, m in enumerate((P, P, NB + META)):
                act.wait_ge(x_in[i], 16 if i < 2 else 32)
                link(a.activation(xn[0:m, i, :], h_tok[0:m, i, :], ACT.Square, accum_out=st3[0:m, i:i + 1]))
            root_of_mean(s.rstd_ready)

            act.wait_ge(s.x_abs, 1)
            a.activation(EX[0:HB, :], HN[0:HB, :], ACT.Exp, scale=-1.0).then_inc(s.x_exp, 1)
            a.activation(c16[:, 5:6], c16[:, 3:4], ACT.Exp).then_inc(s.x_exp, 1)
            def sigmoid_of_conv(n):
                act.wait_ge(s.conv_y, n + 1)
                if n >= 2:
                    act.wait_ge(s.conv_done, n - 1)
                a.activation(CSG[:, n % 2, :], CY[:, n % 2, :], ACT.Sigmoid).then_inc(s.conv_sig, 1)

            def row_exps():
                act.wait_ge(s.rows_pre, 1)
                a.activation(WSR[0:HA, 0:NP], AC[0:HA, 0:NP], ACT.Exp, bias=c16[0:HA, 6:7])
                a.activation(WSR[0:HA, NP:T], WSR[0:HA, NP:T], ACT.Exp)
                a.activation(EDR[0:HB, 0:NP], AR[0:HB, 0:NP], ACT.Exp, bias=c16[:, 7:8])
                a.activation(RX[:, 0:NB], AR[0:HB, NP:T], ACT.Exp, scale=-1.0)
                a.activation(RS[:, :], RS[:, :], ACT.Exp)
                a.activation(ENM[0:HA, :], MROW[0:HA, :], ACT.Exp, scale=-1.0).then_inc(s.rows_exp, 1)

            lag = 6
            for n, (kind, c, _u, _o) in enumerate(UT):
                b = bank[(n + 3) % 4]
                act.wait_ge(s.u_ps, n + 4)
                if kind in ("xa", "xbc"):
                    dst = CA if kind == "xa" else CBX
                    a.activation(dst[:, c, PAD:PAD + NP], b[:, 0:NP], ACT.Copy)
                    a.activation(dst[:, c, SC0 + PAD:SC0 + PAD + TAPS * (NB - 1) + 1:TAPS], b[:, NP:T],
                                 ACT.Copy).then_inc(s.lc_ready, 1)
                    a.activation(LC[:, n, :], b[:, NP - PAD:T], ACT.Copy).then_inc(u_free[(n + 3) % 4], 1)
                    if n == lag - 1:
                        row_exps()
                    if n >= lag:
                        sigmoid_of_conv(n - lag)
                else:
                    if n == NCONV:
                        for n_ in range(NCONV - lag, NCONV):
                            sigmoid_of_conv(n_)
                    if kind == "za":
                        a.activation(ZA[:, c, :], b[:, 0:T], ACT.Sigmoid).then_inc(u_free[(n + 3) % 4], 1)
                    else:
                        a.activation(ZB[:, c, :], b[:, 0:T], ACT.Sigmoid).then_inc(s.z_sig, 1)
            for q in range(5):
                act.wait_ge(s.lct_ps, q + 1)
                a.activation(LCT[0:LAST, q * 512:(q + 1) * 512], bank[6 + q % 2][0:LAST, :], ACT.Copy).then_inc(s.lct_sb, 1)

            act.wait_ge(s.bcs_ps, 1)
            a.activation(BCS, bank[7][0:NB, :], ACT.Copy).then_inc(s.bcs_ready, 1)

            act.wait_ge(s.tm_ready, 1)
            act.wait_ge(s.conv_done, NCONV)
            def head_in(h):
                if h >= 2:
                    act.wait_ge(s.nc_ps, h - 1)
                    act.wait_ge(s.qs_done, h - 1)
                act.wait_ge(s.q_ps, h + 1)
                a.activation(qT[:, h % 2, :], bank[0][:, 0:W], ACT.Copy).then_inc(s.q_sb, 1)
                act.wait_ge(s.k_ps, h + 1)
                a.activation(kT[:, h % 2, :], bank[1][:, 0:W], ACT.Copy, scale=DH ** -0.5).then_inc(s.k_sb, 1)
                act.wait_ge(s.kt_ps, h + 1)
                for j, (_t0, m) in enumerate(S_TILES):
                    last = a.activation(kw[0:m, h % 2, j, :], bank[2][0:m, j * P:(j + 1) * P], ACT.Copy,
                                        scale=TM[0:m, j, 8 + h:9 + h])
                last.then_inc(s.kw_sb, 1)
                act.wait_ge(s.vt_ps, h + 1)
                a.activation(vv[:, h % 2, 0:2, 0:P], bank[3][:, 0:256].rearrange("p (a b) -> p a b", b=P), ACT.Copy)
                a.activation(vv[0:16, h % 2, 2, 0:P], bank[3][0:16, 256:384], ACT.Copy)
                a.activation(VS[:, h * P:(h + 1) * P], bank[3][0:NB, 384:512], ACT.Copy).then_inc(s.v_sb, 1)

            def head_exp(h):
                act.wait_ge(s.arg_done, h + 1)
                a.activation(ARG[:, h % 2, :], ARG[:, h % 2, :], ACT.Exp, scale=-1.0).then_inc(s.exp_done, 1)

            def head_out(h):
                act.wait_ge(s.nc_ps, h + 1)
                if h >= 2:
                    act.wait_ge(cst_out[h % 2], 16 * (h // 2))
                    act.wait_ge(s.nst_ready, h - 1)
                a.activation(NUM[:, h, 0:NP], bank[6][:, 0:NP], ACT.Copy)
                a.activation(CST[:, h % 2, :], bank[6][:, NP:NP + P + 1], ACT.Copy).then_inc(s.num_sb, 1)

            head_in(0)
            for h in range(HA):
                head_exp(h)
                if h + 1 < HA:
                    head_in(h + 1)
                head_out(h)

            for h in range(HA):
                act.wait_ge(s.num_sb, h + 1)
                a.activation(SQA[:, h, 0:NP], NUM[:, h, 0:NP], ACT.Square).then_inc(s.sq_done, 1)

            act.wait_ge(s.bt_ps, 1)
            a.activation(BT[:, 0:2, :], bank[0][:, :].rearrange("p (a b) -> p a b", b=256), ACT.Copy)
            a.activation(BT[0:16, 2, :], bank[1][0:16, 0:256], ACT.Copy).then_inc(s.bt_ready, 1)
            for j in range(NG):
                act.wait_ge(s.gt_ps, j + 1)
                a.activation(GT[:, j, 0:BLK[2]], bank[3 + j][:, 0:BLK[2]], ACT.Copy)
                a.activation(GT[0:16, j, BLK[2]:BLKW], bank[3 + j][0:16, BLK[2]:BLKW], ACT.Copy).then_inc(s.gt_ready, 1)
            def cq_rows(half):
                act.wait_ge(s.cq_ps, 4 * half + 4)
                if half == 0:
                    act.wait_ge(s.rows_out, 64)
                a.activation(VS[:, half * 512:(half + 1) * 512], bank[3][0:HA, :], ACT.Copy).then_inc(s.cq_half, 1)

            def y_square(c):
                act.wait_ge(s.yz_ready, c + 1)
                act.wait_ge(s.sq_ps, c + 1)
                a.activation(SQA[:, c, :], YB[:, c, :], ACT.Square).then_inc(s.sq_done, 1)

            for h in range(HB):
                act.wait_ge(s.arg_done, HA + h + 1)
                a.activation(ARG[:, h % 2, :], ARG[:, h % 2, :], ACT.Exp, scale=-1.0).then_inc(s.exp_done, 1)
                if h % 2 == 1 and h >= 3:
                    y_square((h - 3) // 2)
                if h == 9:
                    cq_rows(0)
            load_ln_table()
            y_square(KD - 1)
            cq_rows(1)
            act.wait_ge(s.cq_ps, NB + 1)
            a.activation(NUM[:, :, NP:T], bank[3][:, 0:64].rearrange("p (b h) -> p h b", h=HA), ACT.Copy)
            a.activation(QN[:], bank[3][:, 0:64], ACT.Square).then_inc(s.cq_sb, 1)

            act.wait_ge(s.sq_ps, HA + KD)
            a.activation(YSC, bank[7][32:32 + NG, 0:T], ACT.Ln, bias=epst[32:32 + NG, 0:1], scale=1.0 / (D // NG))
            for half in range(2):
                act.wait_ge(s.sst_ps, half + 1)
                a.activation(SST[:, half, :], bank[1 + half][:, :], ACT.Copy).then_inc(s.sst_ready, 1)
            act.wait_ge(s.rden_ready, 1)
            link(a.activation(SCL[0:HA, :], SCL[0:HA, :], ACT.Ln, bias=epst[0:HA, 0:1], scale=1.0 / DH))
            a.activation(YSC, YSC, ACT.Exp, scale=-0.5).then_inc(s.ysc_exp, 1)
            a.activation(SCL[0:HA, :], SCL[0:HA, :], ACT.Exp, scale=-0.5).then_inc(s.sc_exp, 1)

            for c in range(KD):
                act.wait_ge(s.mo_ps, c + 1)
                a.activation(MT[:, c, :], bank[c][:, 0:NOUT], ACT.Copy).then_inc(s.mt_sb, 1)

            load_ln_table()
            for i, (_t0, m) in enumerate(TOK):
                act.wait_ge(s.h_ready, i + 1)
                link(a.activation(xn[0:m, i, :], h_tok[0:m, i, :], ACT.Square, accum_out=st3[0:m, i:i + 1]))
            root_of_mean(s.h_rstd)
            act.wait_ge(s.h_rstd, 1)
            for i, (_t0, m) in enumerate(TOK):
                a.activation(xn[0:m, i, :], h_tok[0:m, i, :], ACT.Copy, scale=st3[0:m, 4 + i:5 + i]).then_inc(s.xn2_ready, 1)
            act.wait_ge(s.lx_ready, 1)
            a.activation(LX[:], LX[:], ACT.Exp).then_inc(s.p1_exp, 1)
            act.wait_ge(s.lx_ready, 2)
            a.activation(r1[:, :, 3:4], r1[:, :, 3:4], ACT.Exp).then_inc(s.p1_exp, 1)

            nr = rounds_of(act)
            with act.Fori(0, nr) as r:
                for k in range(1, KD, 2):
                    act.wait_ge(s.xg_ps, r * KD + (k + 1))
                    a.activation(XG[:, k, :], bank[(k + 5) % 8][:, :], ACT.Copy, scale=PV[:, V_NFF + k:V_NFF + k + 1])\
                        .then_inc(s.xg_ready, 1)
                with act.Fori(0, EG) as q:
                    act.wait_ge(s.gu_ps, (r * EG + q) * (2 * EPG) + 1)
                    act.wait_ge(s.xg_ready, r * KD + KD)
                    a.activation(XS[:], XG[:, :, bass.ds(q * P, P)], ACT.Copy).then_inc(s.xs_ready, 1)
                    with act.Fori(0, EPG) as e:
                        x2 = ((r * EG + q) * EPG + e) * 2
                        for j in range(2):
                            act.wait_ge(s.gate_ps, x2 + (j + 1))
                            a.activation(SG[:, j * 512:(j + 1) * 512], bank[2 * j][:, :], ACT.Silu)\
                                .then_inc(s.silu_done, 1)
                            if j == 1:
                                turn_hidden(act, x2, 0)
                        turn_hidden(act, x2, 1)

            load_ln_table()
            for i, (_t0, m) in enumerate(TOK):
                act.wait_ge(s.h_add, nr * 6 + 2 * i)
                link(a.activation(xn[0:m, i, :], h_tok[0:m, i, :], ACT.Square, accum_out=st3[0:m, i:i + 1]))
            root_of_mean(s.f_rstd)
            act.wait_ge(s.f_rstd, 1)
            act.wait_ge(s.y_ready, 1)
            link(a.activation(YN[:, 1, :], YN[:, 1, :], ACT.Copy, scale=st3[:, 5:6]))
            for n, i in enumerate((1, 0, 2)):
                t0, m = TOK[i]
                if n >= 1:
                    act.wait_ge(s.y_ready, n + 1)
                dst = y_p[0, t0:t0 + m, :] if i < 2 else y_s[:, 0, :]
                act.dma_start(dst, YN[0:m, i, :]).then_inc(s.out_y, 16)

        @block.vector
        def _(dve):
            v = nc.vector
            links = [0]

            def link(ins):
                links[0] += 1
                ins.then_inc(dch, 1)
                dve.wait_ge(dch, links[0])

            dve.wait_ge(s.pv_ps, 1)
            v.tensor_copy(PV[:], bank[7][:, 0:132]).then_inc(s.pv_ready, 1)
            dve.wait_ge(s.pv_ready, 1)
            for i, m in enumerate((P, P, NB + META)):
                dve.wait_ge(s.rstd_ready, 1)
                v.tensor_scalar(xn[0:m, i, :], h_tok[0:m, i, :], st3[0:m, 4 + i:5 + i], None, ALU.mult).then_inc(s.xn_ready, 1)
            for i, m in enumerate((P, P, NB + META)):
                for half in range(2):
                    q = 2 * i + half
                    dve.wait_ge(s.ht_ps, q + 1)
                    src = bank[q][:, :].rearrange("p (k n) -> p k n", n=P)
                    gain = PV[:, V_NMIX + 4 * half:V_NMIX + 4 * half + 4]
                    ks = slice(4 * half, 4 * half + 4)
                    if i < 2:
                        v.tensor_tensor(hT[:, ks, META + i * P:META + (i + 1) * P], src, bc_last(gain, P), ALU.mult)\
                            .then_inc(s.ht_ready, 1)
                    else:
                        v.tensor_tensor(hT[:, ks, NP:T], src[:, :, 0:NB], bc_last(gain, NB), ALU.mult)
                        v.tensor_tensor(hT[:, ks, 0:META], src[:, :, NB:NB + META], bc_last(gain, META), ALU.mult)\
                            .then_inc(s.ht_ready, 1)
            dve.wait_ge(s.prev_ps, 2)
            for dst, b, n in ((CA, bank[6], KD), (CBX, bank[7], CB_T)):
                for bb in range(NB):
                    last = v.tensor_copy(dst[:, :, SC0 + TAPS * bb:SC0 + TAPS * bb + PAD],
                                         b[:, 0:n * 24].rearrange("p (c q) -> p c q", q=24)[:, :, 3 * bb:3 * bb + 3])
                last.then_inc(s.prev_ready, 1)

            dve.wait_ge(s.late_in, 16 * 11)
            dve.wait_ge(s.u_ps, 3)
            v.tensor_scalar(RI[0:HA, :], bank[0][0:HA, 0:T], c16[0:HA, 0:1], None, ALU.add).then_inc(u_free[1], 1)
            v.tensor_scalar(XR[0:HA, T:2 * T], bank[0][32:32 + HA, 0:T], c16[0:HA, 1:2], -1.0, ALU.add, ALU.mult).then_inc(u_free[2], 1)
            v.tensor_scalar(XR[0:HB, 0:T], bank[0][64:64 + HB, 0:T], c16[:, 2:3], None, ALU.add).then_inc(u_free[0], 1)
            dve.wait_ge(u_free[0], 1)
            v.scalar_tensor_tensor(out=HN[0:HB, :], in0=XR[0:HB, :], scalar=-1.0, in1=XR[0:HB, :], op0=ALU.mult, op1=ALU.max).then_inc(s.x_abs, 1)
            dve.wait_ge(s.x_exp, 1)
            link(v.tensor_scalar(SS[0:HB, :], EX[0:HB, :], 2.0, None, ALU.add))
            link(v.reciprocal(SS[0:HB, :], SS[0:HB, :]))
            link(v.tensor_tensor(SS[0:HB, :], SS[0:HB, :], EX[0:HB, :], ALU.mult))
            link(v.tensor_tensor(HN[0:HB, :], SS[0:HB, :], SS[0:HB, :], ALU.mult))
            link(v.tensor_scalar(EX[0:HB, :], HN[0:HB, :], ATANH[-1], None, ALU.mult))
            for cf in reversed(ATANH[:-1]):
                link(v.scalar_tensor_tensor(out=EX[0:HB, :], in0=EX[0:HB, :], scalar=cf, in1=HN[0:HB, :], op0=ALU.add, op1=ALU.mult))
            link(v.scalar_tensor_tensor(out=EX[0:HB, :], in0=EX[0:HB, :], scalar=1.0, in1=SS[0:HB, :], op0=ALU.add, op1=ALU.mult))
            link(v.tensor_scalar(HN[0:HB, :], XR[0:HB, :], 0.0, None, ALU.max))
            link(v.scalar_tensor_tensor(out=XR[0:HB, :], in0=EX[0:HB, :], scalar=2.0, in1=HN[0:HB, :], op0=ALU.mult, op1=ALU.add))
            dve.wait_ge(s.x_exp, 2)
            link(v.tensor_scalar(SS[0:HB, 0:T], XR[0:HB, 0:T], c16[:, 5:6], None, ALU.mult))
            v.tensor_tensor_scan(AR[0:HB, 0:NP], ENM[0:HB, 0:NP], SS[0:HB, 0:NP], 0.0, ALU.mult, ALU.add)
            link(v.tensor_copy(AR[0:HB, NP:T], SS[0:HB, NP:T]))
            v.tensor_tensor_scan(BN[0:HA, 0:NP], ENM[0:HA, 0:NP], XR[0:HA, T:T + NP], 0.0, ALU.mult, ALU.add)
            link(v.tensor_copy(BN[0:HA, NP:T], XR[0:HA, T + NP:2 * T]))
            link(v.tensor_tensor(AC[0:HA, :], RI[0:HA, :], BN[0:HA, :], ALU.add))
            dve.wait_ge(s.late_in, 16 * 11)
            v.tensor_tensor_scan(MX[0:HA, 0:NP], AC[0:HA, 0:NP], AC[0:HA, 0:NP], 0.0, ALU.max, ALU.max)
            link(v.tensor_tensor(MX[0:HA, NP:T], AC[0:HA, NP:T], m0s[:, :], ALU.max))
            v.tensor_tensor(MROW[0:HA, :], MX[0:HA, :], BN[0:HA, :], ALU.subtract)
            v.tensor_scalar(c16[0:HA, 6:7], MX[0:HA, NP - 1:NP], -1.0, None, ALU.mult)
            v.tensor_scalar(c16[:, 7:8], AR[0:HB, NP - 1:NP], -1.0, None, ALU.mult)
            v.tensor_tensor(WSR[0:HA, NP:T], AC[0:HA, NP:T], MX[0:HA, NP:T], ALU.subtract)
            v.tensor_tensor(RS[:, 0:NB], m0s[:, :], MX[0:HA, NP:T], ALU.subtract)
            v.tensor_tensor(RS[:, NB:2 * NB], AC[0:HA, NP:T], MX[0:HA, NP:T], ALU.subtract)
            v.tensor_copy(RX[:, NB:2 * NB], XR[0:HB, NP:T])
            v.tensor_copy(RX[:, 16:17], c16[:, 4:5]).then_inc(s.rows_pre, 1)

            def conv_taps(n):
                kind, c, _u, _o = UT[n]
                src = CA if kind == "xa" else CBX
                w0, n0_, bcol = (V_CAW, KD, V_CAB) if kind == "xa" else (V_CBW, CB_T, V_CBB)
                y = CY[:, n % 2, :]
                dve.wait_ge(s.lc_ready, n + 1)
                if n >= 2:
                    dve.wait_ge(s.conv_done, n - 1)
                link(v.tensor_scalar(y, src[:, c, 0:W], PV[:, w0 + c:w0 + c + 1], PV[:, bcol + c:bcol + c + 1], ALU.mult, ALU.add))
                for j in range(1, TAPS):
                    wj = w0 + j * n0_ + c
                    ins = v.scalar_tensor_tensor(out=y, in0=src[:, c, j:j + W], scalar=PV[:, wj:wj + 1], in1=y,
                                                 op0=ALU.mult, op1=ALU.add)
                    if j < TAPS - 1:
                        link(ins)
                ins.then_inc(s.conv_y, 1)

            def conv_gate(n):
                kind, c, _u, _o = UT[n]
                dst = XC[:, c, :] if kind == "xa" else CBX[:, c, 0:W]
                dve.wait_ge(s.conv_sig, n + 1)
                v.tensor_tensor(dst, CY[:, n % 2, :], CSG[:, n % 2, :], ALU.mult).then_inc(s.conv_done, 1)

            dve.wait_ge(s.prev_ready, 2)
            for n in range(NCONV):
                conv_taps(n)
                if n >= 1:
                    conv_gate(n - 1)
            conv_gate(NCONV - 1)
            for n, (kind, c, _u, _o) in enumerate(UT):
                if kind == "zb":
                    dve.wait_ge(s.z_sig, c + 1)
                    v.tensor_tensor(ZB[:, c, :], bank[(n + 3) % 4][:, 0:T], ZB[:, c, :], ALU.mult).then_inc(u_free[(n + 3) % 4], 1)

            dve.wait_ge(s.tm_ps, 1)
            v.tensor_copy(TM[:, 0:2, :], bank[4][:, 0:128].rearrange("p (a b) -> p a b", b=64))
            link(v.tensor_copy(TM[0:16, 2, :], bank[4][0:16, 128:192]))
            v.tensor_scalar(TM[:, 0:2, 8:16], TM[:, 0:2, 8:16], DH ** -0.5, None, ALU.mult)
            v.tensor_scalar(TM[0:16, 2, 8:16], TM[0:16, 2, 8:16], DH ** -0.5, None, ALU.mult).then_inc(s.tm_ready, 1)
            dve.wait_ge(s.bcm_ps, 1)
            v.tensor_copy(BCM[:], bank[5][:, 0:128].rearrange("p (a b) -> p a b", b=16))
            v.tensor_copy(XE[:], bank[5][:, 128:128 + KD * 17].rearrange("p (a b) -> p a b", b=17)).then_inc(s.bcm_ready, 1)

            def decay_args(n, key):
                row = n if key < 16 else HA + n
                b = ROWB[row % 4]
                dve.wait_ge(row_in[row % 4], 16 * (row // 4 + 1))
                for j, (t0, m) in enumerate(S_TILES):
                    w = NP - t0
                    last = v.scalar_tensor_tensor(out=ARG[0:m, n % 2, BLK[j]:BLK[j] + w], in0=b[0:m, t0:NP],
                                                  scalar=TM[0:m, j, key:key + 1], in1=mask[0:m, 0:w],
                                                  op0=ALU.subtract, op1=ALU.max)
                last.then_inc(s.arg_done, 1)

            tmp3 = TMPS.rearrange("p (a b) -> p a b", b=P)
            xs_s = CBX[:, 0:KD, SC0:SC0 + TAPS * (NB - 1) + 1:TAPS]
            dve.wait_ge(s.bcm_ready, 1)
            v.tensor_tensor(YS2[:], xs_s, XE[:, :, 16:17].to_broadcast([P, KD, NB]), ALU.mult)
            link(v.tensor_tensor(XDS[:], xs_s, XE[:, :, NB:2 * NB], ALU.mult))

            def s_update(b):
                dve.wait_ge(bb_in[b % 2], 16 * (b // 2 + 1))
                dve.wait_ge(s.st_dec, b + 1)
                st = stage[:, b % 3, :]
                st3d = st.rearrange("p (a b) -> p a b", b=P)
                for c in range(KD):
                    j = c // (KD // NG)
                    last = v.scalar_tensor_tensor(out=st3d[:, c, :], in0=BB[:, b % 2, j * P:(j + 1) * P],
                                                  scalar=XDS[:, c, b:b + 1], in1=st3d[:, c, :], op0=ALU.mult, op1=ALU.add)
                last.then_inc(s.st_new, 1)
                dve.wait_ge(s.st_new, b + 1)
                for j in range(NG):
                    last = v.tensor_tensor(tmp3[:, 4 * j:4 * j + 4, :], st3d[:, 4 * j:4 * j + 4, :],
                                           BB[:, b % 2, (2 + j) * P:(3 + j) * P].unsqueeze(1).to_broadcast([P, 4, P]), ALU.mult)
                last.then_inc(s.s_y, 1)
                dve.wait_ge(s.s_y, b + 1)
                link(v.tensor_reduce(YS[:, :, b], tmp3, AX, ALU.add))

            dve.wait_ge(s.tm_ready, 1)
            def head_args(h):
                if h >= 2:
                    dve.wait_ge(s.nc_ps, h - 1)
                decay_args(h, h)

            head_args(0)
            for h in range(HA):
                dve.wait_ge(s.exp_done, h + 1)
                dve.wait_ge(s.sc_ps, h + 1)
                v.tensor_tensor(ARG[:, h % 2, 0:BLK[2]], bank[4][:, 0:BLK[2]], ARG[:, h % 2, 0:BLK[2]], ALU.mult)
                v.tensor_tensor(ARG[0:16, h % 2, BLK[2]:BLKW], bank[4][0:16, BLK[2]:BLKW], ARG[0:16, h % 2, BLK[2]:BLKW],
                                ALU.mult).then_inc(s.st_done, 1)
                if h + 1 < HA:
                    head_args(h + 1)
                s_update(h)

            def c_update(b):
                dve.wait_ge(s.st_dec, NB + b + 1)
                st = stage[:, (NB + b) % 3, :]
                v.tensor_tensor(st, st, VB[b % 2], ALU.add).then_inc(s.st_new, 1)

            for j, (_t0, m) in enumerate(S_TILES):
                for half in range(2):
                    q = 2 * j + half
                    dve.wait_ge(s.xs_ps, q + 1)
                    v.tensor_tensor(XDT[0:m, j, half * 512:(half + 1) * 512].rearrange("p (h q) -> p h q", q=HD),
                                    bank[q][0:m, :].rearrange("p (h q) -> p h q", q=HD),
                                    bc_last(TM[0:m, j, 32 + 8 * half:40 + 8 * half], HD), ALU.mult).then_inc(s.xdt_ready, 1)
            dve.wait_ge(s.n0_ps, 1)
            v.tensor_copy(NSTo[:], bank[6][0:HA, 64:64 + P])
            bh = "p (b h) -> p h b"
            dve.wait_ge(s.n0_ps, 1)
            dve.wait_ge(s.qs_done, HA)
            dve.wait_ge(s.bcm_ready, 1)
            v.tensor_tensor(NT[:].rearrange(bh, h=HA), bank[6][:, 0:64].rearrange(bh, h=HA), BCM[:, :, 0:NB], ALU.mult)
            link(v.tensor_tensor(KS[:], KS[:], BCM[:, :, NB:2 * NB], ALU.mult))
            link(v.tensor_tensor(N1[:].rearrange(bh, h=HA), NT[:].rearrange(bh, h=HA), KS[:], ALU.add))
            v.tensor_tensor(QN[:].rearrange(bh, h=HA), N1[:].rearrange(bh, h=HA), QS[:], ALU.mult).then_inc(s.n1_ready, 1)
            link(v.tensor_tensor(YB[:, :, NP:T], YS[:], YS2[:], ALU.add))
            def gate_y(c):
                dve.wait_ge(y_free[c % 2], c // 2 + 1)
                v.tensor_tensor(YB[:, c, :], YB[:, c, :], ZB[:, c, :], ALU.mult).then_inc(s.yz_ready, 1)

            def ssd_args(h):
                if h >= 2:
                    dve.wait_ge(s.y_ps, h - 1)
                decay_args(h, 16 + h)

            dve.wait_ge(s.nc_ps, HA)
            ssd_args(0)
            dve.wait_ge(s.n1_ps, 1)
            v.tensor_copy(N1T[:], bank[6][0:64, 256:256 + P]).then_inc(s.n1_sb, 1)
            dve.wait_ge(s.den_ps, 1)
            v.tensor_copy(DEN[0:HA, :], bank[7][0:HA, 0:T]).then_inc(s.den_sb, 1)
            for h in range(HB):
                if h + 1 < HB:
                    ssd_args(h + 1)
                if h == 0:
                    dve.wait_ge(s.gt_ready, NG)
                dve.wait_ge(s.exp_done, HA + h + 1)
                j = h // (HB // NG)
                v.tensor_tensor(ARG[:, h % 2, 0:BLK[2]], GT[:, j, 0:BLK[2]], ARG[:, h % 2, 0:BLK[2]], ALU.mult)
                v.tensor_tensor(ARG[0:16, h % 2, BLK[2]:BLKW], GT[0:16, j, BLK[2]:BLKW], ARG[0:16, h % 2, BLK[2]:BLKW],
                                ALU.mult).then_inc(s.st_done, 1)
                if h % 2 == 0 and h >= 2:
                    ssd_out(dve, h // 2 - 1)
                    gate_y(h // 2 - 1)
                if h == 0:
                    dve.wait_ge(s.den_sb, 1)
                    link(v.scalar_tensor_tensor(out=DEN[0:HA, :], in0=DEN[0:HA, :], scalar=-1.0, in1=DEN[0:HA, :], op0=ALU.mult, op1=ALU.max))
                    link(v.tensor_tensor(DEN[0:HA, :], DEN[0:HA, :], ENM[0:HA, :], ALU.max))
                    link(v.reciprocal(DEN[0:HA, :], DEN[0:HA, :]))
                if h % 2 == 0:
                    c_update(h // 2)
            ssd_out(dve, KD - 1)
            gate_y(KD - 1)
            dve.wait_ge(s.sq_ps, HA + KD + 1)
            link(v.tensor_tensor(SCL[0:HA, :], bank[7][0:HA, 0:T], DEN[0:HA, :], ALU.mult))
            v.tensor_tensor(SCL[0:HA, :], SCL[0:HA, :], DEN[0:HA, :], ALU.mult).then_inc(s.rden_ready, 1)
            dve.wait_ge(s.za_done, HA)
            dve.wait_ge(s.cq_sb, 1)
            v.tensor_tensor(NUM[:, :, NP:T], NUM[:, :, NP:T], ZA[:, :, NP:T], ALU.mult)
            dve.wait_ge(s.sc_exp, 1)
            v.tensor_tensor(SCL[0:HA, :], SCL[0:HA, :], DEN[0:HA, :], ALU.mult).then_inc(s.scale_ready, 1)
            for c in range(KD):
                if c % 4 == 0:
                    dve.wait_ge(s.gbc_ps, c // 4 + 1)
                v.scalar_tensor_tensor(out=YB[:, c, :], in0=bank[6 if c < 4 else 0][:, 0:T],
                                       scalar=PV[:, V_NB + c:V_NB + c + 1], in1=YB[:, c, :],
                                       op0=ALU.mult, op1=ALU.mult).then_inc(s.yb_norm, 1)
            for h in range(HA):
                if h == 0:
                    dve.wait_ge(s.scale_ready, 1)
                dve.wait_ge(s.hbc_ps, h + 1)
                v.scalar_tensor_tensor(out=NUM[:, h, :], in0=bank[1 + h % 4][:, 0:T], scalar=PV[:, V_NA + h:V_NA + h + 1],
                                       in1=NUM[:, h, :], op0=ALU.mult, op1=ALU.mult).then_inc(s.num_ready, 1)

            for half in range(2):
                for i, (_t0, m) in enumerate(TOK):
                    if half == 0 and i == 0:
                        dve.wait_ge(s.x_again, 16 * 3)
                    dve.wait_ge(s.wt_ps, half + 1)
                    hv = h_tok[0:m, i, half * 512:(half + 1) * 512]
                    ins = v.tensor_tensor(hv, hv, bank[i + 3 * half][0:m, :], ALU.add)
                    if half == 1:
                        ins.then_inc(s.h_ready, 1)
            for i, (t0, m) in enumerate(TOK):
                for half in range(2):
                    q = 2 * i + half
                    dve.wait_ge(s.xt_ps, q + 1)
                    src = bank[(q + 6) % 8][:, :].rearrange("p (k n) -> p k n", n=P)
                    gain = PV[:, V_NFF + 4 * half:V_NFF + 4 * half + 4]
                    v.tensor_tensor(XT[:, 4 * half:4 * half + 4, t0:t0 + m], src[:, :, 0:m], bc_last(gain, m), ALU.mult)\
                        .then_inc(s.xt_ready, 1)
            dve.wait_ge(s.h_rstd, 1)
            dve.wait_ge(s.lg_ps, 1)
            lbias = LP[:].rearrange("p a b c -> p (a b c)")[:, 0:20]
            link(v.tensor_copy(lbias, bank[5][:, 64:84]))
            for i, (_t0, m) in enumerate(TOK):
                last = v.scalar_tensor_tensor(out=L[0:m, i, :], in0=bank[5][0:m, i * 20:(i + 1) * 20],
                                              scalar=st3[0:m, 4 + i:5 + i], in1=lbias[0:m, :], op0=ALU.mult, op1=ALU.add)
            link(last)
            LG = L[:, :, 0:4]

            def bc4(c):
                return r1[:, :, c:c + 1].to_broadcast([P, 3, 4])

            ord3 = order[:].unsqueeze(1).to_broadcast([P, 3, 4])

            def first_best(out, vals, c, ck, done=None):
                link(v.tensor_tensor(K1[:], vals, bc4(c), ALU.is_equal))
                link(v.tensor_tensor(K1[:], K1[:], ord3, ALU.mult))
                link(v.tensor_reduce(r1[:, :, ck], K1[:], AX, ALU.max))
                ins = v.tensor_tensor(out, K1[:], bc4(ck), ALU.is_equal)
                if done is None:
                    link(ins)
                else:
                    ins.then_inc(done, 1)
                    dve.wait_ge(done, 1)

            link(v.tensor_reduce(r1[:, :, 0], LG, AX, ALU.max))
            v.tensor_tensor(LX[:], LG, bc4(0), ALU.subtract).then_inc(s.lx_ready, 1)
            first_best(M1[:], LG, 0, 1, s.router)
            for i in range(3):
                last = v.tensor_tensor(LP[:, i], L[:, i, 4:20].rearrange("p (g e) -> p e g", g=EG),
                                       M1[:, i, :].unsqueeze(1).to_broadcast([P, EPG, EG]), ALU.mult)
            link(last)
            link(v.tensor_reduce(L2[:], LP[:], AX, ALU.add))
            link(v.tensor_reduce(r1[:, :, 2], L2[:], AX, ALU.max))
            first_best(O1[:], L2[:], 2, 1)
            link(v.scalar_tensor_tensor(out=L2[:], in0=O1[:], scalar=-BIG, in1=L2[:], op0=ALU.mult, op1=ALU.add))
            link(v.tensor_reduce(r1[:, :, 4], L2[:], AX, ALU.max))
            v.tensor_tensor(r1[:, :, 3], r1[:, :, 4], r1[:, :, 2], ALU.subtract).then_inc(s.lx_ready, 1)
            first_best(O2[:], L2[:], 4, 1)
            dve.wait_ge(s.p1_exp, 1)
            link(v.tensor_reduce(r1[:, :, 5], LX[:], AX, ALU.add))
            dve.wait_ge(s.p1_exp, 2)
            link(v.tensor_scalar(r1[:, :, 6], r1[:, :, 3], 1.0, None, ALU.add))
            link(v.tensor_tensor(r1[:, :, 6], r1[:, :, 6], r1[:, :, 5], ALU.mult))
            link(v.reciprocal(r1[:, :, 6], r1[:, :, 6]))
            link(v.tensor_tensor(r1[:, :, 7], r1[:, :, 6], r1[:, :, 3], ALU.mult))
            v.tensor_tensor(O1[:], O1[:], bc4(6), ALU.mult)
            link(v.tensor_tensor(O2[:], O2[:], bc4(7), ALU.mult))
            v.tensor_tensor(GATE[:], O1[:], O2[:], ALU.add).then_inc(s.router, 1)
            dve.wait_ge(s.rank_ps, 1)
            v.tensor_copy(rank[:, 0:2, :], bank[0][:, 0:8].rearrange("p (a b) -> p a b", b=4)).then_inc(s.h_add, 4)
            v.tensor_copy(rank[0:NB, 2, :], bank[0][0:NB, 8:12]).then_inc(s.rank_ready, 1)
            link(v.tensor_reduce(cnt[:, 0:1], bank[0][:, 12:16], AX, ALU.max))
            v.tensor_scalar(cnt[:, 1:2], cnt[:, 0:1], 128.0, 1.0, ALU.is_gt, ALU.add).then_inc(s.yg_done, 1)
            link(v.tensor_scalar(cnt[:, 2:3], cnt[:, 0:1], 256.0, None, ALU.is_gt))
            v.tensor_tensor(rounds[:], cnt[:, 1:2], cnt[:, 2:3], ALU.add).then_inc(s.rounds_ready, 1)

            nr = rounds_of(dve)
            with dve.Fori(0, nr) as r:
                dve.wait_ge(s.rank_ready, r + 1)
                for i, (_t0, m) in enumerate(TOK):
                    for q in range(EG):
                        last = v.tensor_scalar(PG[0:m, i, q * P:(q + 1) * P], iota[0:m, :], rank[0:m, i, q:q + 1],
                                               M1[0:m, i, q:q + 1], ALU.is_equal, ALU.mult)
                    if i != 1:
                        last.then_inc(s.p_ready, 1)
                dve.wait_ge(s.pt_ps, r * 2 + 1)
                for q in range(EG):
                    last = v.tensor_copy(PT[:, q, :], bank[1 + q][:, 0:NOUT])
                last.then_inc(s.pt_ready, 1)
                for k in range(0, KD, 2):
                    if k == KD - 2:
                        v.memset(YG.rearrange("p a b -> p (a b)"), 0.0).then_inc(s.pt_ready, 1)
                    dve.wait_ge(s.xg_ps, r * KD + (k + 1))
                    v.tensor_scalar(XG[:, k, :], bank[(k + 5) % 8][:, :], PV[:, V_NFF + k:V_NFF + k + 1], None, ALU.mult)\
                        .then_inc(s.xg_ready, 1)
                dve.wait_ge(s.pt_ps, r * 2 + 2)
                v.tensor_copy(GS[:], bank[5][:, 0:16]).then_inc(s.pt_ready, 1)
                with dve.Fori(0, EG) as q:
                    with dve.Fori(0, EPG) as e:
                        x = (r * EG + q) * EPG + e
                        for j in range(2):
                            if j == 0:
                                dve.wait_ge(s.pt_ready, r * 3 + 3)
                            dve.wait_ge(s.silu_done, x * 2 + (j + 1))
                            dve.wait_ge(s.gu_ps, x * 2 + (j + 2))
                            v.scalar_tensor_tensor(out=AH[:, j * 512:(j + 1) * 512], in0=bank[2 * j + 1][:, :],
                                                   scalar=GS[:, bass.ds(q * EPG + e, 1)], in1=SG[:, j * 512:(j + 1) * 512],
                                                   op0=ALU.mult, op1=ALU.mult).then_inc(s.a_ready, 1)
                        dve.wait_ge(s.xg_ready, r * KD + KD)
                        dve.wait_ge(s.d_ps, x + 1)
                        dve.wait_ge(s.yg_done, x + 1)
                        yv = YG.rearrange("p a b -> p (a b)")
                        for j in range(2):
                            o = yv[:, bass.ds(q * D + j * 512, 512)]
                            last = v.tensor_tensor(o, o, bank[6 + j][:, :], ALU.add)
                        last.then_inc(s.yg_done, 1)
                for i, (_t0, m) in enumerate(TOK):
                    for half in range(2):
                        dve.wait_ge(s.sc_out_ps, r * 6 + (2 * i + half + 1))
                        hv = h_tok[0:m, i, half * 512:(half + 1) * 512]
                        v.tensor_tensor(hv, hv, bank[2 * i + half][0:m, :], ALU.add).then_inc(s.h_add, 1)
                v.tensor_scalar(rank[:, 0:2, :], rank[:, 0:2, :], float(P), None, ALU.subtract)
                v.tensor_scalar(rank[0:NB, 2, :], rank[0:NB, 2, :], float(P), None, ALU.subtract).then_inc(s.rank_ready, 1)

            dve.wait_ge(s.nf_in, 16)
            dve.wait_ge(s.h_add, nr * 6 + 4)
            for i, (_t0, m) in enumerate(TOK):
                last = v.tensor_tensor(YN[0:m, i, :], h_tok[0:m, i, :], NF[0:m, :], ALU.mult)
            last.then_inc(s.y_ready, 1)
            dve.wait_ge(s.y_ready, 1)
            dve.wait_ge(s.f_rstd, 1)
            for i in (0, 2):
                m = TOK[i][1]
                v.tensor_scalar(YN[0:m, i, :], YN[0:m, i, :], st3[0:m, 4 + i:5 + i], None, ALU.mult).then_inc(s.y_ready, 1)

        @block.tensor
        def _(pe):
            mm = nc.tensor.matmul
            tr = nc.tensor.transpose

            pe.wait_ge(s.consts, 1)
            pe.wait_ge(s.params_in, 16 * 8)
            tr(bank[7][:, 0:84], PR[0:84, 0, :], ident[0:84, 0:84])
            tr(bank[7][:, 84:132], PR[0:48, 1, :], ident[0:48, 0:48]).then_inc(s.pv_ps, 1)
            for i, m in enumerate((P, P, NB + META)):
                pe.wait_ge(s.xn_ready, i + 1)
                for k in range(KD):
                    last = tr(bank[2 * i + k // 4][:, (k % 4) * P:(k % 4) * P + m], xn[0:m, i, k * P:(k + 1) * P], ident[0:m, 0:m])
                    if k % 4 == 3:
                        last.then_inc(s.ht_ps, 1)
            pe.wait_ge(s.prev_in, 32)
            pe.wait_ge(s.pv_ready, 1)
            for base, b, n in ((0, bank[6], KD), (KD, bank[7], CB_T)):
                for c in range(n):
                    last = tr(b[:, c * 24:(c + 1) * 24], CPREV[0:24, (base + c) * P:(base + c + 1) * P], ident[0:24, 0:24])
                last.then_inc(s.prev_ps, 1)

            pe.wait_ge(s.ht_ready, 6)
            pe.wait_ge(s.gates_in, 48)
            for k in range(KD):
                last = mm(bank[0][0:80, 0:T], WG[:, k, :], hT[:, k, :], start=(k == 0), stop=(k == KD - 1))
            last.then_inc(s.u_ps, 3)
            for n0_, (kind, c, u, o) in enumerate(UT):
                n = n0_ + 3
                if o == 0:
                    i, cnt_ = unit_at(u)
                    pe.wait_ge(arrived[i], cnt_)
                if n >= 4:
                    pe.wait_ge(u_free[n % 4], n // 4)
                for k in range(KD):
                    last = mm(bank[n % 4][:, 0:T], slot_k(u % MR, 512)[:, k, o:o + P], hT[:, k, :],
                              start=(k == 0), stop=(k == KD - 1))
                last.then_inc(s.u_ps, 1)

            pe.wait_ge(s.rows_pre, 1)
            pe.wait_ge(s.rows_exp, 1)
            for j, (t0, m) in enumerate(S_TILES):
                for rows, nrow, c0 in ((AC, HA, 0), (WSR, HA, 8), (AR, HB, 16), (XR, HB, 32), (EDR, HB, 48)):
                    last = tr(bank[4][0:m, j * 64 + c0:j * 64 + c0 + nrow], rows[0:nrow, t0:t0 + m], ident[0:nrow, 0:nrow])
            last.then_inc(s.tm_ps, 1)
            for h in range(HA):
                mm(bank[5][:, h * 16:(h + 1) * 16], col(ident[0:HA, :], h), RS[:, :], start=True, stop=True)
            for c in range(KD):
                for j in range(2):
                    last = mm(bank[5][j * HD:(j + 1) * HD, 128 + c * 17:128 + (c + 1) * 17],
                              ident[0:HB, 2 * c + j:2 * c + j + 1].to_broadcast([HB, HD]), RX[:, :], start=True, stop=True)
            last.then_inc(s.bcm_ps, 1)
            for q in range(5):
                if q >= 2:
                    pe.wait_ge(s.lct_sb, q - 1)
                if q == 0:
                    pe.wait_ge(u_free[(NCONV + 2) % 4], (NCONV + 2) // 4 + 1)
                for c in range(4):
                    last = tr(bank[6 + q % 2][0:LAST, c * P:(c + 1) * P], LC[:, 4 * q + c, :], ident[:, :])
                last.then_inc(s.lct_ps, 1)

            pe.wait_ge(s.conv_done, NCONV)
            pe.wait_ge(s.lct_sb, 5)
            for c in range(4):
                last = tr(bank[7][0:NB, c * P:(c + 1) * P], smp(CBX[:, KD + c, :]), ident[:, :])
            last.then_inc(s.bcs_ps, 1)

            iq, cq = unit_at(U_QKV)
            pe.wait_ge(arrived[iq], cq)
            wq, wk, wv = (slot[iq][:, j * D:(j + 1) * D].rearrange("p (h e) -> p h e", e=DH) for j in range(3))
            for b, n in enumerate((10, 10, 10, 9)):
                pe.wait_ge(u_free[b], n)

            def head_proj(h):
                if h >= 1:
                    pe.wait_ge(s.q_sb, h)
                    pe.wait_ge(s.k_sb, h)
                    pe.wait_ge(s.kw_sb, h)
                    pe.wait_ge(s.v_sb, h)
                mm(bank[0][:, 0:W], wq[:, h, :], XC[:, h, :], start=True, stop=True).then_inc(s.q_ps, 1)
                mm(bank[1][:, 0:W], wk[:, h, :], XC[:, h, :], start=True, stop=True).then_inc(s.k_ps, 1)
                for j, (t0, m) in enumerate(S_TILES):
                    last = mm(bank[2][0:m, j * P:(j + 1) * P], XC[:, h, t0:t0 + m], wk[:, h, :], start=True, stop=True)
                last.then_inc(s.kt_ps, 1)
                for j, (t0, m) in enumerate(S_TILES):
                    mm(bank[3][0:m, j * P:(j + 1) * P], CA[:, h, PAD + t0:PAD + t0 + m], wv[:, h, :], start=True, stop=True)
                mm(bank[3][0:NB, 384:512], CA[:, h, SC0 + PAD:SC0 + PAD + TAPS * (NB - 1) + 1:TAPS], wv[:, h, :],
                   start=True, stop=True).then_inc(s.vt_ps, 1)

            def block_mm(b, c0, lhs, rhs, key, start, accumulate):
                for j, (t0, m) in enumerate(S_TILES):
                    w = NP - t0
                    if accumulate:
                        o = b[:, c0 + t0:c0 + NP]
                    else:
                        o = b[0:m, BLK[j]:BLK[j] + w]
                    last = mm(o, lhs(j, t0, m), rhs(j, t0, m, w), start=(start and (j == 0 or not accumulate)),
                              stop=(j == 2 or not accumulate))
                return last

            head_proj(0)
            pe.wait_ge(s.tm_ready, 1)
            pe.wait_ge(s.bcm_ready, 1)
            for h in range(HA):
                if h >= 1:
                    pe.wait_ge(s.st_done, h)
                pe.wait_ge(s.q_sb, h + 1)
                pe.wait_ge(s.k_sb, h + 1)
                block_mm(bank[4], 0, lambda j, t0, m: kT[:, h % 2, t0:t0 + m], lambda j, t0, m, w: qT[:, h % 2, t0:NP],
                         None, True, False).then_inc(s.sc_ps, 1)
                if h + 1 < HA:
                    head_proj(h + 1)
                pe.wait_ge(s.st_done, h + 1)
                pe.wait_ge(s.v_sb, h + 1)
                pe.wait_ge(s.kw_sb, h + 1)
                if h >= 1:
                    pe.wait_ge(s.num_sb, h)
                else:
                    pe.wait_ge(s.bcs_ready, 1)
                sc = lambda j, t0, m, w: ARG[0:m, h % 2, BLK[j]:BLK[j] + w]
                block_mm(bank[6], 0, lambda j, t0, m: vv[0:m, h % 2, j, 0:P], sc, None, True, True)
                for j, (t0, m) in enumerate(S_TILES):
                    mm(bank[7][0:HA, t0:NP], strip[0:m, 7 - h:15 - h], sc(j, t0, m, NP - t0),
                       start=(h == 0 and j == 0), stop=(h == HA - 1 and j == 2), skip_group_check=True)
                for j, (t0, m) in enumerate(S_TILES):
                    last = mm(bank[6][:, NP:NP + P + 1], kw[0:m, h % 2, j, :], vv[0:m, h % 2, j, :], start=(j == 0), stop=(j == 2))
                last.then_inc(s.nc_ps, 1)
            for j, (t0, m) in enumerate(S_TILES):
                for half in range(2):
                    q = 2 * j + half
                    if q == 0:
                        pe.wait_ge(s.q_sb, HA)
                        pe.wait_ge(s.k_sb, HA)
                        pe.wait_ge(s.kw_sb, HA)
                        pe.wait_ge(s.v_sb, HA)
                    bq = bank[q]
                    for c in range(4):
                        last = tr(bq[0:m, c * P:(c + 1) * P], CBX[:, 4 * half + c, t0:t0 + m], ident[:, :])
                    last.then_inc(s.xs_ps, 1)
            pe.wait_ge(s.late_in, 16 * 11)
            pe.wait_ge(s.nst_ready, HA)
            pe.wait_ge(s.num_sb, HA)
            tr(bank[6][:, 0:64], N0[:, :], ident[0:64, 0:64])
            tr(bank[6][0:HA, 64:64 + P], NSTt[:, :], ident[:, :]).then_inc(s.n0_ps, 1)
            pe.wait_ge(s.xdt_ready, 6)
            for j, (t0, m) in enumerate(S_TILES):
                for g_ in range(NG):
                    last = tr(bank[j // 2][0:m, (j % 2) * 256 + g_ * P:(j % 2) * 256 + (g_ + 1) * P], CBX[:, KD + g_, t0:t0 + m], ident[:, :])
            last.then_inc(s.bt_ps, 1)
            for g_ in range(NG):
                block_mm(bank[3 + g_], 0, lambda j, t0, m: CBX[:, KD + g_, t0:t0 + m], lambda j, t0, m, w: CBX[:, KD + NG + g_, t0:NP],
                         None, True, False).then_inc(s.gt_ps, 1)
            pe.wait_ge(s.n1_ready, 1)
            for h in range(HA):
                last = mm(bank[7][0:HA, NP:T], strip[:, 7 - h:15 - h], QN[:].rearrange("p (b h) -> p h b", h=HA)[:, h, :],
                          start=(h == 0), stop=(h == HA - 1), skip_group_check=True)
            last.then_inc(s.den_ps, 1)
            tr(bank[6][0:64, 256:256 + P], N1[:, :], ident[:, :]).then_inc(s.n1_ps, 1)
            pe.wait_ge(s.n1_sb, 1)

            def c_read(b):
                pe.wait_ge(s.st_new, NB + b + 1)
                if b == NB // 2:
                    pe.wait_ge(s.cq_half, 1)
                o = bank[3][0:HA, (b % 4) * P:(b % 4 + 1) * P]
                for h in range(HA):
                    last = mm(o, QZ[:, h, b, :], stage[:, (NB + b) % 3, h * P:(h + 1) * P], start=(h == 0), stop=(h == HA - 1))
                last.then_inc(s.cq_ps, 1)

            summed = [0]

            def group_sum():
                c = summed[0]
                summed[0] += 1
                g_ = c // 4
                pe.wait_ge(s.sq_done, HA + c + 1)
                mm(bank[7][32:32 + NG, 0:T], strip[:, 7 - g_:9 - g_], SQA[:, c, :], start=(c == 0), stop=(c == KD - 1)).then_inc(s.sq_ps, 1)

            for h in range(HB):
                c = h // 2
                if h == 0:
                    pe.wait_ge(s.bt_ready, 1)
                    pe.wait_ge(s.gt_ready, NG)
                if h % 2 == 0 and c >= 1:
                    c_read(c - 1)
                if h == 0:
                    pe.wait_ge(s.den_sb, 1)
                if h == 1:
                    pe.wait_ge(s.xw_ready, 3)
                if h % 2 == 1:
                    for j, (t0, m) in enumerate(S_TILES):
                        last = mm(bank[1 + c // 4][:, (c % 4) * P:(c % 4 + 1) * P], XWT[0:m, j, c * P:(c + 1) * P],
                                  BT[0:m, j, (c // 4) * P:(c // 4 + 1) * P], start=(j == 0), stop=(j == 2))
                    if c % 4 == 3:
                        last.then_inc(s.sst_ps, 1)
                if h < HA:
                    pe.wait_ge(s.sq_done, h + 1)
                    mm(bank[7][0:HA, 0:NP], strip[:, 7 - h:15 - h], SQA[:, h, 0:NP], start=(h == 0), stop=(h == HA - 1)).then_inc(s.sq_ps, 1)
                if h >= HA and h % 2 == 0:
                    for cc in range({8: 3, 10: 1, 12: 1, 14: 1}[h]):
                        group_sum()
                pe.wait_ge(s.st_done, HA + h + 1)
                if h % 2 == 0 and c >= 2:
                    pe.wait_ge(y_free[c % 2], c // 2)
                yb = bank[6 if c % 2 == 0 else 0]
                q0 = HD * (h % 2)
                for j, (t0, m) in enumerate(S_TILES):
                    last = mm(yb[q0:q0 + HD, t0:NP], XDT[0:m, j, h * HD:(h + 1) * HD], ARG[0:m, h % 2, BLK[j]:BLK[j] + NP - t0],
                              start=(j == 0), stop=(j == 2))
                last.then_inc(s.y_ps, 1)
            c_read(NB - 1)
            group_sum()
            group_sum()
            pe.wait_ge(s.cq_half, 2)
            for b in range(NB):
                last = tr(bank[3][:, b * HA:(b + 1) * HA], VS[:, b * P:(b + 1) * P], ident[0:HA, 0:HA])
            last.then_inc(s.cq_ps, 1)
            pe.wait_ge(s.cq_sb, 1)
            for h in range(HA):
                last = mm(bank[7][0:HA, NP:T], strip[:, 7 - h:15 - h], QN[:].rearrange("p (b h) -> p h b", h=HA)[:, h, :],
                          start=(h == 0), stop=(h == HA - 1), skip_group_check=True)
            last.then_inc(s.sq_ps, 1)
            pe.wait_ge(s.sst_ready, 2)
            pe.wait_ge(s.arg_done, HA + HB)
            pe.wait_ge(y_free[0], 4)
            pe.wait_ge(y_free[1], 4)
            pe.wait_ge(s.ysc_exp, 1)
            for j in range(NG):
                mm(bank[6 if j == 0 else 0][:, 0:T], col(ident[32:32 + NG, :], 32 + j), YSC, start=True, stop=True).then_inc(s.gbc_ps, 1)
            pe.wait_ge(s.scale_ready, 1)
            for h in range(HA):
                if h >= 4:
                    pe.wait_ge(s.num_ready, h - 3)
                mm(bank[1 + h % 4][:, 0:T], col(ident[0:HA, :], h), SCL[0:HA, :], start=True, stop=True).then_inc(s.hbc_ps, 1)

            pe.wait_ge(s.yb_norm, KD)

            def out_part(kc, dt):
                w = slot_k(unit_at(U_OUT + kc // 4)[0], D)
                src = NUM if kc < HA else YB
                return mm(bank[dt][:, 0:NOUT], w[:, kc % 4, dt * P:(dt + 1) * P], src[:, kc % 8, META:T],
                          start=(kc == 0), stop=(kc == 15), skip_group_check=True)

            def out_turn(dt):
                if dt == 0:
                    pe.wait_ge(s.mt_sb, 3)
                if dt == 4:
                    pe.wait_ge(s.mt_sb, 6)
                pe.wait_ge(s.mt_sb, dt + 1)
                for i, (t0, m) in enumerate(TOK):
                    last = tr(bank[i + 3 * (dt // 4)][0:m, (dt % 4) * P:(dt % 4 + 1) * P], MT[:, dt, t0:t0 + m], ident[:, :])
                if dt % 4 == 3:
                    last.then_inc(s.wt_ps, 1)

            for j in range(4):
                i, cnt_ = unit_at(U_OUT + j)
                pe.wait_ge(arrived[i], cnt_)
                if j < 3:
                    for kk in range(4):
                        if 4 * j + kk < HA:
                            pe.wait_ge(s.num_ready, 4 * j + kk + 1)
                        for dt in range(KD) if j + kk else (5, 7, 0, 6, 1, 2, 3, 4):
                            if j + kk == 0 and 1 <= dt <= 4:
                                pe.wait_ge(s.num_ready, 4 + dt)
                            last = out_part(4 * j + kk, dt)
                    last.then_inc(s.wo_unit, 1)
                else:
                    for dt in range(KD):
                        for kk in range(4):
                            last = out_part(4 * j + kk, dt)
                        last.then_inc(s.mo_ps, 1)
                        if dt >= 3:
                            out_turn(dt - 3)
                    for dt in range(5, 8):
                        out_turn(dt)

            for i, (t0, m) in enumerate(TOK):
                pe.wait_ge(s.h_ready, i + 1)
                for k in range(KD):
                    last = tr(bank[(2 * i + k // 4 + 6) % 8][:, (k % 4) * P:(k % 4) * P + m], h_tok[0:m, i, k * P:(k + 1) * P],
                              ident[0:m, 0:m])
                    if k % 4 == 3:
                        last.then_inc(s.xt_ps, 1)
            pe.wait_ge(s.late_in, 16 * 11)
            mm(bank[5][:, 64:84], ones[0:1, :], br[:, :], start=True, stop=True)
            for i, (t0, m) in enumerate(TOK):
                pe.wait_ge(s.xt_ready, 2 * i + 2)
                for k in range(KD):
                    last = mm(bank[5][0:m, i * 20:(i + 1) * 20], XT[:, k, t0:t0 + m], wr[:, k, :], start=(k == 0), stop=(k == KD - 1))
            last.then_inc(s.lg_ps, 1)
            pe.wait_ge(s.router, 1)
            for i, (_t0, m) in enumerate(TOK):
                for i2 in range(i):
                    mm(bank[0][0:m, 4 * i:4 * i + 4], ones[:, 0:m], M1[:, i2, :], start=(i2 == 0), stop=False)
                last = mm(bank[0][0:m, 4 * i:4 * i + 4], before[0:m, 0:m], M1[0:m, i, :], start=(i == 0), stop=True)
            last.then_inc(s.gu_ps, 1)
            for i, (_t0, m) in enumerate(TOK):
                last = mm(bank[0][:, 12:16], ones[0:m, :], M1[0:m, i, :], start=(i == 0), stop=(i == 2))
            last.then_inc(s.rank_ps, 1)

            nr = rounds_of(pe)
            with pe.Fori(0, nr) as r:
                for i, (t0, m) in enumerate(TOK):
                    if i < 2:
                        pe.wait_ge(s.p_ready, r * 2 + (i + 1))
                    for q in range(EG):
                        last = tr(bank[1 + q][:, t0:t0 + m], PG[0:m, i, q * P:(q + 1) * P], ident[0:m, 0:m])
                last.then_inc(s.pt_ps, 1)
                for k in range(KD):
                    if k == 0:
                        pe.wait_ge(s.xn2_ready, 3)
                    if k == 3:
                        pe.wait_ge(s.pt_ready, r * 3 + 1)
                    for i, (_t0, m) in enumerate(TOK):
                        last = mm(bank[(k + 5) % 8][:, :], xn[0:m, i, k * P:(k + 1) * P], PG[0:m, i, :], start=(i == 0), stop=(i == 2))
                    last.then_inc(s.xg_ps, 1)
                pe.wait_ge(s.router, 2)
                pe.wait_ge(s.pt_ready, r * 3 + 2)
                for q in range(EG):
                    for i, (_t0, m) in enumerate(TOK):
                        last = mm(bank[5][:, 4 * q:4 * q + 4], PG[0:m, i, q * P:(q + 1) * P], GATE[0:m, i, :], start=(i == 0), stop=(i == 2))
                last.then_inc(s.pt_ps, 1)
                with pe.Fori(0, EG) as q:
                    with pe.Fori(0, EPG) as e:
                        x = (r * EG + q) * EPG + e
                        pe.wait_ge(s.pt_ready, r * 3 + 1)
                        pe.wait_ge(s.xs_ready, r * EG + q + 1)

                        def weights(c):
                            i = EXP_SLOT[c]
                            pe.wait_ge(arrived[i], x * 16 + (mix_in[i] + 16))
                            return slot_k(i, 512 if c < 4 else D)

                        def project(j, up):
                            w = weights(2 * j + up)
                            for k in range(KD):
                                last = mm(bank[2 * j + up][:, :], XS[:, k, :], w[:, k, :], start=(k == 0), stop=(k == KD - 1))
                            return last

                        def turn(j):
                            pe.wait_ge(s.a_ready, x * 2 + (j + 1))
                            for k in range(4):
                                last = tr(bank[4 + j][:, k * P:(k + 1) * P], AH[:, (4 * j + k) * P:(4 * j + k + 1) * P], ident[:, :])
                            last.then_inc(s.ft_ps, 1)

                        def down(j, half, w):
                            for k in range(4):
                                last = mm(bank[6 + half][:, :], HT[:, 4 * j + k, :], w[:, k, half * 512:(half + 1) * 512],
                                          start=(j == 0 and k == 0), stop=(j == 1 and k == 3), skip_group_check=True)
                            return last

                        project(0, 0).then_inc(s.gate_ps, 1)
                        project(0, 1).then_inc(s.gu_ps, 1)
                        project(1, 0).then_inc(s.gate_ps, 1)
                        turn(0)
                        project(1, 1).then_inc(s.gu_ps, 1)
                        pe.wait_ge(s.yg_done, x + 1)
                        pe.wait_ge(s.ht_sb, x * 2 + 1)
                        w = weights(4)
                        down(0, 0, w)
                        turn(1)
                        down(0, 1, w).then_inc(s.down_ps, 1)
                        pe.wait_ge(s.ht_sb, x * 2 + 2)
                        w = weights(5)
                        down(1, 0, w)
                        down(1, 1, w).then_inc(s.d_ps, 1)
                for q in range(EG):
                    for i, (t0, m) in enumerate(TOK):
                        for half in range(2):
                            if i == 0 and half == 0:
                                pe.wait_ge(s.yg_done, (r * EG + (q + 1)) * EPG + 1)
                            last = mm(bank[2 * i + half][0:m, :], PT[:, q, t0:t0 + m], YG[:, q, half * 512:(half + 1) * 512],
                                      start=(q == 0), stop=(q == EG - 1), skip_group_check=True)
                            if q == EG - 1:
                                last.then_inc(s.sc_out_ps, 1)
                pe.wait_ge(s.h_add, r * 6 + 10)


_INS = ["x_prompt", "x_sample", "state_mlstm_C", "state_mlstm_n", "state_mlstm_m", "state_mlstm_conv",
        "state_ssm", "state_ssm_conv", "meta_tokens", "norm_mix", "w_in", "conv_a_w", "conv_a_b", "w_q",
        "w_k", "w_v", "b_i", "b_f", "norm_a", "conv_b_w", "conv_b_b", "dt_bias", "a_log", "d_skip",
        "norm_b", "w_out", "norm_ffn", "w_r1", "b_r1", "w_r2", "b_r2", "w_gate", "w_up", "w_down",
        "norm_final"]
_OUTS = [(1, SEQ, D), (NB, 1, D),
         (1, 1, HA, DH, DH), (1, 1, HA, DH), (1, 1, HA), (1, 1, PAD, D), (1, 1, HB, HD, NST), (1, 1, PAD, CB_T * P),
         (1, NB, HA, DH, DH), (1, NB, HA, DH), (1, NB, HA), (1, NB, PAD, D), (1, NB, HB, HD, NST), (1, NB, PAD, CB_T * P)]


def kernel(**inputs):
    import numpy as _np
    import concourse.bacc as _bacc
    from concourse.bass_utils import run_bass_kernel_spmd as _run

    nc = _bacc.Bacc("TRN2", target_bir_lowering=False, num_devices=1)
    arrays, args = {}, []
    for name in _INS:
        a = _np.ascontiguousarray(inputs[name])
        arrays[f"in_{name}"] = a
        args.append(nc.dram_tensor(f"in_{name}", a.shape, mybir.dt.from_np(a.dtype), kind="ExternalInput").ap())
    for i, shape in enumerate(_OUTS):
        args.append(nc.dram_tensor(f"out_{i}", shape, F32, kind="ExternalOutput").ap())
    args.append(nc.dram_tensor("rows_dram", (NB, 512 + D), F32, kind="Internal").ap())
    args.append(nc.dram_tensor("heads_dram", (HA + HB, NP), F32, kind="Internal").ap())
    program(nc, *args)
    r = _run(nc, [arrays], core_ids=[0])
    return tuple(r.results[0][f"out_{i}"] for i in range(len(_OUTS)))
```
